# Optimizing a Trainium2 kernel written in Bass

```python
import math
import jax, jax.numpy as jnp
from jax import lax
import numpy as np
import jax
import jax.numpy as jnp

D_MODEL = 1024
BATCH = 1
SEQ = 512
DEPTH = 2

D_FF = 2816
PLE_DIM = 256
CONV_WIDTH = 3
CONV_CH = 512
S5_CH = 512
S5_GROUP = 16
S5_GROUPS = S5_CH // S5_GROUP
S5_STATE = 64
AB_IN = 3 * CONV_CH + S5_CH
N_HEADS = 8
HEAD_DIM = 128
N_KV_HEADS = 2
IDX_HEADS = 8
IDX_DIM = 64
TOPK_MAX = 256
Q_BLOCK = 128
C_SIZES = (N_HEADS * HEAD_DIM, N_KV_HEADS * HEAD_DIM, N_KV_HEADS * HEAD_DIM,
           IDX_HEADS * IDX_DIM, IDX_DIM, IDX_HEADS)
C_SPLITS = tuple(int(v) for v in np.cumsum(C_SIZES)[:-1])
C_IN = int(sum(C_SIZES))
ROPE_THETA = 500000.0
ROT_FRAC = 4
LN_EPS = 1e-5
DN_ALPHA = (2 * DEPTH) ** 0.25
DN_BETA = (8 * DEPTH) ** -0.25
N_EVEN = (DEPTH + 1) // 2
N_ODD = DEPTH // 2


def layer_norm(x, g, b):
    xf = x.astype(jnp.float32)
    mu = jnp.mean(xf, axis=-1, keepdims=True)
    var = jnp.mean(jnp.square(xf - mu), axis=-1, keepdims=True)
    return ((xf - mu) * lax.rsqrt(var + LN_EPS) * g.astype(jnp.float32) + b.astype(jnp.float32)).astype(x.dtype)

def swiglu(x, w1, w3, w2):
    return (jax.nn.silu(x @ w1) * (x @ w3)) @ w2

def rope_tables(positions, rot_dim):
    inv = ROPE_THETA ** (-jnp.arange(0, rot_dim, 2, dtype=jnp.float32) / rot_dim)
    ang = positions.astype(jnp.float32)[..., None] * inv
    return jnp.cos(ang), jnp.sin(ang)

def partial_rope(t, cos, sin):
    half = cos.shape[-1]
    r = 2 * half
    tr = t[..., :r].astype(jnp.float32)
    t1, t2 = tr[..., :half], tr[..., half:]
    rot = jnp.concatenate([t1 * cos - t2 * sin, t2 * cos + t1 * sin], axis=-1).astype(t.dtype)
    return jnp.concatenate([rot, t[..., r:]], axis=-1)

def short_conv_mixer(h, gb, gc, conv_w):
    u = gc * h
    L = u.shape[1]
    up = jnp.pad(u, ((0, 0), (CONV_WIDTH - 1, 0), (0, 0)))
    v = sum(conv_w[j] * up[:, j:j + L] for j in range(CONV_WIDTH))
    return gb * v

def s5_mixer(u, lam_re, lam_im, log_dt, b_re, b_im, c_re, c_im, d_skip, w_glu, b_glu):
    f32 = jnp.float32
    Bt, L, _ = u.shape
    uf = u.astype(f32)
    ug = uf.reshape(Bt, L, S5_GROUPS, S5_GROUP)
    lr = jnp.minimum(lam_re.astype(f32), -1e-4)
    li = lam_im.astype(f32)
    dt = jnp.exp(log_dt.astype(f32))[:, None]
    mag = jnp.exp(lr * dt)
    ab_re = mag * jnp.cos(li * dt)
    ab_im = mag * jnp.sin(li * dt)
    nr, ni = ab_re - 1.0, ab_im
    den = lr * lr + li * li
    f_re = (nr * lr + ni * li) / den
    f_im = (ni * lr - nr * li) / den
    br, bi = b_re.astype(f32), b_im.astype(f32)
    bb_re = f_re[..., None] * br - f_im[..., None] * bi
    bb_im = f_re[..., None] * bi + f_im[..., None] * br
    bu_re = jnp.einsum('blgc,gpc->blgp', ug, bb_re)
    bu_im = jnp.einsum('blgc,gpc->blgp', ug, bb_im)
    a_re = jnp.broadcast_to(ab_re, bu_re.shape)
    a_im = jnp.broadcast_to(ab_im, bu_im.shape)

    def combine(e1, e2):
        a1r, a1i, b1r, b1i = e1
        a2r, a2i, b2r, b2i = e2
        return (a2r * a1r - a2i * a1i, a2r * a1i + a2i * a1r,
                a2r * b1r - a2i * b1i + b2r, a2r * b1i + a2i * b1r + b2i)

    _, _, s_re, s_im = lax.associative_scan(combine, (a_re, a_im, bu_re, bu_im), axis=1)
    y = (jnp.einsum('blgp,gcp->blgc', s_re, c_re.astype(f32))
         - jnp.einsum('blgp,gcp->blgc', s_im, c_im.astype(f32)))
    y = y.reshape(Bt, L, S5_CH) + d_skip.astype(f32) * uf
    z = jax.nn.gelu(y)
    out = z * jax.nn.sigmoid(z @ w_glu.astype(f32) + b_glu.astype(f32))
    return out.astype(u.dtype)

def dsa_mixer(proj, cos_a, sin_a, cos_i, sin_i):
    f32 = jnp.float32
    Bt, L, _ = proj.shape
    q, k, v, qi, ki, wi = jnp.split(proj, C_SPLITS, axis=-1)
    q = partial_rope(q.reshape(Bt, L, N_HEADS, HEAD_DIM), cos_a[:, :, None], sin_a[:, :, None])
    k = partial_rope(k.reshape(Bt, L, N_KV_HEADS, HEAD_DIM), cos_a[:, :, None], sin_a[:, :, None])
    v = v.reshape(Bt, L, N_KV_HEADS, HEAD_DIM)
    qi = partial_rope(qi.reshape(Bt, L, IDX_HEADS, IDX_DIM), cos_i[:, :, None], sin_i[:, :, None])
    ki = partial_rope(ki, cos_i, sin_i).astype(f32)
    wi = wi.astype(f32) * (IDX_HEADS ** -0.5 * IDX_DIM ** -0.5)
    topk = min(TOPK_MAX, L // 4)
    nb = L // Q_BLOCK

    def to_blocks(t):
        return jnp.moveaxis(t.reshape(Bt, nb, Q_BLOCK, *t.shape[2:]), 1, 0)

    t_pos = jnp.arange(L, dtype=jnp.int32).reshape(nb, Q_BLOCK)
    key_pos = jnp.arange(L, dtype=jnp.int32)
    bidx = jnp.arange(Bt)[:, None, None]
    rep = N_HEADS // N_KV_HEADS

    def block(args):
        qb, qib, wb, tb = args
        logits = jax.nn.relu(jnp.einsum('bthd,bsd->bths', qib.astype(f32), ki))
        score = jnp.einsum('bths,bth->bts', logits, wb)
        causal = key_pos[None, :] <= tb[:, None]
        score = jnp.where(causal[None], score, -jnp.inf)
        _, idx = lax.top_k(score, topk)
        valid = idx <= tb[None, :, None]
        k_sel = k[bidx, idx]
        v_sel = v[bidx, idx]
        qg = qb.reshape(Bt, Q_BLOCK, N_KV_HEADS, rep, HEAD_DIM)
        s = jnp.einsum('btgrd,btjgd->btgrj', qg, k_sel).astype(f32) * (HEAD_DIM ** -0.5)
        s = jnp.where(valid[:, :, None, None, :], s, -jnp.inf)
        pr = jax.nn.softmax(s, axis=-1)
        o = jnp.einsum('btgrj,btjgd->btgrd', pr.astype(v.dtype), v_sel)
        return o.reshape(Bt, Q_BLOCK, N_HEADS * HEAD_DIM)

    out = lax.map(block, (to_blocks(q), to_blocks(qi), to_blocks(wi), t_pos))
    return jnp.moveaxis(out, 0, 1).reshape(Bt, L, N_HEADS * HEAD_DIM)

def first_inputs(seed: int = 0) -> dict:
    key = jax.random.key(seed)
    ks = jax.random.split(key, 32)
    f32 = jnp.float32

    def nrm(i, shape, scale):
        return jax.random.normal(ks[i], shape, f32) * scale

    x = nrm(0, (BATCH, SEQ, D_MODEL), 1.0)
    p = nrm(1, (DEPTH, BATCH, SEQ, PLE_DIM), 1.0)
    offs = jax.random.randint(ks[2], (BATCH, 1), 0, 1024, dtype=jnp.int32)
    positions = offs + jnp.arange(SEQ, dtype=jnp.int32)[None, :]
    ln_g = 1.0 + nrm(3, (DEPTH, 3, D_MODEL), 0.02)
    ln_b = nrm(4, (DEPTH, 3, D_MODEL), 0.02)
    ffn_w1 = nrm(5, (DEPTH, 2, D_MODEL, D_FF), D_MODEL ** -0.5)
    ffn_w3 = nrm(6, (DEPTH, 2, D_MODEL, D_FF), D_MODEL ** -0.5)
    ffn_w2 = nrm(7, (DEPTH, 2, D_FF, D_MODEL), D_FF ** -0.5 * DN_BETA)
    ple_w_proj = nrm(8, (DEPTH, PLE_DIM, D_MODEL), PLE_DIM ** -0.5)
    ple_w_gate = nrm(9, (DEPTH, D_MODEL, D_MODEL), D_MODEL ** -0.5)
    ab_w_in = nrm(10, (N_EVEN, D_MODEL, AB_IN), D_MODEL ** -0.5)
    ab_w_out = nrm(11, (N_EVEN, CONV_CH + S5_CH, D_MODEL), (CONV_CH + S5_CH) ** -0.5 * DN_BETA)
    conv_w = nrm(12, (N_EVEN, CONV_WIDTH, CONV_CH), CONV_WIDTH ** -0.5)
    s5_lam_re = -0.5 + nrm(13, (N_EVEN, S5_GROUPS, S5_STATE), 0.01)
    s5_lam_im = (math.pi * jnp.arange(S5_STATE, dtype=f32))[None, None, :] + nrm(14, (N_EVEN, S5_GROUPS, S5_STATE), 0.01)
    s5_log_dt = jax.random.uniform(ks[15], (N_EVEN, S5_GROUPS), f32, math.log(1e-3), math.log(1e-1))
    s5_b_re = nrm(16, (N_EVEN, S5_GROUPS, S5_STATE, S5_GROUP), (2 * S5_GROUP) ** -0.5)
    s5_b_im = nrm(17, (N_EVEN, S5_GROUPS, S5_STATE, S5_GROUP), (2 * S5_GROUP) ** -0.5)
    s5_c_re = nrm(18, (N_EVEN, S5_GROUPS, S5_GROUP, S5_STATE), S5_STATE ** -0.5)
    s5_c_im = nrm(19, (N_EVEN, S5_GROUPS, S5_GROUP, S5_STATE), S5_STATE ** -0.5)
    s5_d = nrm(20, (N_EVEN, S5_CH), 1.0)
    s5_w_glu = nrm(21, (N_EVEN, S5_CH, S5_CH), S5_CH ** -0.5)
    s5_b_glu = nrm(22, (N_EVEN, S5_CH), 0.02)
    c_w_in = nrm(23, (N_ODD, D_MODEL, C_IN), D_MODEL ** -0.5)
    c_w_out = nrm(24, (N_ODD, N_HEADS * HEAD_DIM, D_MODEL), (N_HEADS * HEAD_DIM) ** -0.5 * DN_BETA)
    return {'x': x, 'p': p, 'positions': positions, 'ln_g': ln_g, 'ln_b': ln_b,
            'ffn_w1': ffn_w1, 'ffn_w3': ffn_w3, 'ffn_w2': ffn_w2,
            'ple_w_proj': ple_w_proj, 'ple_w_gate': ple_w_gate,
            'ab_w_in': ab_w_in, 'ab_w_out': ab_w_out, 'conv_w': conv_w,
            's5_lam_re': s5_lam_re, 's5_lam_im': s5_lam_im, 's5_log_dt': s5_log_dt,
            's5_b_re': s5_b_re, 's5_b_im': s5_b_im, 's5_c_re': s5_c_re, 's5_c_im': s5_c_im,
            's5_d': s5_d, 's5_w_glu': s5_w_glu, 's5_b_glu': s5_b_glu,
            'c_w_in': c_w_in, 'c_w_out': c_w_out}

def first_block(x, p, positions, ln_g, ln_b, ffn_w1, ffn_w3, ffn_w2, ple_w_proj, ple_w_gate,
              ab_w_in, ab_w_out, conv_w, s5_lam_re, s5_lam_im, s5_log_dt, s5_b_re, s5_b_im,
              s5_c_re, s5_c_im, s5_d, s5_w_glu, s5_b_glu, c_w_in, c_w_out):
    cos_a, sin_a = rope_tables(positions, HEAD_DIM // ROT_FRAC)
    cos_i, sin_i = rope_tables(positions, IDX_DIM // ROT_FRAC)
    h = x
    for i in range(DEPTH):
        h = layer_norm(DN_ALPHA * h + 0.5 * swiglu(h, ffn_w1[i, 0], ffn_w3[i, 0], ffn_w2[i, 0]),
                       ln_g[i, 0], ln_b[i, 0])
        j = i // 2
        if i % 2 == 0:
            proj = h @ ab_w_in[j]
            hc, gb, gc, u = jnp.split(proj, [CONV_CH, 2 * CONV_CH, 3 * CONV_CH], axis=-1)
            ya = short_conv_mixer(hc, gb, gc, conv_w[j])
            yb = s5_mixer(u, s5_lam_re[j], s5_lam_im[j], s5_log_dt[j], s5_b_re[j], s5_b_im[j],
                          s5_c_re[j], s5_c_im[j], s5_d[j], s5_w_glu[j], s5_b_glu[j])
            mix = jnp.concatenate([ya, yb], axis=-1) @ ab_w_out[j]
        else:
            proj = h @ c_w_in[j]
            mix = dsa_mixer(proj, cos_a, sin_a, cos_i, sin_i) @ c_w_out[j]
        h = layer_norm(DN_ALPHA * h + mix, ln_g[i, 1], ln_b[i, 1])
        h = layer_norm(DN_ALPHA * h + 0.5 * swiglu(h, ffn_w1[i, 1], ffn_w3[i, 1], ffn_w2[i, 1]),
                       ln_g[i, 2], ln_b[i, 2])
        h = h + (p[i] @ ple_w_proj[i]) * jax.nn.sigmoid(h @ ple_w_gate[i])
    return h


DEPTH_2 = 1

HEAD_DIM_2 = 64
NSA_HEADS = 8
NSA_KV_HEADS = 2
NSA_GROUP = NSA_HEADS // NSA_KV_HEADS
SWA_HEADS = 8
SWA_KV_HEADS = 2
SWA_GROUP = SWA_HEADS // SWA_KV_HEADS
NSA_WIDTH = NSA_HEADS * HEAD_DIM_2
SWA_WIDTH = SWA_HEADS * HEAD_DIM_2
NSA_KV_WIDTH = NSA_KV_HEADS * HEAD_DIM_2
SWA_KV_WIDTH = SWA_KV_HEADS * HEAD_DIM_2
CMP_LEN = 32
CMP_STRIDE = 16
CMP_HIDDEN = 256
SLC_LEN = 64
SLC_TOPK = 8
NSA_WINDOW = 256
SLC_QUERY_CHUNK = 64
SWA_WINDOW = 128
BAND_BLOCK = 128
N_GROUPS = 4
EXPERTS_PER_GROUP = 8
N_EXPERTS = N_GROUPS * EXPERTS_PER_GROUP
EXPERT_TOPK = 2
EXPERT_FF = 256
MOE_BLOCK = 128
IN_SIZES = (NSA_WIDTH, NSA_KV_WIDTH, NSA_KV_WIDTH, NSA_KV_WIDTH, NSA_KV_WIDTH, NSA_KV_WIDTH, NSA_KV_WIDTH,
            3 * NSA_HEADS, SWA_WIDTH, SWA_KV_WIDTH, SWA_KV_WIDTH, 2 * D_MODEL)
IN_WIDTH = sum(IN_SIZES)
RMS_EPS = 1e-6
NEG_INF = -1e30
FORCE_SCORE = 1e9


def rms_norm(x, g):
    x32 = x.astype(jnp.float32)
    y = x32 * lax.rsqrt(jnp.mean(x32 * x32, axis=-1, keepdims=True) + RMS_EPS)
    return (y * g.astype(jnp.float32)).astype(x.dtype)

def masked_softmax(s, mask):
    s = jnp.where(mask, s, NEG_INF)
    m = jnp.max(s, axis=-1, keepdims=True)
    e = jnp.where(mask, jnp.exp(s - m), 0.0)
    z = jnp.sum(e, axis=-1, keepdims=True)
    return e / jnp.where(z > 0, z, 1.0)

def alibi_slopes():
    n = NSA_HEADS + SWA_HEADS
    s = 2.0 ** (-8.0 * np.arange(1, n + 1) / n)
    return jnp.asarray(s[:SWA_HEADS], jnp.float32), jnp.asarray(s[SWA_HEADS:], jnp.float32)

def compress_blocks(kv, pos, w1, w2):
    B, S, H, d = kv.shape
    r = CMP_LEN // CMP_STRIDE
    nc = S // CMP_STRIDE - r + 1
    kc = kv.reshape(B, S // CMP_STRIDE, CMP_STRIDE, H, d)
    blocks = jnp.concatenate([kc[:, i:i + nc] for i in range(r)], axis=2)
    blocks = blocks + pos[None, None, :, None, :]
    flat = jnp.transpose(blocks, (0, 1, 3, 2, 4)).reshape(B, nc, H, CMP_LEN * d)
    return jax.nn.silu(flat @ w1) @ w2

def compressed_branch(q, kc, vc, slopes):
    B, S, Hkv, G, d = q.shape
    nc = kc.shape[1]
    s = jnp.einsum('bshgd,bchd->bhgsc', q, kc, preferred_element_type=jnp.float32) * (d ** -0.5)
    end = jnp.arange(nc) * CMP_STRIDE + CMP_LEN - 1
    dist = jnp.arange(S)[:, None] - end[None, :]
    s = s - slopes.reshape(Hkv, G, 1, 1) * dist.astype(jnp.float32)
    p = masked_softmax(s, dist >= 0)
    o = jnp.einsum('bhgsc,bchd->bshgd', p.astype(vc.dtype), vc)
    return o, p

def select_blocks(p_cmp, S):
    nc = p_cmp.shape[-1]
    ns = S // SLC_LEN
    c0 = np.arange(nc) * CMP_STRIDE
    s0 = np.arange(ns) * SLC_LEN
    ov = np.clip(np.minimum(c0[:, None] + CMP_LEN, s0[None, :] + SLC_LEN)
                 - np.maximum(c0[:, None], s0[None, :]), 0, None) / CMP_LEN
    imp = jnp.einsum('bhsc,cj->bhsj', jnp.sum(p_cmp, axis=2), jnp.asarray(ov, jnp.float32))
    t = jnp.arange(S)[:, None]
    j = jnp.arange(ns)[None, :]
    cur = t // SLC_LEN
    valid = j * SLC_LEN <= t
    forced = (j == 0) | (j == cur) | (j == cur - 1)
    score = jnp.where(forced, FORCE_SCORE, jnp.where(valid, imp, NEG_INF))
    vals, idx = lax.top_k(score, min(SLC_TOPK, ns))
    return idx, vals > 0.5 * NEG_INF

def selected_branch(q, k, v, idx, valid, slopes):
    B, S, Hkv, G, d = q.shape
    ns = S // SLC_LEN
    n = idx.shape[-1]
    QC = SLC_QUERY_CHUNK
    nq = S // QC
    kb = jnp.transpose(k.reshape(B, ns, SLC_LEN, Hkv, d), (0, 3, 1, 2, 4))
    vb = jnp.transpose(v.reshape(B, ns, SLC_LEN, Hkv, d), (0, 3, 1, 2, 4))
    qc = jnp.swapaxes(q.reshape(B, nq, QC, Hkv, G, d), 0, 1)
    ic = jnp.transpose(idx.reshape(B, Hkv, nq, QC, n), (2, 0, 1, 3, 4))
    vc = jnp.transpose(valid.reshape(B, Hkv, nq, QC, n), (2, 0, 1, 3, 4))
    tc = jnp.arange(S).reshape(nq, QC)
    bi = jnp.arange(B)[:, None, None, None]
    hi = jnp.arange(Hkv)[None, :, None, None]
    sl = slopes.reshape(1, Hkv, G, 1, 1, 1)
    scale = d ** -0.5

    def chunk(args):
        qq, ii, vv, tt = args
        kg = kb[bi, hi, ii]
        vg = vb[bi, hi, ii]
        s = jnp.einsum('bqhgd,bhqnld->bhgqnl', qq, kg, preferred_element_type=jnp.float32) * scale
        kpos = ii[..., None] * SLC_LEN + jnp.arange(SLC_LEN)
        dist = tt[None, None, :, None, None] - kpos
        mask = (vv[..., None] & (dist >= 0))[:, :, None]
        s = s - sl * dist[:, :, None].astype(jnp.float32)
        p = masked_softmax(s.reshape(B, Hkv, G, QC, n * SLC_LEN), mask.reshape(B, Hkv, 1, QC, n * SLC_LEN))
        return jnp.einsum('bhgqk,bhqkd->bqhgd', p.astype(vg.dtype), vg.reshape(B, Hkv, QC, n * SLC_LEN, d))

    out = lax.map(chunk, (qc, ic, vc, tc))
    return jnp.swapaxes(out, 0, 1).reshape(B, S, Hkv, G, d)

def banded_attention(q, k, v, slopes, window, sinks):
    B, S, Hkv, G, d = q.shape
    nb = S // BAND_BLOCK
    nprev = -(-(window - 1) // BAND_BLOCK)
    pad = nprev * BAND_BLOCK
    kw = (nprev + 1) * BAND_BLOCK

    def band(a):
        ap = jnp.pad(a, ((0, 0), (pad, 0), (0, 0), (0, 0))).reshape(B, nb + nprev, BAND_BLOCK, Hkv, d)
        return jnp.concatenate([ap[:, j:j + nb] for j in range(nprev + 1)], axis=2)

    kb, vb = band(k), band(v)
    qb = q.reshape(B, nb, BAND_BLOCK, Hkv, G, d)
    s = jnp.einsum('bnqhgd,bnkhd->bnhgqk', qb, kb, preferred_element_type=jnp.float32) * (d ** -0.5)
    blk = jnp.arange(nb)[:, None] * BAND_BLOCK
    tpos = blk + jnp.arange(BAND_BLOCK)
    kpos = blk - pad + jnp.arange(kw)
    dist = tpos[:, :, None] - kpos[:, None, :]
    mask = ((dist >= 0) & (dist < window) & (kpos[:, None, :] >= 0))[None, :, None, None]
    s = s - slopes.reshape(1, 1, Hkv, G, 1, 1) * dist.astype(jnp.float32)[None, :, None, None]
    s = jnp.where(mask, s, NEG_INF)
    m = jnp.max(s, axis=-1, keepdims=True)
    if sinks is not None:
        sk = sinks.astype(jnp.float32).reshape(1, 1, Hkv, G, 1, 1)
        m = jnp.maximum(m, sk)
    e = jnp.where(mask, jnp.exp(s - m), 0.0)
    z = jnp.sum(e, axis=-1, keepdims=True)
    if sinks is not None:
        z = z + jnp.exp(sk - m)
    p = e / z
    o = jnp.einsum('bnhgqk,bnkhd->bnqhgd', p.astype(v.dtype), vb)
    return o.reshape(B, S, Hkv, G, d)

def hier_moe(h, w_group, b_group, w_expert, b_expert, w_gate_e, w_up_e, w_down_e):
    B, S, D = h.shape
    N = B * S
    hf = h.reshape(N, D)
    g_logits = (hf @ w_group).astype(jnp.float32) + b_group.astype(jnp.float32)
    g_prob = jax.nn.softmax(g_logits, axis=-1)
    grp = jnp.argmax(g_logits, axis=-1)
    p_grp = jnp.take_along_axis(g_prob, grp[:, None], axis=-1)[:, 0]
    e_logits = ((hf @ w_expert).astype(jnp.float32) + b_expert.astype(jnp.float32)).reshape(N, N_GROUPS, EXPERTS_PER_GROUP)
    e_in = jnp.take_along_axis(e_logits, grp[:, None, None], axis=1)[:, 0]
    top_v, top_i = lax.top_k(e_in, EXPERT_TOPK)
    weight = p_grp[:, None] * jax.nn.softmax(top_v, axis=-1)
    eid = (grp[:, None] * EXPERTS_PER_GROUP + top_i).reshape(-1)
    w_f = weight.reshape(-1)
    NK = N * EXPERT_TOPK
    tok = jnp.arange(NK) // EXPERT_TOPK
    order = jnp.argsort(eid)
    e_sorted = eid[order]
    counts = jnp.bincount(eid, length=N_EXPERTS)
    padded = (counts + MOE_BLOCK - 1) // MOE_BLOCK * MOE_BLOCK
    pad_end = jnp.cumsum(padded)
    pad_start = pad_end - padded
    cnt_start = jnp.cumsum(counts) - counts
    dest = pad_start[e_sorted] + jnp.arange(NK) - cnt_start[e_sorted]
    n_blocks = -(-(NK + N_EXPERTS * (MOE_BLOCK - 1)) // MOE_BLOCK)
    buf = jnp.zeros((n_blocks * MOE_BLOCK, D), h.dtype).at[dest].set(hf[tok[order]])
    block_e = jnp.minimum(jnp.searchsorted(pad_end, jnp.arange(n_blocks) * MOE_BLOCK, side='right'), N_EXPERTS - 1)

    def expert_block(args):
        xb, e = args
        return (jax.nn.silu(xb @ w_gate_e[e]) * (xb @ w_up_e[e])) @ w_down_e[e]

    yb = lax.map(expert_block, (buf.reshape(n_blocks, MOE_BLOCK, D), block_e)).reshape(-1, D)
    y_slot = yb[dest] * w_f[order][:, None].astype(yb.dtype)
    y = jnp.zeros((N, D), h.dtype).at[tok[order]].add(y_slot)
    return y.reshape(B, S, D)

def second_inputs(seed: int = 0) -> dict:
    key = jax.random.key(seed)
    ks = jax.random.split(key, 24)
    f32 = jnp.float32
    L = DEPTH_2
    d = HEAD_DIM_2

    def nrm(k, shape, scale):
        return jax.random.normal(k, shape, f32) * scale

    return {
        "x": nrm(ks[0], (BATCH, SEQ, D_MODEL), 1.0),
        "norm_mix_g": 1.0 + nrm(ks[1], (L, D_MODEL), 0.02),
        "w_in": nrm(ks[2], (L, D_MODEL, IN_WIDTH), D_MODEL ** -0.5),
        "cmp_pos_k": nrm(ks[3], (L, CMP_LEN, d), 0.1),
        "cmp_w1_k": nrm(ks[4], (L, CMP_LEN * d, CMP_HIDDEN), (CMP_LEN * d) ** -0.5),
        "cmp_w2_k": nrm(ks[5], (L, CMP_HIDDEN, d), CMP_HIDDEN ** -0.5),
        "cmp_pos_v": nrm(ks[6], (L, CMP_LEN, d), 0.1),
        "cmp_w1_v": nrm(ks[7], (L, CMP_LEN * d, CMP_HIDDEN), (CMP_LEN * d) ** -0.5),
        "cmp_w2_v": nrm(ks[8], (L, CMP_HIDDEN, d), CMP_HIDDEN ** -0.5),
        "sinks": nrm(ks[9], (L, SWA_HEADS), 0.5),
        "w_a": nrm(ks[10], (L, NSA_WIDTH, D_MODEL), NSA_WIDTH ** -0.5),
        "w_b": nrm(ks[11], (L, SWA_WIDTH, D_MODEL), SWA_WIDTH ** -0.5),
        "w_o": nrm(ks[12], (L, D_MODEL, D_MODEL), D_MODEL ** -0.5),
        "norm_ffn_g": 1.0 + nrm(ks[13], (L, D_MODEL), 0.02),
        "w_group": nrm(ks[14], (L, D_MODEL, N_GROUPS), D_MODEL ** -0.5),
        "b_group": nrm(ks[15], (L, N_GROUPS), 0.01),
        "w_expert": nrm(ks[16], (L, D_MODEL, N_EXPERTS), D_MODEL ** -0.5),
        "b_expert": nrm(ks[17], (L, N_EXPERTS), 0.01),
        "w_gate_e": nrm(ks[18], (L, N_EXPERTS, D_MODEL, EXPERT_FF), D_MODEL ** -0.5),
        "w_up_e": nrm(ks[19], (L, N_EXPERTS, D_MODEL, EXPERT_FF), D_MODEL ** -0.5),
        "w_down_e": nrm(ks[20], (L, N_EXPERTS, EXPERT_FF, D_MODEL), EXPERT_FF ** -0.5),
        "norm_final_g": 1.0 + nrm(ks[21], (D_MODEL,), 0.02),
    }

def second_block(x, norm_mix_g, w_in, cmp_pos_k, cmp_w1_k, cmp_w2_k, cmp_pos_v, cmp_w1_v, cmp_w2_v,
              sinks, w_a, w_b, w_o, norm_ffn_g, w_group, b_group, w_expert, b_expert,
              w_gate_e, w_up_e, w_down_e, norm_final_g):
    B, S, _ = x.shape
    slopes_swa, slopes_nsa = alibi_slopes()
    split_points = [int(c) for c in np.cumsum(IN_SIZES)[:-1]]
    for l in range(DEPTH_2):
        h = rms_norm(x, norm_mix_g[l])
        proj = h @ w_in[l]
        (q_a, k_cmp, v_cmp, k_slc, v_slc, k_win, v_win, g_nsa,
         q_b, k_b, v_b, g_merge) = jnp.split(proj, split_points, axis=-1)
        q_a = q_a.reshape(B, S, NSA_KV_HEADS, NSA_GROUP, HEAD_DIM_2)
        kv_a = [t.reshape(B, S, NSA_KV_HEADS, HEAD_DIM_2) for t in (k_cmp, v_cmp, k_slc, v_slc, k_win, v_win)]
        kc = compress_blocks(kv_a[0], cmp_pos_k[l], cmp_w1_k[l], cmp_w2_k[l])
        vc = compress_blocks(kv_a[1], cmp_pos_v[l], cmp_w1_v[l], cmp_w2_v[l])
        o_cmp, p_cmp = compressed_branch(q_a, kc, vc, slopes_nsa)
        idx, valid = select_blocks(p_cmp, S)
        o_slc = selected_branch(q_a, kv_a[2], kv_a[3], idx, valid, slopes_nsa)
        o_win = banded_attention(q_a, kv_a[4], kv_a[5], slopes_nsa, NSA_WINDOW, None)
        g = jax.nn.sigmoid(g_nsa).reshape(B, S, NSA_KV_HEADS, NSA_GROUP, 3)
        o_a = (g[..., 0:1] * o_cmp + g[..., 1:2] * o_slc + g[..., 2:3] * o_win).reshape(B, S, NSA_WIDTH)
        q_b = q_b.reshape(B, S, SWA_KV_HEADS, SWA_GROUP, HEAD_DIM_2)
        k_b = k_b.reshape(B, S, SWA_KV_HEADS, HEAD_DIM_2)
        v_b = v_b.reshape(B, S, SWA_KV_HEADS, HEAD_DIM_2)
        o_b = banded_attention(q_b, k_b, v_b, slopes_swa, SWA_WINDOW, sinks[l]).reshape(B, S, SWA_WIDTH)
        gate_a, gate_b = jnp.split(jax.nn.sigmoid(g_merge), 2, axis=-1)
        mix = (gate_a * (o_a @ w_a[l]) + gate_b * (o_b @ w_b[l])) @ w_o[l]
        x = x + mix
        x = x + hier_moe(rms_norm(x, norm_ffn_g[l]), w_group[l], b_group[l], w_expert[l], b_expert[l],
                         w_gate_e[l], w_up_e[l], w_down_e[l])
    return rms_norm(x, norm_final_g)


def setup_inputs(seed=0):
    out = dict(first_inputs(seed))
    for name, value in second_inputs(seed + 1).items():
        if name != "x":
            out[name + "_2"] = value
    return out


def reference(
    x, p, positions, ln_g, ln_b, ffn_w1, ffn_w3, ffn_w2, ple_w_proj, ple_w_gate, ab_w_in,
    ab_w_out, conv_w, s5_lam_re, s5_lam_im, s5_log_dt, s5_b_re, s5_b_im, s5_c_re, s5_c_im, s5_d,
    s5_w_glu, s5_b_glu, c_w_in, c_w_out, norm_mix_g_2, w_in_2, cmp_pos_k_2, cmp_w1_k_2,
    cmp_w2_k_2, cmp_pos_v_2, cmp_w1_v_2, cmp_w2_v_2, sinks_2, w_a_2, w_b_2, w_o_2, norm_ffn_g_2,
    w_group_2, b_group_2, w_expert_2, b_expert_2, w_gate_e_2, w_up_e_2, w_down_e_2,
    norm_final_g_2,
):
    x = first_block(
        x, p, positions, ln_g, ln_b, ffn_w1, ffn_w3, ffn_w2, ple_w_proj, ple_w_gate, ab_w_in,
        ab_w_out, conv_w, s5_lam_re, s5_lam_im, s5_log_dt, s5_b_re, s5_b_im, s5_c_re, s5_c_im,
        s5_d, s5_w_glu, s5_b_glu, c_w_in, c_w_out,
    )
    return second_block(
        x, norm_mix_g_2, w_in_2, cmp_pos_k_2, cmp_w1_k_2, cmp_w2_k_2, cmp_pos_v_2, cmp_w1_v_2,
        cmp_w2_v_2, sinks_2, w_a_2, w_b_2, w_o_2, norm_ffn_g_2, w_group_2, b_group_2,
        w_expert_2, b_expert_2, w_gate_e_2, w_up_e_2, w_down_e_2, norm_final_g_2,
    )


_drawn_inputs = setup_inputs


def setup_inputs(seed=0):
    import zlib

    import numpy as np

    out = dict(_drawn_inputs(seed))
    spreads = {}
    factors = {'s5_lam_re': 64.0,
     's5_lam_im': 38.648,
     's5_log_dt': 41.992,
     's5_b_re': 33.448,
     's5_b_im': 35.832,
     's5_c_re': 41.648,
     's5_c_im': 30.072,
     's5_b_glu': 8.0,
     'norm_mix_g_2': 4.84,
     'cmp_pos_k_2': 8.0,
     'b_group_2': 26.335,
     'b_expert_2': 30.446,
     'norm_final_g_2': 8.043,
     'cmp_pos_v_2': 6.448,
     'sinks_2': 8.0,
     'norm_ffn_g_2': 6.508}
    for name, (base, spread) in spreads.items():
        noise = np.random.default_rng([zlib.crc32(name.encode()), seed]).standard_normal(out[name].shape)
        drawn = base * np.exp(spread * noise) if base else spread * noise
        out[name] = jnp.asarray(drawn.astype(out[name].dtype))
    for name, factor in factors.items():
        out[name] = (out[name] * factor).astype(out[name].dtype)
    return out
```

```python
from contextlib import ExitStack

import numpy as np

import concourse.bass as bass
from concourse import mybir

F32 = mybir.dt.float32
I32 = mybir.dt.int32
U32 = mybir.dt.uint32
ALU = mybir.AluOpType
ACT = mybir.ActivationFunctionType
AX = mybir.AxisListType

P = 128
T = 512
TB = T // P
D = 1024
KD = D // P
DEPTH = 2
FF = 2816
KF = FF // P
PLE = 256
CC = 512
KC = CC // P
GROUPS, GCH, STATES = 32, 16, 64
PAIRS = GROUPS // 2
PPC = P // (2 * GCH)
HEADS, HD, KVH = 8, 128, 2
IH, ID = 8, 64
TOPK = 128
AQ, AK, AV, AI, AKI, AW = np.cumsum([0, 1024, 256, 256, 512, 64]).tolist()
THETA = 500000.0
LN_EPS, RMS_EPS = 1e-5, 1e-6
ALPHA = float((2 * DEPTH) ** 0.25)
BH, BD = 8, 64
CL, CS, CHID = 32, 16, 256
NCMP = T // CS - CL // CS + 1
(BQA, BKC, BVC, BKS, BVS, BKW, BVW, BG, BQB, BKB, BVB, BM) = np.cumsum(
    [0, 512, 128, 128, 128, 128, 128, 128, 24, 512, 128, 128]).tolist()
NGRP, EPG, NEXP, EFF = 4, 8, 32, 256
EXPERTS_AT_ONCE = 4
NEG = -1e30
CAUSAL_FILL = -1e30
TAKEN = -3e38
SLOPES = 2.0 ** (-8.0 * np.arange(1, 17) / 16)
SLOPES = np.asarray(SLOPES, np.float32)
PI = float(np.pi)
ROUND = 12582912.0
ROUND13 = 1536.0
TWO_PI_1 = 6.28125
TWO_PI_2 = 0.0019350051879882812
TWO_PI_3 = float(2 * np.pi - TWO_PI_1 - TWO_PI_2)

BLOCK = 16 * P
RING = 6


def dense(name, index, n_rows, col0, n_cols, width=P):
    return [[(name, index, ((k * P, P),), ((col0 + m * width, min(width, n_cols - m * width)),))
             for k in range(n_rows // P)] for m in range(-(-n_cols // width))]


def columns(name, index, n_rows, *segments):
    return [(name, index, ((k * P, P),), tuple(segments)) for k in range(n_rows // P)]


def ffn_pieces(layer, i):
    up = []
    for g, u in zip(dense("ffn_w1", (layer, i), D, 0, FF), dense("ffn_w3", (layer, i), D, 0, FF)):
        up += [g, u]
    return up, dense("ffn_w2", (layer, i), FF, 0, D)


def ple_pieces(layer):
    out = []
    for g, p in zip(dense("ple_w_gate", (layer,), D, 0, D), dense("ple_w_proj", (layer,), PLE, 0, D)):
        out += [g, p]
    return out


def pair_rows(name, index, first):
    return [[(name, index, ((j * BD, BD), ((4 + j) * BD, BD)), ((m * P, P),)) for j in range(4)]
            for m in range(D // P)]


def head_columns(base, j):
    return ((base + j * BD, BD), (base + (4 + j) * BD, BD))


def weight_plan():
    plan = {}
    plan["ffn0_up"], plan["ffn0_down"] = ffn_pieces(0, 0)
    plan["ab_in"] = dense("ab_w_in", (0,), D, 0, 4 * CC)
    plan["glu"] = dense("s5_w_glu", (0,), CC, 0, CC)
    plan["ab_out"] = dense("ab_w_out", (0,), 2 * CC, 0, D)
    plan["ffn1_up"], plan["ffn1_down"] = ffn_pieces(0, 1)
    plan["ple0"] = ple_pieces(0)
    plan["ffn2_up"], plan["ffn2_down"] = ffn_pieces(1, 0)
    plan["c_index"] = (dense("c_w_in", (0,), D, AI, IH * ID) +
                       [columns("c_w_in", (0,), D, (AKI, ID), (AKI, ID))])
    plan["c_weight"] = [columns("c_w_in", (0,), D, (AW, IH))]
    plan["c_value"] = [columns("c_w_in", (0,), D, (AV, 256))]
    plan["c_qk"] = dense("c_w_in", (0,), D, AQ, HEADS * HD) + dense("c_w_in", (0,), D, AK, KVH * HD)
    plan["c_out"] = dense("c_w_out", (0,), D, 0, D)
    plan["ffn3_up"], plan["ffn3_down"] = ffn_pieces(1, 1)
    plan["ple1"] = ple_pieces(1)
    w = ("w_in_2", (0,), D)
    plan["b_compress_in"] = [columns(*w, (BKC, P)), columns(*w, (BVC, P))]
    plan["b_compress"] = [[(f"cmp_w1_{c}_2", (0,), ((l * BD, BD), (l * BD, BD)), ((m * P, P),))
                           for l in range(CL)] for c in "kv" for m in range(CHID // P)]
    plan["b_compress_k"] = [[("cmp_w2_k_2", (0,), ((k * P, P),), ((0, BD), (0, BD))) for k in range(CHID // P)]]
    plan["b_compress_v"] = [[("cmp_w2_v_2", (0,), ((k * P, P),), ((0, BD),)) for k in range(CHID // P)]]
    plan["b_value"] = [columns(*w, (BVS, P), (BVW, P), (BVB, P))]
    plan["b_gate"] = [columns(*w, (BG, 24))]
    plan["b_key"] = [columns(*w, (b, P)) for b in (BKS, BKW, BKB)]
    plan["b_query"] = [columns(*w, *head_columns(b, j)) for b in (BQA, BQB) for j in range(4)]
    plan["b_merge"] = []
    for m in range(KD):
        plan["b_merge"] += [columns(*w, (BM + m * P, P)), columns(*w, (BM + D + m * P, P)),
                            pair_rows("w_a_2", (0,), 0)[m], pair_rows("w_b_2", (0,), 0)[m]]
    plan["b_out"] = dense("w_o_2", (0,), D, 0, D)
    plan["router"] = [columns("w_group_2", (0,), D, (0, NGRP)), columns("w_expert_2", (0,), D, (0, NEXP))]
    for e0 in range(0, NEXP, EXPERTS_AT_ONCE):
        up = []
        for e in range(e0, e0 + EXPERTS_AT_ONCE):
            for g, u in zip(dense("w_gate_e_2", (0, e), D, 0, EFF), dense("w_up_e_2", (0, e), D, 0, EFF)):
                up += [g, u]
        plan[f"moe{e0}_up"] = up
        plan[f"moe{e0}_down"] = [[("w_down_e_2", (0, e), ((k * P, P),), ((m * P, P),))
                                  for e in range(e0, e0 + EXPERTS_AT_ONCE) for k in range(EFF // P)]
                                 for m in range(KD)]
    return plan


def width_of(piece):
    return sum(n for _, n in piece[3])


def place_pieces(plan):
    places, block, col = [], 0, 0
    for products in plan.values():
        for product in products:
            for piece in product:
                n = width_of(piece)
                if col + n > BLOCK:
                    block, col = block + 1, 0
                places.append((block, col))
                col += n
    return places, block + 1


def small_layout():
    at, n = {}, 0
    for name, width in (("ln_g", DEPTH * 3 * KD), ("ln_b", DEPTH * 3 * KD), ("conv_w", 3 * KC), ("s5_d", KC),
                        ("b_glu", KC), ("log_dt", PAIRS), ("lam_re", PAIRS), ("lam_im", PAIRS),
                        ("mix_g", KD), ("ffn_g", KD), ("final_g", KD), ("pos_k", CL), ("pos_v", CL),
                        ("sinks", BH), ("b_group", NGRP), ("b_expert", NEXP)):
        at[name] = (n, n + width)
        n += width
    return at, n


def const_layout():
    at, n = {}, 0
    for name, width in (("ident", P), ("mean", P), ("far_causal", T), ("far_256", T), ("far_128", T),
                        ("steps", T), ("swap_a", P), ("swap_i", P), ("inv_a", 1), ("inv_i", 1),
                        ("sgn_a", 1), ("sgn_i", 1), ("far_cmp", TB * (NCMP + 1)), ("see_cmp", TB * (NCMP + 1)),
                        ("expert", NEXP), ("group", EPG)):
        at[name] = (n, n + width)
        n += width
    return at, n


def constants():
    at, n = const_layout()
    c = np.zeros((P, n), np.float32)

    def put(name, value):
        c[:, at[name][0]:at[name][1]] = value

    p = np.arange(P)[:, None]
    put("ident", np.eye(P))
    put("mean", np.full((P, P), 1.0 / D))
    back = (np.arange(T)[None, :] - (T - P)) - p
    for name, window in (("far_causal", T), ("far_256", 256), ("far_128", 128)):
        put(name, np.where((back <= 0) & (back > -window), back, NEG))
    put("steps", np.arange(T)[None, :])
    for name, rot, period, inv in (("a", HD // 4, HD, "inv_a"), ("i", ID // 4, ID, "inv_i")):
        half = rot // 2
        swap, freq, sign = np.zeros((P, P)), np.zeros((P, 1), np.float32), np.ones((P, 1))
        table = np.float32(THETA) ** (-np.arange(0, rot, 2, dtype=np.float32) / np.float32(rot))
        for base in range(0, P, period):
            for j in range(half):
                swap[base + j + half, base + j] = swap[base + j, base + j + half] = 1
                freq[base + j] = freq[base + j + half] = table[j]
                sign[base + j] = -1
        put(f"swap_{name}", swap)
        put(inv, freq)
        put(f"sgn_{name}", 2 * sign)
    end = np.arange(NCMP) * CS + CL - 1
    far = np.full((P, TB, NCMP + 1), NEG, np.float32)
    see = np.zeros((P, TB, NCMP + 1), np.float32)
    for b in range(TB):
        back = end[None, :] - (b * P + p)
        far[:, b, :NCMP] = np.where(back <= 0, back, NEG)
        see[:, b, :NCMP] = back <= 0
    put("far_cmp", far.reshape(P, -1))
    put("see_cmp", see.reshape(P, -1))
    put("expert", np.arange(NEXP)[None, :])
    put("group", np.arange(EPG)[None, :])
    return c


class Queue:

    def __init__(self, done, chained):
        self.done, self.chained, self.count, self.items, self.seen = done, chained, 0, [], {}

    def wait(self, *after):
        for sem, value in after:
            if self.seen.get(id(sem), 0) < value:
                self.seen[id(sem)] = value
                self.items.append(["wait", sem, value])

    def last(self):
        if self.items and self.items[-1][0] == "quiet":
            self.items[-1][0] = "signal"
            self.count += 1
        return (self.done, self.count)

    def do(self, instruction, after=(), free=False):
        if self.chained and not free and self.count:
            self.wait((self.done, self.count))
        self.wait(*after)
        self.count += 1
        self.items.append(["signal", instruction, None])
        return (self.done, self.count)

    def quiet(self, instruction, after=()):
        self.wait(*after)
        self.items.append(["quiet", instruction, None])

    def dma(self, instruction, sem, value, after=()):
        self.wait(*after)
        self.items.append(["dma", instruction, sem])
        return (sem, value)

    def issue(self, engine):
        for kind, what, arg in self.items:
            if kind == "wait":
                engine.wait_ge(what, arg)
            elif kind == "signal":
                what(engine).then_inc(self.done, 1)
            elif kind == "quiet":
                what(engine)
            else:
                what(engine).then_inc(arg, 16)


class Slot:

    def __init__(self, ap):
        self.ap, self.free = ap, []


class Ring:
    def __init__(self, aps):
        self.slots, self.n = [Slot(a) for a in aps], 0

    def take(self):
        for _ in self.slots:
            self.n += 1
            slot = self.slots[(self.n - 1) % len(self.slots)]
            if slot.free is not None:
                free, slot.free = slot.free, None
                return slot, free
        raise AssertionError("every slot is held")


def build(nc, io):
    ctx = ExitStack()
    with ctx:
        build_in(nc, io, ctx)


def build_in(nc, io, ctx):
    def sbuf(name, n, dt=F32):
        return ctx.enter_context(nc.sbuf_tensor(name, [P, n], dt))

    def sem(name):
        return ctx.enter_context(nc.semaphore(name))

    def chunks(ap, c):
        return ap.rearrange("p (c n) -> p c n", c=c)

    const_at, n_const = const_layout()
    small_at, n_small = small_layout()
    const = sbuf("const", n_const)
    small = sbuf("small", n_small)
    ring = sbuf("ring", RING * BLOCK)
    buf_a = chunks(sbuf("buf_a", KD * T)[:, :], KD)
    buf_b = chunks(sbuf("buf_b", KD * T)[:, :], KD)
    norm = sbuf("norm", 4 * T)
    stat = sbuf("stat", 512)
    area = sbuf("area", 24576)
    banks = Ring([ctx.enter_context(nc.psum_tensor(f"bank{i}", [P, T], F32))[:, :] for i in range(8)])
    tables_dram = nc.dram_tensor("turn_tables", [PAIRS, P, 2 * T], F32, kind="Internal").ap()
    combine_dram = nc.dram_tensor("combine", [NEXP, T], F32, kind="Internal").ap()

    def C(name, a=0, b=None):
        lo, hi = const_at[name]
        return const[:, lo + a:hi if b is None else lo + b]

    def S(name, a=0, b=None):
        lo, hi = small_at[name]
        return small[:, lo + a:hi if b is None else lo + b]

    def region(lo, n):
        return area[:, lo:lo + n]

    pe = Queue(sem("tensor_done"), False)
    dve = Queue(sem("vector_done"), True)
    act = Queue(sem("scalar_done"), True)
    pool = Queue(sem("pool_done"), True)
    sp = Queue(sem("sync_done"), False)
    block_loaded = [sem(f"block_loaded{i}") for i in range(RING)]

    def tt(q, out, a, b, op, after=(), free=False):
        return q.do(lambda e: e.tensor_tensor(out, a, b, op), after, free)

    def ts(q, out, a, s1, op0, s2=None, op1=None, after=(), free=False):
        if op1 is None:
            return q.do(lambda e: e.tensor_scalar(out, a, s1, None, op0), after, free)
        return q.do(lambda e: e.tensor_scalar(out, a, s1, s2, op0, op1), after, free)

    def stt(out, a, s, b, op0, op1, after=(), free=False):
        return dve.do(lambda e: e.scalar_tensor_tensor(out, a, s, b, op0, op1), after, free)

    def activate(out, a, func, scale=1.0, bias=0.0, accum=None, after=(), free=False):
        return act.do(lambda e: e.activation(out, a, func, bias=bias, scale=scale, accum_out=accum), after, free)

    def copy(q, out, a, after=(), free=False):
        if q is act:
            return activate(out, a, ACT.Copy, after=after, free=free)
        return q.do(lambda e: e.tensor_copy(out, a), after, free)

    def reciprocal(out, a, after=()):
        return dve.do(lambda e: e.reciprocal(out, a), after)

    def reduce(out, a, op, after=()):
        return dve.do(lambda e: e.tensor_reduce(out, a, AX.X, op), after)

    def scan(out, rate, a, after=()):
        return dve.do(lambda e: e.tensor_tensor_scan(out, rate, a, 0.0, ALU.mult, ALU.add), after)

    def memset(ap, value, after=()):
        return dve.do(lambda e: e.memset(ap, value), after)

    def top_eight(out, a):
        return dve.do(lambda e: e.max(out, a))

    def replace_eight(a, values, by):
        return dve.do(lambda e: e.match_replace(a, values, a, by))

    def where_eight(out, values, a):
        return dve.do(lambda e: e.max_index(out, values, a))

    def load(q, name, out, src, after=()):
        return q.dma(lambda e: e.dma_start(out, src), sem(name), 16, after)

    plan = weight_plan()
    places, n_blocks = place_pieces(plan)
    stream = {"next": 0, "block": -1}

    def load_block(b, after=()):
        slot = b % RING
        sp.dma(lambda e: e.dma_start(ring[:, slot * BLOCK:(slot + 1) * BLOCK], io["weights"][b]),
               block_loaded[slot], 0, after)

    def take(piece):
        block, col = places[stream["next"]]
        stream["next"] += 1
        if block != stream["block"]:
            if stream["block"] >= 0 and stream["block"] + RING < n_blocks:
                load_block(stream["block"] + RING, [pe.last()])
            stream["block"] = block
            pe.wait((block_loaded[block % RING], 16 * (block // RING + 1)))
        at = (block % RING) * BLOCK + col
        return ring[:, at:at + width_of(piece)]

    def matmul(out, lhsT, rhs, start, stop, after=()):
        pe.quiet(lambda e: e.matmul(out, lhsT, rhs, start=start, stop=stop), after)

    def transpose(out, in_, after=()):
        n = in_.shape[0]
        pe.quiet(lambda e: e.transpose(out, in_, C("ident")[0:n, 0:n]), after)

    def product(pieces, x, after=(), bank=None, start=True, stop=True, n=T):
        if bank is None:
            bank, free = banks.take()
            pe.wait(*free)
        pe.wait(*after)
        for k, piece in enumerate(pieces):
            w = take(piece)
            matmul(bank.ap[0:w.shape[1], 0:n], w, x[k], start and k == 0, stop and k == len(pieces) - 1)
        return bank, pe.last()

    def tokens_product(pieces, x, width, after=()):
        out = []
        for _ in range(TB):
            bank, free = banks.take()
            pe.wait(*free)
            out.append(bank)
        pe.wait(*after)
        for k, piece in enumerate(pieces):
            w = take(piece)
            for b in range(TB):
                matmul(out[b].ap[:, 0:width], x[k][:, b * P:(b + 1) * P], w, k == 0, k == len(pieces) - 1)
        return out, pe.last()

    for b in range(RING):
        load_block(b)
    x_loaded = load(act, "x_loaded", buf_a, io["x"].rearrange("(c p) t -> p c t", p=P))
    const_loaded = load(act, "const_loaded", const[:, :], io["const"])
    small_loaded = load(act, "small_loaded", small[:, :], io["small"])

    mean, rstd = norm[:, 0:T], norm[:, T:2 * T]
    squares = Ring([norm[:, (2 + i) * T:(3 + i) * T] for i in range(2)])
    one_over_d = C("mean")

    def column_sums(x, ready):
        bank, free = banks.take()
        pe.wait(*free)
        pe.wait(const_loaded)
        for k in range(KD):
            matmul(bank.ap, one_over_d, x[k], k == 0, k == KD - 1, [ready[k]])
        return bank, pe.last()

    def inverse_root(bank, summed, eps):
        a = ts(dve, rstd, bank.ap, eps, ALU.add, after=[summed])
        bank.free = [a]
        a = activate(rstd, rstd, ACT.Sqrt, after=[a])
        return reciprocal(rstd, rstd, [a])

    def layer_norm(src, ready, dst, g, b):
        bank, summed = column_sums([src[:, k, :] for k in range(KD)], ready)
        centred, squared = [], []
        sq_bank, free = banks.take()
        pe.wait(*free)
        for k in range(KD):
            centred.append(tt(dve, src[:, k, :], src[:, k, :], bank.ap, ALU.subtract, after=[summed], free=k > 0))
            slot, free = squares.take()
            done = activate(slot.ap, src[:, k, :], ACT.Square, after=free + [centred[k]])
            matmul(sq_bank.ap, one_over_d, slot.ap, k == 0, k == KD - 1, [done])
            slot.free = [pe.last()]
        bank.free = [centred[-1]]
        r = inverse_root(sq_bank, pe.last(), LN_EPS)
        out = []
        for k in range(KD):
            n = tt(dve, src[:, k, :], src[:, k, :], rstd, ALU.mult, after=[r], free=k > 0)
            out.append(activate(dst[:, k, :], src[:, k, :], ACT.Identity, scale=S("ln_g", g + k, g + k + 1),
                                bias=S("ln_b", b + k, b + k + 1), after=[n, small_loaded]))
        return out

    def rms_norm(src, ready, dst, g):
        bank, free = banks.take()
        pe.wait(*free)
        for k in range(KD):
            slot, free = squares.take()
            done = activate(slot.ap, src[:, k, :], ACT.Square, after=free + [ready[k]])
            matmul(bank.ap, one_over_d, slot.ap, k == 0, k == KD - 1, [done])
            slot.free = [pe.last()]
        r = inverse_root(bank, pe.last(), RMS_EPS)
        return [stt(dst[:, k, :], src[:, k, :], S(g, k, k + 1), rstd, ALU.mult, ALU.mult,
                    after=[r, small_loaded], free=k > 0) for k in range(KD)]

    def ffn(name, h, ready, r, aside=()):
        aside = list(aside)
        hidden = chunks(region(0, KF * T), KF)
        x = [h[:, k, :] for k in range(KD)]
        written = []
        for m in range(KF):
            gate, g_done = product(plan[name + "_up"][2 * m], x, ready)
            up, u_done = product(plan[name + "_up"][2 * m + 1], x)
            a = activate(hidden[:, m, :], gate.ap, ACT.Silu, after=[g_done])
            gate.free = [a]
            v = tt(dve, hidden[:, m, :], hidden[:, m, :], up.ap, ALU.mult, after=[a, u_done])
            up.free = [v]
            written.append(v)
            if aside:
                aside.pop(0)()
        out = []
        for m in range(KD):
            bank, done = product(plan[name + "_down"][m], [hidden[:, k, :] for k in range(KF)], written)
            a = activate(r[:, m, :], bank.ap, ACT.Copy, scale=0.5, after=[done])
            bank.free = [a]
            out.append(stt(r[:, m, :], h[:, m, :], ALPHA, r[:, m, :], ALU.mult, ALU.add, after=[a] + ready))
            if aside:
                aside.pop(0)()
        assert not aside
        return out

    def ple(layer, h, ready, r):
        pt = chunks(region(0, 2 * T), 2)
        p_loaded = load(act, f"p_loaded{layer}", pt, io["p"][layer].rearrange("(c p) t -> p c t", p=P),
                        [pe.last()])
        gates = Ring([region((2 + i) * T, T) for i in range(2)])
        out = []
        for m in range(KD):
            gate, g_done = product(plan[f"ple{layer}"][2 * m], [h[:, k, :] for k in range(KD)], ready)
            proj, p_done = product(plan[f"ple{layer}"][2 * m + 1], [pt[:, k, :] for k in range(2)], [p_loaded])
            s, free = gates.take()
            a = activate(s.ap, gate.ap, ACT.Sigmoid, after=free + [g_done, pe.last()])
            gate.free = [a]
            v = tt(dve, s.ap, s.ap, proj.ap, ALU.mult, after=[a, p_done])
            proj.free = [v]
            v = tt(dve, r[:, m, :], s.ap, h[:, m, :], ALU.add, after=ready)
            s.free = [v]
            out.append(v)
        return out

    def reduce_angle(r, k, x):
        ts(dve, k, x, 1.0 / (2 * PI), ALU.mult, ROUND, ALU.add)
        ts(dve, k, k, -ROUND, ALU.add)
        stt(r, k, -TWO_PI_1, x, ALU.mult, ALU.add)
        stt(r, k, -TWO_PI_2, r, ALU.mult, ALU.add)
        return stt(r, k, -TWO_PI_3, r, ALU.mult, ALU.add)

    def sin_cos(sin, cos, r, half, double, after=()):
        a = activate(sin, r, ACT.Sin, scale=half, after=after)
        v = stt(cos, r, -1.0, r, ALU.mult, ALU.max, after=after)
        v = ts(dve, cos, cos, -half, ALU.mult, PI / 2, ALU.add)
        c = activate(r, cos, ACT.Sin, after=[v, a])
        v = tt(dve, cos, sin, sin, ALU.mult, after=[c])
        v = ts(dve, cos, cos, -2.0, ALU.mult, 1.0, ALU.add)
        return stt(sin, sin, double, r, ALU.mult, ALU.mult, after=[c])

    BASE = KF * T
    bt_re = chunks(region(BASE, PAIRS * P), PAIRS)
    bt_im = chunks(region(BASE + PAIRS * P, PAIRS * P), PAIRS)
    c_re = chunks(region(BASE + 2 * PAIRS * P, PAIRS * P), PAIRS)
    c_im = chunks(region(BASE + 3 * PAIRS * P, PAIRS * P), PAIRS)
    top = BASE + 4 * PAIRS * P
    assert top + 5 * T <= 24576
    work = [region(top + i * T, T) for i in range(5)]
    st = [stat[:, i * PAIRS:(i + 1) * PAIRS] for i in range(16)]
    mag, f_re, f_im, nf_im, turn_hi, turn_lo = st[0:6]
    s5 = {}

    def s5_factors():
        dt, lr, x, r, k, sn, cs, den, t = st[6:15]
        w = [const_loaded, small_loaded]
        a = activate(dt, S("log_dt"), ACT.Exp, after=w)
        ts(dve, lr, S("lam_re"), -1e-4, ALU.min, after=w)
        tt(dve, x, S("lam_im"), dt, ALU.mult, after=[a])
        tt(dve, mag, lr, dt, ALU.mult)
        v = reduce_angle(r, k, x)
        a = activate(mag, mag, ACT.Exp, after=[v])
        v = ts(dve, turn_hi, r, 1.0 / (2 * PI), ALU.mult)
        ts(dve, turn_lo, turn_hi, ROUND13, ALU.add)
        ts(dve, k, turn_lo, -ROUND13, ALU.add)
        tt(dve, turn_lo, turn_hi, k, ALU.subtract)
        v = copy(dve, turn_hi, k)
        sin_cos(sn, cs, r, 0.5, 2.0, [v])
        tt(dve, cs, cs, mag, ALU.mult, after=[a])
        ts(dve, cs, cs, -1.0, ALU.add)
        tt(dve, sn, sn, mag, ALU.mult)
        tt(dve, den, lr, lr, ALU.mult)
        tt(dve, t, S("lam_im"), S("lam_im"), ALU.mult)
        tt(dve, den, den, t, ALU.add)
        reciprocal(den, den)
        tt(dve, f_re, cs, lr, ALU.mult)
        tt(dve, t, sn, S("lam_im"), ALU.mult)
        tt(dve, f_re, f_re, t, ALU.add)
        tt(dve, f_re, f_re, den, ALU.mult)
        tt(dve, f_im, sn, lr, ALU.mult)
        tt(dve, t, cs, S("lam_im"), ALU.mult)
        tt(dve, f_im, f_im, t, ALU.subtract)
        tt(dve, f_im, f_im, den, ALU.mult)
        s5["factors"] = ts(dve, nf_im, f_im, -1.0, ALU.mult)

    def s5_c():
        a = load(act, "c_re_loaded", c_re, io["c_re"])
        b = load(act, "c_im_loaded", c_im, io["c_im"])
        s5["c"] = [a, ts(dve, c_im, c_im, -1.0, ALU.mult, after=[b])]

    b_slots = Ring([work[i] for i in range(2)])
    b_sems = [sem("b_loaded0"), sem("b_loaded1")]
    s5["b"] = []

    def s5_b(q):
        slot, free = b_slots.take()
        br, bi, fr, fi = (slot.ap[:, i * P:(i + 1) * P] for i in range(4))
        loaded = act.dma(lambda e: e.dma_start(slot.ap[:, 0:2 * P], io["b"][q]), b_sems[q % 2], 16 * (q // 2 + 1), free)
        a = s5["factors"]
        ts(dve, fr, br, f_re[:, q:q + 1], ALU.mult, after=[loaded, a])
        ts(dve, fi, bi, f_re[:, q:q + 1], ALU.mult)
        stt(fr, bi, nf_im[:, q:q + 1], fr, ALU.mult, ALU.add)
        v = stt(fi, br, f_im[:, q:q + 1], fi, ALU.mult, ALU.add)
        bank, free = banks.take()
        pe.wait(*free)
        transpose(bank.ap[:, 0:P], fr, [v])
        transpose(bank.ap[:, P:2 * P], fi)
        slot.free = [pe.last()]
        a = copy(act, bt_re[:, q, :], bank.ap[:, 0:P], [pe.last()])
        a = copy(act, bt_im[:, q, :], bank.ap[:, P:2 * P])
        bank.free = [a]
        s5["b"].append(a)

    table_sems = [sem("table_stored0"), sem("table_stored1")]
    tables = Ring([region(top + 2 * T, 2 * T)])
    s5["tables"] = []

    def s5_turn(q):
        slot, free = tables.take()
        cos, sin = slot.ap[:, 0:T], slot.ap[:, T:2 * T]
        r = work[4]
        steps = C("steps")
        ts(dve, r, steps, turn_hi[:, q:q + 1], ALU.mult, after=free + [s5["factors"]])
        ts(dve, cos, r, ROUND, ALU.add, -ROUND, ALU.add)
        tt(dve, r, r, cos, ALU.subtract)
        v = stt(r, steps, turn_lo[:, q:q + 1], r, ALU.mult, ALU.add)
        v = sin_cos(sin, cos, r, PI, 2.0, [v])
        n = len(s5["tables"])
        stored = act.dma(lambda e: e.dma_start(tables_dram[q], slot.ap), table_sems[n % 2], 16 * (n // 2 + 1), [v])
        slot.free = [stored]
        s5["tables"].append(stored)

    def mixer_ab(h, ready, r):
        hc = chunks(region(0, KC * T), KC)
        u = chunks(region(KC * T, KC * T), KC)
        y = chunks(region(2 * KC * T, KC * T), KC)
        gb = chunks(region(3 * KC * T, KC * T), KC)
        pad = region(4 * KC * T, T + 2)
        x = [h[:, k, :] for k in range(KD)]
        hc_done, gb_done = [], []
        zeroed = memset(pad[:, 0:2], 0.0, [pe.last()])
        for m in range(KC):
            bank, done = product(plan["ab_in"][m], x, ready)
            hc_done.append(copy(act, hc[:, m, :], bank.ap, [done]))
            bank.free = [hc_done[-1]]
        for m in range(KC):
            bank, done = product(plan["ab_in"][KC + m], x)
            gb_done.append(copy(act, gb[:, m, :], bank.ap, [done]))
            bank.free = [gb_done[-1]]
        conv = []
        for m in range(KC):
            bank, done = product(plan["ab_in"][2 * KC + m], x)
            v = tt(dve, pad[:, 2:T + 2], hc[:, m, :], bank.ap, ALU.mult, after=[done, hc_done[m], zeroed])
            bank.free = [v]
            w = [S("conv_w", j * KC + m, j * KC + m + 1) for j in range(3)]
            ts(dve, hc[:, m, :], pad[:, 0:T], w[0], ALU.mult)
            stt(hc[:, m, :], pad[:, 1:T + 1], w[1], hc[:, m, :], ALU.mult, ALU.add)
            stt(hc[:, m, :], pad[:, 2:T + 2], w[2], hc[:, m, :], ALU.mult, ALU.add)
            conv.append(tt(dve, hc[:, m, :], hc[:, m, :], gb[:, m, :], ALU.mult, after=[gb_done[m]]))
        u_done = []
        for m in range(KC):
            bank, done = product(plan["ab_in"][3 * KC + m], x)
            u_done.append(copy(act, u[:, m, :], bank.ap, [done]))
            bank.free = [u_done[-1]]
        spare = 3 * KC * T
        turn = Ring([region(spare, 2 * T), region(spare + 2 * T, 2 * T)])
        turn_sems = [sem("turn_loaded0"), sem("turn_loaded1")]
        sets = Ring([(region(4 * KC * T, 5 * T)), region(top, 5 * T)])
        states = Ring([norm[:, 2 * T:4 * T]])
        assert 4 * KC * T + 5 * T <= BASE
        y_done = []
        for ct in range(KC):
            y_bank, free = banks.take()
            pe.wait(*free)
            for q in range(ct * PPC, (ct + 1) * PPC):
                tslot, free = turn.take()
                loaded = act.dma(lambda e, q=q, tslot=tslot: e.dma_start(tslot.ap, tables_dram[q]),
                                 turn_sems[q % 2], 16 * (q // 2 + 1), free + [conv[-1]] + s5["tables"])
                cos, sin = tslot.ap[:, 0:T], tslot.ap[:, T:2 * T]
                banks_b = []
                for w in (bt_re, bt_im):
                    bank, free = banks.take()
                    pe.wait(*free)
                    matmul(bank.ap, w[:, q, :], u[:, ct, :], True, True, [u_done[ct]] + s5["b"])
                    banks_b.append(bank)
                done = pe.last()
                wslot, free = sets.take()
                b_re, b_im, v_re, v_im, t1 = (wslot.ap[:, i * T:(i + 1) * T] for i in range(5))
                a_re = copy(act, b_re, banks_b[0].ap, [done, conv[-1]] + free)
                a_im = copy(act, b_im, banks_b[1].ap)
                banks_b[0].free, banks_b[1].free = [a_re], [a_im]
                tt(dve, v_re, b_re, cos, ALU.mult, after=[loaded, a_re] + free)
                tt(dve, t1, b_im, sin, ALU.mult, after=[a_im])
                tt(dve, v_re, v_re, t1, ALU.add)
                tt(pool, v_im, b_im, cos, ALU.mult, after=[loaded, a_im] + free)
                g = tt(pool, b_re, b_re, sin, ALU.mult, after=[dve.last()])
                g = tt(pool, v_im, v_im, b_re, ALU.subtract)
                sslot, free = states.take()
                z_re, z_im = sslot.ap[:, 0:T], sslot.ap[:, T:2 * T]
                rate = mag[:, q:q + 1].to_broadcast([P, T])
                scan(z_re, rate, v_re, free)
                v = scan(z_im, rate, v_im, [g])
                tt(pool, v_im, z_re, sin, ALU.mult, after=[v])
                tt(pool, t1, z_im, cos, ALU.mult)
                g = tt(pool, v_im, v_im, t1, ALU.add)
                tt(dve, v_re, z_re, cos, ALU.mult)
                tt(dve, b_im, z_im, sin, ALU.mult)
                v = tt(dve, v_re, v_re, b_im, ALU.subtract)
                sslot.free = [v, g]
                tslot.free = [v, g]
                first = q % PPC == 0
                matmul(y_bank.ap, c_re[:, q, :], v_re, first, False, [v] + s5["c"])
                matmul(y_bank.ap, c_im[:, q, :], v_im, False, q % PPC == PPC - 1, [g])
                wslot.free = [pe.last()]
            v = stt(y[:, ct, :], u[:, ct, :], S("s5_d", ct, ct + 1), y_bank.ap, ALU.mult, ALU.add, after=[pe.last()])
            y_bank.free = [v]
            y_done.append(v)
        z_done = []
        c2 = 2.0 * float(np.sqrt(2.0 / np.pi))
        for m in range(KC):
            t1, t2 = gb[:, 0, :], gb[:, 1, :]
            tt(dve, t1, y[:, m, :], y[:, m, :], ALU.mult)
            ts(dve, t1, t1, 0.044715, ALU.mult, 1.0, ALU.add)
            v = tt(dve, t1, t1, y[:, m, :], ALU.mult)
            a = activate(t2, t1, ACT.Sigmoid, scale=c2, after=[v])
            z_done.append(tt(dve, y[:, m, :], y[:, m, :], t2, ALU.mult, after=[a]))
        o_done = []
        for m in range(KC):
            bank, done = product(plan["glu"][m], [y[:, k, :] for k in range(KC)], z_done)
            a = activate(gb[:, 2 + m % 2, :], bank.ap, ACT.Sigmoid, bias=S("b_glu", m, m + 1), after=[done] + z_done + o_done)
            bank.free = [a]
            o_done.append(tt(dve, u[:, m, :], y[:, m, :], gb[:, 2 + m % 2, :], ALU.mult, after=[a]))
        cat = [hc[:, k, :] for k in range(KC)] + [u[:, k, :] for k in range(KC)]
        return residual("ab_out", cat, conv + o_done, h, r)

    def residual(name, x, x_ready, h, r):
        out = []
        for m in range(KD):
            bank, done = product(plan[name][m], x, x_ready)
            v = stt(r[:, m, :], h[:, m, :], ALPHA, bank.ap, ALU.mult, ALU.add, after=[done] + x_ready)
            bank.free = [v]
            out.append(v)
        return out

    def turn_probabilities(p_ap, n, dst, p_ready, evac):
        bank, free = banks.take()
        pe.wait(*free)
        nch = -(-n // P)
        for c in range(nch):
            w = min(P, n - c * P)
            transpose(bank.ap[0:w, c * P:(c + 1) * P], p_ap[:, c * P:c * P + w], [p_ready])
        rows = min(P, n)
        a = copy(evac, dst[0:rows, 0:nch * P], bank.ap[0:rows, 0:nch * P], [pe.last()])
        bank.free = [a]
        return a

    def mixer_c(h, ready, r):
        at = [0]

        def get(n):
            at[0] += n
            assert at[0] <= 24576
            return region(at[0] - n, n)

        x = [h[:, k, :] for k in range(KD)]
        qT, kT = chunks(get(HEADS * T), HEADS), chunks(get(KVH * T), KVH)
        qi, ki = chunks(get(4 * T), 4), get(T)
        v_tok = chunks(get(TB * 256), TB)
        wi = chunks(get(TB * IH), TB)
        bias = [get((b + 1) * P) for b in range(TB)]
        rope = {n: (get(T), get(T)) for n in "ai"}
        raws = Ring([get(T) for _ in range(2)])
        score = get(T)
        relus = Ring([get(T) for _ in range(2)])
        begin = [pe.last()]
        pos_i, ang, kk = raws.slots[0].ap, score, relus.slots[0].ap
        pos_loaded = load(act, "pos_loaded", pos_i.bitcast(I32), io["positions"], begin)
        pos = relus.slots[1].ap
        copy(dve, pos, pos_i.bitcast(I32), [pos_loaded] + begin)
        rope_ready = []
        for n in "ai":
            cos, sin = rope[n]
            ts(dve, ang, pos, C(f"inv_{n}"), ALU.mult)
            v = reduce_angle(ang, kk, ang)
            rope_ready.append(sin_cos(sin, cos, ang, 0.5, C(f"sgn_{n}"), [v]))

        def rotated(pieces, dst, n):
            cos, sin = rope[n]
            bank, done = product(pieces, x, ready)
            slot, free = raws.take()
            a = copy(act, slot.ap, bank.ap, [done, rope_ready[0]] + free)
            bank.free = [a]
            other, free = banks.take()
            matmul(other.ap, C(f"swap_{n}"), slot.ap, True, True, free + [a])
            done = pe.last()
            tt(pool, dst, slot.ap, cos, ALU.mult, after=[a] + rope_ready)
            g = pool.last()
            v = tt(dve, slot.ap, other.ap, sin, ALU.mult, after=[done, g])
            other.free = [v]
            v = tt(dve, dst, dst, slot.ap, ALU.add)
            slot.free = [v]
            return v

        qi_ready = [rotated(plan["c_index"][m], qi[:, m, :], "i") for m in range(4)]
        ki_ready = rotated(plan["c_index"][4], ki, "i")
        outs, done = tokens_product(plan["c_weight"][0], x, IH)
        for b in range(TB):
            wi_ready = ts(dve, wi[:, b, :], outs[b].ap[:, 0:IH], float(IH ** -0.5 * ID ** -0.5), ALU.mult, after=[done])
            outs[b].free = [wi_ready]
        outs, done = tokens_product(plan["c_value"][0], x, 256)
        v_ready = []
        for b in range(TB):
            v_ready.append(copy(act, v_tok[:, b, :], outs[b].ap[:, 0:256], [done]))
            outs[b].free = [v_ready[-1]]
        bias_ready = []
        top8 = stat[:, 0:8]
        for b in range(TB):
            n = (b + 1) * P
            far = C("far_causal", T - P - b * P, T)
            if b == 0:
                bias_ready.append(ts(dve, bias[b], far, -1e29, ALU.is_le, NEG, ALU.mult))
                continue
            for i in range(IH):
                half = slice((i % 2) * ID, (i % 2 + 1) * ID)
                bank, free = banks.take()
                matmul(bank.ap[:, 0:n], qi[half, i // 2, b * P:(b + 1) * P], ki[half, 0:n], True, True,
                       free + qi_ready + [ki_ready])
                done = pe.last()
                slot, free = relus.take()
                a = activate(slot.ap[:, 0:n], bank.ap[:, 0:n], ACT.Relu, after=[done] + free + rope_ready)
                bank.free = [a]
                w = wi[:, b, i:i + 1]
                if i == 0:
                    v = ts(dve, score[:, 0:n], slot.ap[:, 0:n], w, ALU.mult, after=[a])
                else:
                    v = stt(score[:, 0:n], slot.ap[:, 0:n], w, score[:, 0:n], ALU.mult, ALU.add, after=[a])
                slot.free = [v]
            slot, free = relus.take()
            ts(dve, slot.ap[:, 0:n], far, -1e29, ALU.is_le, CAUSAL_FILL, ALU.mult, after=free)
            v = tt(dve, score[:, 0:n], score[:, 0:n], slot.ap[:, 0:n], ALU.add)
            slot.free = [v]
            for _ in range(TOPK // 8):
                top_eight(top8, score[:, 0:n])
                replace_eight(score[:, 0:n], top8, TAKEN)
            bias_ready.append(ts(dve, bias[b], score[:, 0:n], -2e38, ALU.is_ge, NEG, ALU.mult))
        qk_ready = []
        for m in range(HEADS + KVH):
            qk_ready.append(rotated(plan["c_qk"][m], qT[:, m, :] if m < HEADS else kT[:, m - HEADS, :], "a"))
        logits = Ring([raws.slots[0].ap, raws.slots[1].ap])
        turned = Ring([relus.slots[0].ap, relus.slots[1].ap, rope["i"][0], rope["i"][1]])
        stats = Ring([stat[:, 16 + 4 * i:20 + 4 * i] for i in range(4)])
        scale = float(HD ** -0.5)
        items = [(hd, b) for hd in range(HEADS) for b in range(TB)]
        state, o_ready, o_bank = {}, [], {}

        def scores(i):
            hd, b = items[i]
            n = (b + 1) * P
            bank, free = banks.take()
            matmul(bank.ap[:, 0:n], qT[:, hd, b * P:(b + 1) * P], kT[:, hd // 4, 0:n], True, True, free + qk_ready)
            state[i] = (bank, pe.last())

        def weigh(i):
            hd, b = items[i]
            n = (b + 1) * P
            bank, done = state[i]
            slot, free = logits.take()
            l = slot.ap[:, 0:n]
            st, sfree = stats.take()
            m, z = st.ap[:, 0:1], st.ap[:, 1:2]
            v = tt(dve, l, bias[b], bank.ap[:, 0:n], ALU.add, after=[done] + free + sfree + qk_ready)
            bank.free = [v]
            reduce(m, l, ALU.max)
            v = ts(dve, m, m, -scale, ALU.mult)
            a = activate(l, l, ACT.Exp, scale=scale, bias=m, accum=z, after=[v])
            reciprocal(z, z, [a])
            v = ts(dve, l, l, z, ALU.mult)
            st.free = [v]
            state[i] = (slot, v)

        def attend(i):
            hd, b = items[i]
            n = (b + 1) * P
            slot, p_ready = state[i]
            pt, free = turned.take()
            pe.wait(*free)
            act.wait(*free)
            a = turn_probabilities(slot.ap, n, pt.ap, p_ready, act)
            slot.free = [pe.last()]
            if b == 0:
                o_bank[hd], free = banks.take()
                pe.wait(*free)
            for c in range(b + 1):
                matmul(o_bank[hd].ap[:, b * P:(b + 1) * P], v_tok[:, c, (hd // 4) * HD:(hd // 4 + 1) * HD],
                       pt.ap[:, c * P:(c + 1) * P], c == 0, c == b, [a] + v_ready)
            pt.free = [pe.last()]
            if b == TB - 1:
                o_ready.append(copy(act, qT[:, hd, :], o_bank[hd].ap, [pe.last()]))
                o_bank[hd].free = [o_ready[-1]]

        scores(0)
        for i in range(len(items) + 1):
            if i + 1 < len(items):
                scores(i + 1)
            if i < len(items):
                weigh(i)
            if i >= 1:
                attend(i - 1)
        return residual("c_out", [qT[:, k, :] for k in range(HEADS)], o_ready, h, r)

    def nsa(h, ready, r, r_ready):
        at = [0]

        def get(n):
            at[0] += n
            assert at[0] <= 24576, at[0]
            return region(at[0] - n, n)

        x = [h[:, k, :] for k in range(KD)]
        begin = [pe.last()] + r_ready
        q = chunks(get(8 * T), 8)
        keys = chunks(get(3 * T), 3)
        vals = chunks(get(TB * 384), TB)
        gate = chunks(get(TB * 24), TB)
        kc = get(NCMP + 1)
        vc = get(P)
        merge_at = at[0]
        cmp_in = [get(T) for _ in range(2)]
        blocks = chunks(get(CL * 2 * NCMP), CL)
        hid = [[get(2 * NCMP) for _ in range(2)] for _ in range(2)]
        sig = get(2 * NCMP)
        hid_ready = [[], []]
        cin = []
        for c in range(2):
            bank, done = product(plan["b_compress_in"][c], x, ready)
            cin.append(copy(act, cmp_in[c], bank.ap, [done] + begin))
            bank.free = [cin[-1]]
        for c in range(2):
            z = memset(blocks, 0.0, [pe.last()] + begin)
            for kv in range(2):
                half = slice(kv * BD, (kv + 1) * BD)
                for l in range(2):
                    src = cmp_in[c][half, l * CS:l * CS + NCMP * CS].rearrange("p (b l) -> p l b", l=CS)
                    dst = blocks[half, l * CS:(l + 1) * CS, kv * NCMP:(kv + 1) * NCMP]
                    pos = S("pos_k" if c == 0 else "pos_v", l * CS, (l + 1) * CS)[half, :]
                    v = tt(dve, dst, src, pos.unsqueeze(2).to_broadcast([BD, CS, NCMP]), ALU.add, after=[cin[c]])
            for m in range(2):
                bank, free = banks.take()
                pe.wait(*free)
                pieces = plan["b_compress"][2 * c + m]
                for l in range(CL):
                    w = take(pieces[l])
                    matmul(bank.ap[:, 0:2 * NCMP], w, blocks[:, l, :], l == 0, l == CL - 1, [v])
                a = activate(hid[c][m], bank.ap[:, 0:2 * NCMP], ACT.Silu, after=[pe.last()])
                bank.free = [a]
                hid_ready[c].append(a)
        bank, free = banks.take()
        for k in range(2):
            w = take(plan["b_compress_k"][0][k])
            matmul(bank.ap[:, 0:2 * NCMP], w, hid[0][k], k == 0, k == 1, free + hid_ready[0])
        done = pe.last()
        for kv in range(2):
            half = slice(kv * BD, (kv + 1) * BD)
            cmp_ready = copy(dve, kc[half, 0:NCMP], bank.ap[half, kv * NCMP:(kv + 1) * NCMP], [done])
        bank.free = [cmp_ready]
        bank, free = banks.take()
        pe.wait(*free)
        ws = [take(plan["b_compress_v"][0][k]) for k in range(2)]
        for kv in range(2):
            for k in range(2):
                matmul(bank.ap[0:NCMP, kv * BD:(kv + 1) * BD], hid[1][k][:, kv * NCMP:(kv + 1) * NCMP], ws[k],
                       k == 0, k == 1, hid_ready[1])
        vc_ready = copy(dve, vc[0:NCMP, :], bank.ap[0:NCMP, 0:P], [pe.last()])
        bank.free = [vc_ready]
        outs, done = tokens_product(plan["b_value"][0], x, 384)
        for b in range(TB):
            v_ready = copy(act, vals[:, b, :], outs[b].ap[:, 0:384], [done])
            outs[b].free = [v_ready]
        outs, done = tokens_product(plan["b_gate"][0], x, 24)
        for b in range(TB):
            gate_ready = activate(gate[:, b, :], outs[b].ap[:, 0:24], ACT.Sigmoid, after=[done])
            outs[b].free = [gate_ready]
        k_ready = []
        for i in range(3):
            bank, done = product(plan["b_key"][i], x)
            k_ready.append(copy(act, keys[:, i, :], bank.ap, [done]))
            bank.free = [k_ready[-1]]
        q_ready = []
        for j in range(8):
            bank, done = product(plan["b_query"][j], x)
            q_ready.append(activate(q[:, j, :], bank.ap, ACT.Copy, scale=float(BD ** -0.5), after=[done]))
            bank.free = [q_ready[-1]]
        at[0] = merge_at
        freed = [pe.last(), (dve.done, dve.count), (act.done, act.count)]
        logits = Ring([get(T) for _ in range(8)])
        turned = Ring([get(T) for _ in range(6)])
        m_at = at[0]
        stats = Ring([stat[:, 16 + 8 * i:24 + 8 * i] for i in range(12)])
        inputs = q_ready + k_ready + [v_ready, gate_ready, cmp_ready, vc_ready]

        def branches(kind, head, b):
            if kind == "b":
                return [("swa", max(0, b - 1) * P)]
            return [("cmp", 0), ("slc", 0), ("win", max(0, b - 2) * P)]

        items = [(kind, j, kv, b) for kind in "ab" for j in range(4) for kv in range(2) for b in range(TB)]
        state, o_ready, o_bank = {}, [], {}
        far_of = {"slc": "far_causal", "win": "far_256", "swa": "far_128"}
        key_of = {"slc": 0, "win": 1, "swa": 2}

        def span(name, s0, b):
            return NCMP if name == "cmp" else (b + 1) * P - s0

        def scores(i):
            kind, j, kv, b = items[i]
            half = slice(kv * BD, (kv + 1) * BD)
            qq = q[half, j + (4 if kind == "b" else 0), b * P:(b + 1) * P]
            got = []
            for name, s0 in branches(kind, j + 4 * kv, b):
                n = span(name, s0, b)
                bank, free = banks.take()
                kk = kc[half, 0:NCMP] if name == "cmp" else keys[half, key_of[name], s0:s0 + n]
                matmul(bank.ap[:, 0:n], qq, kk, True, True, free + inputs)
                got.append((name, s0, bank, pe.last()))
            state[i] = got

        def weigh(i):
            kind, j, kv, b = items[i]
            head = j + 4 * kv
            got = []
            for name, s0, bank, done in state[i]:
                n = span(name, s0, b)
                slope = float(SLOPES[head + (0 if name == "swa" else 8)])
                slot, free = logits.take()
                l = slot.ap[:, 0:n]
                st, sfree = stats.take()
                m, z, w = (st.ap[:, c:c + 1] for c in range(3))
                far = (C("far_cmp", b * (NCMP + 1), b * (NCMP + 1) + NCMP) if name == "cmp" else
                       C(far_of[name], T - P - b * P + s0, T))
                v = stt(l, far, slope, bank.ap[:, 0:n], ALU.mult, ALU.add, after=[done] + free + sfree + freed + inputs)
                bank.free = [v]
                reduce(m, l, ALU.max)
                if name == "swa":
                    ts(dve, m, m, S("sinks", head, head + 1), ALU.max)
                v = ts(dve, m, m, -1.0, ALU.mult)
                if name == "swa":
                    activate(w, S("sinks", head, head + 1), ACT.Exp, bias=m, after=[v])
                a = activate(l, l, ACT.Exp, bias=m, accum=z, after=[v])
                if name == "cmp":
                    tt(dve, l, l, C("see_cmp", b * (NCMP + 1), b * (NCMP + 1) + NCMP), ALU.mult, after=[a])
                    reduce(z, l, ALU.add)
                    ts(dve, z, z, 1e-30, ALU.max)
                if name == "swa":
                    tt(dve, z, z, w, ALU.add, after=[a])
                reciprocal(z, z, [a])
                if name != "swa":
                    g = 3 * head + {"cmp": 0, "slc": 1, "win": 2}[name]
                    tt(dve, z, z, gate[:, b, g:g + 1], ALU.mult)
                v = ts(dve, l, l, z, ALU.mult)
                st.free = [v]
                got.append((name, s0, slot, v))
            state[i] = got

        def attend(i):
            kind, j, kv, b = items[i]
            rows = slice(kv * BD, (kv + 1) * BD)
            pts = []
            for name, s0, slot, p_ready in state[i]:
                pt, free = turned.take()
                act.wait(*free)
                a = turn_probabilities(slot.ap, span(name, s0, b), pt.ap, p_ready, act)
                slot.free = [pe.last()]
                pts.append((name, s0, pt, a))
            if b == 0:
                o_bank[kv], free = banks.take()
                pe.wait(*free)
            steps = []
            for name, s0, pt, a in pts:
                if name == "cmp":
                    steps.append((vc[0:NCMP, kv * BD:(kv + 1) * BD], pt.ap[0:NCMP, 0:P], a))
                    continue
                for c in range(span(name, s0, b) // P):
                    col = key_of[name] * P + kv * BD
                    steps.append((vals[:, s0 // P + c, col:col + BD], pt.ap[:, c * P:(c + 1) * P], a))
            for n, (w, p, a) in enumerate(steps):
                matmul(o_bank[kv].ap[rows, b * P:(b + 1) * P], w, p, n == 0, n == len(steps) - 1, [a])
            for _, _, pt, _ in pts:
                pt.free = [pe.last()]
            if b == TB - 1:
                o_ready.append(copy(act, q[rows, j + (4 if kind == "b" else 0), :], o_bank[kv].ap[rows, :], [pe.last()]))
                o_bank[kv].free = [o_ready[-1]]

        scores(0)
        for i in range(len(items) + 1):
            if i < len(items):
                weigh(i)
            if i + 1 < len(items):
                scores(i + 1)
            if i >= 1:
                attend(i - 1)
        at[0] = 8 * T
        mix = chunks(get(KD * T), KD)
        tmp = Ring([get(2 * T) for _ in range(2)])
        done_all = [pe.last(), (act.done, act.count), (dve.done, dve.count)]
        mix_ready = []
        for m in range(KD):
            pc = plan["b_merge"][4 * m:4 * m + 4]
            ga, ga_done = product(pc[0], x)
            gb, gb_done = product(pc[1], x)
            pa, pa_done = product(pc[2], [q[:, k, :] for k in range(4)], o_ready)
            pb, pb_done = product(pc[3], [q[:, 4 + k, :] for k in range(4)])
            slot, free = tmp.take()
            t1, t2 = slot.ap[:, 0:T], slot.ap[:, T:2 * T]
            a1 = activate(t1, ga.ap, ACT.Sigmoid, after=[ga_done] + free + done_all)
            a2 = activate(t2, gb.ap, ACT.Sigmoid, after=[gb_done])
            ga.free, gb.free = [a1], [a2]
            v1 = tt(dve, t1, t1, pa.ap, ALU.mult, after=[a1, pa_done])
            v2 = tt(dve, t2, t2, pb.ap, ALU.mult, after=[a2, pb_done])
            pa.free, pb.free = [v1], [v2]
            v = tt(dve, mix[:, m, :], t1, t2, ALU.add, after=done_all)
            slot.free = [v]
            mix_ready.append(v)
        out = []
        for m in range(KD):
            bank, done = product(plan["b_out"][m], [mix[:, k, :] for k in range(KD)], mix_ready)
            v = tt(dve, r[:, m, :], r[:, m, :], bank.ap, ALU.add, after=[done])
            bank.free = [v]
            out.append(v)
        return out

    def moe(h, ready, r, r_ready):
        x = [h[:, k, :] for k in range(KD)]
        begin = [pe.last()] + r_ready
        logit = chunks(region(0, TB * 40), TB)
        comb = chunks(region(160, TB * NEXP), TB)
        combT = region(1024, T)
        v = memset(region(0, TB * 40), -3e38, begin)
        outs, done = tokens_product(plan["router"][0], x, NGRP, ready)
        for b in range(TB):
            v = tt(dve, logit[:, b, 0:NGRP], outs[b].ap[:, 0:NGRP], S("b_group"), ALU.add, after=[done])
            outs[b].free = [v]
        outs, done = tokens_product(plan["router"][1], x, NEXP)
        for b in range(TB):
            v = tt(dve, logit[:, b, 8:40], outs[b].ap[:, 0:NEXP], S("b_expert"), ALU.add, after=[done])
            outs[b].free = [v]
        bank, free = banks.take()
        pe.wait(*free)
        for b in range(TB):
            gtop, gidx = stat[:, 0:8], stat[:, 8:16].bitcast(U32)
            etop, eidx = stat[:, 16:24], stat[:, 24:32].bitcast(U32)
            gi, ei, chosen, ge, gz, e_in, m, w = (stat[:, 32:33], stat[:, 33:35], stat[:, 40:44], stat[:, 44:48],
                                                 stat[:, 48:49], stat[:, 56:64], stat[:, 49:50], stat[:, 50:52])
            gl, el = logit[:, b, 0:8], logit[:, b, 8:40]
            top_eight(gtop, gl)
            where_eight(gidx, gtop, gl)
            copy(dve, gi, gidx[:, 0:1])
            v = ts(dve, m, gtop[:, 0:1], -1.0, ALU.mult)
            a = activate(ge, gl[:, 0:NGRP], ACT.Exp, bias=m, accum=gz, after=[v])
            ts(dve, chosen, C("group", 0, NGRP), gi, ALU.is_equal)
            ts(dve, e_in, el[:, 0:EPG], chosen[:, 0:1], ALU.mult)
            for g in range(1, NGRP):
                stt(e_in, el[:, g * EPG:(g + 1) * EPG], chosen[:, g:g + 1], e_in, ALU.mult, ALU.add)
            top_eight(etop, e_in)
            where_eight(eidx, etop, e_in)
            copy(dve, ei, eidx[:, 0:2])
            for i in range(2):
                stt(ei[:, i:i + 1], gi, float(EPG), ei[:, i:i + 1], ALU.mult, ALU.add)
            v = tt(dve, m, etop[:, 1:2], etop[:, 0:1], ALU.subtract, after=[a])
            a = activate(w[:, 1:2], m, ACT.Exp, after=[v])
            ts(dve, m, w[:, 1:2], 1.0, ALU.add, after=[a])
            tt(dve, m, m, gz, ALU.mult)
            reciprocal(m, m)
            copy(dve, w[:, 0:1], m)
            tt(dve, w[:, 1:2], w[:, 1:2], m, ALU.mult)
            ts(dve, comb[:, b, :], C("expert"), ei[:, 0:1], ALU.is_equal, w[:, 0:1], ALU.mult)
            slot = region(1024 + T + 32 * b, NEXP)
            ts(dve, slot, C("expert"), ei[:, 1:2], ALU.is_equal, w[:, 1:2], ALU.mult)
            v = tt(dve, comb[:, b, :], comb[:, b, :], slot, ALU.add)
            transpose(bank.ap[0:NEXP, b * P:(b + 1) * P], comb[:, b, :], [v])
        a = copy(act, combT[0:NEXP, :], bank.ap[0:NEXP, :], [pe.last()])
        bank.free = [a]
        stored = act.dma(lambda e: e.dma_start(combine_dram, combT[0:NEXP, :]), sem("combine_stored"), 16, [a])
        hidden = Ring([region(4 * T + i * EXPERTS_AT_ONCE * 2 * T, EXPERTS_AT_ONCE * 2 * T) for i in range(2)])
        wts = Ring([region(4 * T + 16 * T + i * T, T) for i in range(4)])
        wsems = [sem(f"combine_loaded{i}") for i in range(4)]
        last = r_ready
        for e0 in range(0, NEXP, EXPERTS_AT_ONCE):
            hslot, hfree = hidden.take()
            hid = chunks(hslot.ap, 2 * EXPERTS_AT_ONCE)
            written = []
            for i in range(EXPERTS_AT_ONCE):
                e_ = e0 + i
                wt, free = wts.take()
                loaded = sp.dma(lambda e, e_=e_, wt=wt: e.dma_start(wt.ap, combine_dram[e_:e_ + 1, :].to_broadcast([P, T])),
                                wsems[e_ % 4], 16 * (e_ // 4 + 1), free + [stored])
                for m in range(2):
                    gate, g_done = product(plan[f"moe{e0}_up"][4 * i + 2 * m], x)
                    up, u_done = product(plan[f"moe{e0}_up"][4 * i + 2 * m + 1], x)
                    c = 2 * i + m
                    a = activate(hid[:, c, :], gate.ap, ACT.Silu, after=[g_done] + hfree)
                    gate.free = [a]
                    v = tt(dve, hid[:, c, :], hid[:, c, :], up.ap, ALU.mult, after=[a, u_done])
                    up.free = [v]
                    v = tt(pool, hid[:, c, :], hid[:, c, :], wt.ap, ALU.mult, after=[v, loaded])
                    written.append(v)
                wt.free = [v]
            out = []
            for m in range(KD):
                bank, done = product(plan[f"moe{e0}_down"][m], [hid[:, k, :] for k in range(2 * EXPERTS_AT_ONCE)], written)
                v = tt(dve, r[:, m, :], r[:, m, :], bank.ap, ALU.add, after=[done])
                bank.free = [v]
                out.append(v)
            hslot.free = [pe.last()]
        return out

    aside = [s5_factors, s5_c]
    for i in range(0, PAIRS, 2):
        aside.append(lambda i=i: (s5_b(i), s5_b(i + 1)))
    for q in range(PAIRS):
        aside.append(lambda q=q: s5_turn(q))
    r_ready = ffn("ffn0", buf_a, [x_loaded], buf_b, aside)
    h_ready = layer_norm(buf_b, r_ready, buf_a, 0, 0)
    r_ready = mixer_ab(buf_a, h_ready, buf_b)
    h_ready = layer_norm(buf_b, r_ready, buf_a, KD, KD)
    r_ready = ffn("ffn1", buf_a, h_ready, buf_b)
    h_ready = layer_norm(buf_b, r_ready, buf_a, 2 * KD, 2 * KD)
    r_ready = ple(0, buf_a, h_ready, buf_b)
    r_ready = ffn("ffn2", buf_b, r_ready, buf_a)
    h_ready = layer_norm(buf_a, r_ready, buf_b, 3 * KD, 3 * KD)
    r_ready = mixer_c(buf_b, h_ready, buf_a)
    h_ready = layer_norm(buf_a, r_ready, buf_b, 4 * KD, 4 * KD)
    r_ready = ffn("ffn3", buf_b, h_ready, buf_a)
    h_ready = layer_norm(buf_a, r_ready, buf_b, 5 * KD, 5 * KD)
    r_ready = ple(1, buf_b, h_ready, buf_a)
    h_ready = rms_norm(buf_a, r_ready, buf_b, "mix_g")
    r_ready = nsa(buf_b, h_ready, buf_a, r_ready)
    h_ready = rms_norm(buf_a, r_ready, buf_b, "ffn_g")
    r_ready = moe(buf_b, h_ready, buf_a, r_ready)
    h_ready = rms_norm(buf_a, r_ready, buf_b, "final_g")
    assert stream["next"] == len(places)
    stored = load(act, "out_stored", io["out"].rearrange("(c p) t -> p c t", p=P), buf_b, h_ready)
    act.wait(stored)

    block = ctx.enter_context(nc.Block())

    @block.tensor
    def _(e):
        pe.issue(e)

    @block.vector
    def _(e):
        dve.issue(e)

    @block.scalar
    def _(e):
        act.issue(e)

    @block.gpsimd
    def _(e):
        pool.issue(e)

    @block.sync
    def _(e):
        sp.issue(e)


def pack_weights(inputs):
    plan = weight_plan()
    places, n_blocks = place_pieces(plan)
    out = np.zeros((n_blocks, P, BLOCK), np.float32)
    i = 0
    for products in plan.values():
        for product in products:
            for name, index, rows, cols in product:
                w = inputs[name][index]
                b, c = places[i]
                i += 1
                r = 0
                for r0, nr in rows:
                    at = c
                    for c0, nc_ in cols:
                        out[b, r:r + nr, at:at + nc_] = w[r0:r0 + nr, c0:c0 + nc_]
                        at += nc_
                    r += nr
    return out


def by_chunk(a):
    a = np.asarray(a)
    return a.reshape(-1, P).T


def pack_small(inp):
    at, n = small_layout()
    out = np.zeros((P, n), np.float32)

    def put(name, value):
        out[:, at[name][0]:at[name][1]] = value

    put("ln_g", by_chunk(inp["ln_g"]))
    put("ln_b", by_chunk(inp["ln_b"]))
    put("conv_w", by_chunk(inp["conv_w"][0]))
    put("s5_d", by_chunk(inp["s5_d"][0]))
    put("b_glu", by_chunk(inp["s5_b_glu"][0]))
    put("log_dt", np.repeat(inp["s5_log_dt"][0].reshape(PAIRS, 2, 1), STATES, axis=2).reshape(PAIRS, P).T)
    put("lam_re", inp["s5_lam_re"][0].reshape(PAIRS, P).T)
    put("lam_im", inp["s5_lam_im"][0].reshape(PAIRS, P).T)
    put("mix_g", by_chunk(inp["norm_mix_g_2"][0]))
    put("ffn_g", by_chunk(inp["norm_ffn_g_2"][0]))
    put("final_g", by_chunk(inp["norm_final_g_2"]))
    put("pos_k", np.tile(inp["cmp_pos_k_2"][0].T, (2, 1)))
    put("pos_v", np.tile(inp["cmp_pos_v_2"][0].T, (2, 1)))
    put("sinks", np.broadcast_to(inp["sinks_2"][0], (P, BH)))
    put("b_group", np.broadcast_to(inp["b_group_2"][0], (P, NGRP)))
    put("b_expert", np.broadcast_to(inp["b_expert_2"][0], (P, NEXP)))
    return out


def spread_groups(a):
    out = np.zeros((PAIRS, P, P), np.float32)
    for g in range(GROUPS):
        q, half = g // 2, g % 2
        c = GCH * (g % (P // GCH))
        out[q, half * STATES:(half + 1) * STATES, c:c + GCH] = a[g]
    return out


def kernel(**inputs):
    import concourse.bacc as bacc
    from concourse.bass_utils import run_bass_kernel_spmd

    inp = {k: np.asarray(v) for k, v in inputs.items()}
    arrays = {
        "x": np.ascontiguousarray(inp["x"][0].T),
        "p": np.ascontiguousarray(inp["p"][:, 0].transpose(0, 2, 1)),
        "positions": np.ascontiguousarray(np.broadcast_to(inp["positions"][0].astype(np.int32), (P, T))),
        "weights": pack_weights(inp),
        "small": pack_small(inp),
        "const": constants(),
        "b": np.ascontiguousarray(np.concatenate([spread_groups(inp["s5_b_re"][0]), spread_groups(inp["s5_b_im"][0])], 2)),
        "c_re": np.ascontiguousarray(spread_groups(inp["s5_c_re"][0].transpose(0, 2, 1)).transpose(1, 0, 2)),
        "c_im": np.ascontiguousarray(spread_groups(inp["s5_c_im"][0].transpose(0, 2, 1)).transpose(1, 0, 2)),
    }
    nc = bacc.Bacc("TRN2", target_bir_lowering=False, num_devices=1)
    io = {n: nc.dram_tensor("in_" + n, a.shape, mybir.dt.from_np(a.dtype), kind="ExternalInput").ap()
          for n, a in arrays.items()}
    io["out"] = nc.dram_tensor("out", [D, T], F32, kind="ExternalOutput").ap()
    build(nc, io)
    got = run_bass_kernel_spmd(nc, [{"in_" + n: a for n, a in arrays.items()}], core_ids=[0])
    return np.ascontiguousarray(got.results[0]["out"].T)[None]
```

```python
from contextlib import ExitStack

import numpy as np

import concourse.bass as bass
from concourse import mybir

F32 = mybir.dt.float32
I32 = mybir.dt.int32
U32 = mybir.dt.uint32
ALU = mybir.AluOpType
ACT = mybir.ActivationFunctionType
AX = mybir.AxisListType

P = 128
T = 512
TB = T // P
D = 1024
KD = D // P
DEPTH = 2
FF = 2816
KF = FF // P
PLE = 256
CC = 512
KC = CC // P
GROUPS, GCH, STATES = 32, 16, 64
PAIRS = GROUPS // 2
PCH = 2 * GCH
PPC = P // PCH
STEPS = 4
NB = T // STEPS
HEADS, HD, KVH = 8, 128, 2
IH, ID = 8, 64
TOPK = 128
AQ, AK, AV, AI, AKI, AW = np.cumsum([0, 1024, 256, 256, 512, 64]).tolist()
THETA = 500000.0
LN_EPS, RMS_EPS = 1e-5, 1e-6
ALPHA = float((2 * DEPTH) ** 0.25)
BH, BD = 8, 64
CL, CS, CHID = 32, 16, 256
NCMP = T // CS - CL // CS + 1
(BQA, BKC, BVC, BKS, BVS, BKW, BVW, BG, BQB, BKB, BVB, BM) = np.cumsum(
    [0, 512, 128, 128, 128, 128, 128, 128, 24, 512, 128, 128]).tolist()
NGRP, EPG, NEXP, EFF = 4, 8, 32, 256
SLOTS = 64
NEG = -1e30
CAUSAL_FILL = -1e30
TAKEN = -3e38
SLOPES = 2.0 ** (-8.0 * np.arange(1, 17) / 16)
SLOPES = np.asarray(SLOPES, np.float32)
PI = float(np.pi)
ROUND = 12582912.0
ROUND13 = 1536.0
TWO_PI_1 = 6.28125
TWO_PI_2 = 0.0019350051879882812
TWO_PI_3 = float(2 * np.pi - TWO_PI_1 - TWO_PI_2)

BLOCK = 16 * P
RING = 6


def dense(name, index, n_rows, col0, n_cols, width=P):
    return [[(name, index, ((k * P, P),), ((col0 + m * width, min(width, n_cols - m * width)),))
             for k in range(n_rows // P)] for m in range(-(-n_cols // width))]


def columns(name, index, n_rows, *segments):
    return [(name, index, ((k * P, P),), tuple(segments)) for k in range(n_rows // P)]


def ffn_pieces(layer, i):
    up = []
    for g, u in zip(dense("ffn_w1", (layer, i), D, 0, FF), dense("ffn_w3", (layer, i), D, 0, FF)):
        up += [g, u]
    return up, dense("ffn_w2", (layer, i), FF, 0, D)


def pair_rows(name, index, first):
    return [[(name, index, ((j * BD, BD), ((4 + j) * BD, BD)), ((m * P, P),)) for j in range(4)]
            for m in range(D // P)]


def head_columns(base, j):
    return ((base + j * BD, BD), (base + (4 + j) * BD, BD))


def weight_plan():
    plan = {}
    plan["ffn0_up"], plan["ffn0_down"] = ffn_pieces(0, 0)
    plan["ab_in"] = dense("ab_w_in", (0,), D, 0, 4 * CC)
    plan["glu"] = dense("s5_w_glu", (0,), CC, 0, CC)
    plan["ab_out"] = dense("ab_w_out", (0,), 2 * CC, 0, D)
    plan["ffn1_up"], plan["ffn1_down"] = ffn_pieces(0, 1)
    plan["ple0_proj"] = dense("ple_w_proj", (0,), PLE, 0, D)
    plan["ple0_gate"] = dense("ple_w_gate", (0,), D, 0, D)
    plan["ffn2_up"], plan["ffn2_down"] = ffn_pieces(1, 0)
    plan["c_index"] = (dense("c_w_in", (0,), D, AI, IH * ID) +
                       [columns("c_w_in", (0,), D, (AKI, ID), (AKI, ID))])
    plan["c_weight"] = [columns("c_w_in", (0,), D, (AW, IH))]
    plan["c_value"] = [columns("c_w_in", (0,), D, (AV, 256))]
    plan["c_qk"] = dense("c_w_in", (0,), D, AQ, HEADS * HD) + dense("c_w_in", (0,), D, AK, KVH * HD)
    plan["c_out"] = dense("c_w_out", (0,), D, 0, D)
    plan["ffn3_up"], plan["ffn3_down"] = ffn_pieces(1, 1)
    plan["ple1_proj"] = dense("ple_w_proj", (1,), PLE, 0, D)
    plan["ple1_gate"] = dense("ple_w_gate", (1,), D, 0, D)
    w = ("w_in_2", (0,), D)
    plan["b_compress_in"] = [columns(*w, (BKC, P)), columns(*w, (BVC, P))]
    plan["b_compress"] = [[(f"cmp_w1_{c}_2", (0,), ((l * BD, BD), (l * BD, BD)), ((m * P, P),))
                           for l in range(CL)] for c in "kv" for m in range(CHID // P)]
    plan["b_compress_k"] = [[("cmp_w2_k_2", (0,), ((k * P, P),), ((0, BD), (0, BD))) for k in range(CHID // P)]]
    plan["b_compress_v"] = [[("cmp_w2_v_2", (0,), ((k * P, P),), ((0, BD),)) for k in range(CHID // P)]]
    plan["b_value"] = [columns(*w, (BVS, P), (BVW, P), (BVB, P))]
    plan["b_gate"] = [columns(*w, (BG, 24))]
    plan["b_key"] = [columns(*w, (b, P)) for b in (BKS, BKW, BKB)]
    plan["b_query"] = [columns(*w, *head_columns(b, j)) for b in (BQA, BQB) for j in range(4)]
    plan["b_merge"] = []
    for m in range(KD):
        plan["b_merge"] += [columns(*w, (BM + m * P, P)), columns(*w, (BM + D + m * P, P)),
                            pair_rows("w_a_2", (0,), 0)[m], pair_rows("w_b_2", (0,), 0)[m]]
    plan["b_out"] = dense("w_o_2", (0,), D, 0, D)
    plan["router"] = [columns("w_group_2", (0,), D, (0, NGRP)), columns("w_expert_2", (0,), D, (0, NEXP))]
    for e in range(NEXP):
        up = []
        for g, u in zip(dense("w_gate_e_2", (0, e), D, 0, EFF), dense("w_up_e_2", (0, e), D, 0, EFF)):
            up += [g, u]
        plan[f"moe{e}_up"] = up
        plan[f"moe{e}_down"] = [[("w_down_e_2", (0, e), ((k * P, P),), ((n * T, T),))
                                 for k in range(EFF // P) for n in range(D // T)]]
    return plan


def width_of(piece):
    return sum(n for _, n in piece[3])


LEAD = {"ffn1_up": 4, "ffn2_up": 4, "ffn3_up": 4, "ab_in": 4, "c_index": 5, "ple0_gate": 4, "ple1_gate": 4,
        "b_compress_in": 2}


def in_order(plan):
    for name, products in plan.items():
        n = LEAD.get(name, 0)
        for pieces in zip(*products[:n]):
            for piece in pieces:
                yield name, piece
        for product in products[n:]:
            for piece in product:
                yield name, piece


def place_pieces(plan):
    places, block, col, last = [], 0, 0, None
    for name, piece in in_order(plan):
        if name != last and name.startswith("moe") and col:
            block, col = block + 1, 0
        last = name
        n = width_of(piece)
        if col + n > BLOCK:
            block, col = block + 1, 0
        places.append((block, col))
        col += n
    return places, block + 1


def small_layout():
    at, n = {}, 0
    for name, width in (("ln_g", DEPTH * 3 * KD), ("ln_b", DEPTH * 3 * KD), ("conv_w", 3 * KC), ("s5_d", KC),
                        ("b_glu", KC), ("log_dt", PAIRS), ("lam_re", PAIRS), ("lam_im", PAIRS),
                        ("mix_g", KD), ("ffn_g", KD), ("pos_k", CL), ("pos_v", CL),
                        ("sinks", BH), ("b_group", NGRP), ("b_expert", NEXP)):
        at[name] = (n, n + width)
        n += width
    return at, n


def const_layout():
    at, n = {}, 0
    for name, width in (("ident", P), ("mean", P), ("far_causal", T), ("far_256", T), ("far_128", T),
                        ("steps", T), ("swap_a", P), ("swap_i", P), ("inv_a", 1), ("inv_i", 1),
                        ("sgn_a", 1), ("sgn_i", 1), ("far_cmp", TB * (NCMP + 1)), ("see_cmp", TB * (NCMP + 1)),
                        ("expert", NEXP), ("group", EPG), ("before", P), ("ones", P)):
        at[name] = (n, n + width)
        n += width
    return at, n


def constants():
    at, n = const_layout()
    c = np.zeros((P, n), np.float32)

    def put(name, value):
        c[:, at[name][0]:at[name][1]] = value

    p = np.arange(P)[:, None]
    put("ident", np.eye(P))
    put("mean", np.full((P, P), 1.0 / D))
    back = (np.arange(T)[None, :] - (T - P)) - p
    for name, window in (("far_causal", T), ("far_256", 256), ("far_128", 128)):
        put(name, np.where((back <= 0) & (back > -window), back, NEG))
    put("steps", np.arange(T)[None, :])
    for name, rot, period, inv in (("a", HD // 4, HD, "inv_a"), ("i", ID // 4, ID, "inv_i")):
        half = rot // 2
        swap, freq, sign = np.zeros((P, P)), np.zeros((P, 1), np.float32), np.ones((P, 1))
        table = np.float32(THETA) ** (-np.arange(0, rot, 2, dtype=np.float32) / np.float32(rot))
        for base in range(0, P, period):
            for j in range(half):
                swap[base + j + half, base + j] = swap[base + j, base + j + half] = 1
                freq[base + j] = freq[base + j + half] = table[j]
                sign[base + j] = -1
        put(f"swap_{name}", swap)
        put(inv, freq)
        put(f"sgn_{name}", 2 * sign)
    end = np.arange(NCMP) * CS + CL - 1
    far = np.full((P, TB, NCMP + 1), NEG, np.float32)
    see = np.zeros((P, TB, NCMP + 1), np.float32)
    for b in range(TB):
        back = end[None, :] - (b * P + p)
        far[:, b, :NCMP] = np.where(back <= 0, back, NEG)
        see[:, b, :NCMP] = back <= 0
    put("far_cmp", far.reshape(P, -1))
    put("see_cmp", see.reshape(P, -1))
    put("expert", np.arange(NEXP)[None, :])
    put("group", np.arange(EPG)[None, :])
    put("before", p < np.arange(P)[None, :])
    put("ones", 1.0)
    return c


class Queue:

    def __init__(self, done, chained):
        self.done, self.chained, self.count, self.items, self.seen = done, chained, 0, [], {}
        self.flag, self.branches = None, []

    def branch(self, flag, state=None):
        if state is None:
            self.common, self.flag = self.items, flag
            state = (self.count, dict(self.seen))
        self.count, self.seen = state[0], dict(state[1])
        self.items = []
        self.branches.append(self.items)
        return state

    def wait(self, *after):
        for sem, value in after:
            if self.seen.get(id(sem), 0) < value:
                self.seen[id(sem)] = value
                self.items.append(["wait", sem, value])

    def last(self):
        if self.items and self.items[-1][0] == "quiet":
            self.items[-1][0] = "signal"
            self.count += 1
        return (self.done, self.count)

    def do(self, instruction, after=(), free=False):
        if self.chained and not free and self.count:
            self.wait((self.done, self.count))
        self.wait(*after)
        self.count += 1
        self.items.append(["signal", instruction, None])
        return (self.done, self.count)

    def quiet(self, instruction, after=()):
        self.wait(*after)
        self.items.append(["quiet", instruction, None])

    def dma(self, instruction, sem, value, after=()):
        self.wait(*after)
        self.items.append(["dma", instruction, sem])
        return (sem, value)

    def issue(self, engine):
        self.issue_items(engine, self.common)
        flag = engine.value_load(self.flag, min_val=0, max_val=1)
        with engine.If(flag != 0):
            self.issue_items(engine, self.branches[0])
        with engine.Else():
            self.issue_items(engine, self.branches[1])

    def issue_items(self, engine, items):
        for kind, what, arg in items:
            if kind == "wait":
                engine.wait_ge(what, arg)
            elif kind == "signal":
                what(engine).then_inc(self.done, 1)
            elif kind == "quiet":
                what(engine)
            else:
                what(engine).then_inc(arg, 16)


class Slot:

    def __init__(self, ap):
        self.ap, self.free = ap, []


class Ring:
    def __init__(self, aps):
        self.slots, self.n = [Slot(a) for a in aps], 0

    def take(self):
        for _ in self.slots:
            self.n += 1
            slot = self.slots[(self.n - 1) % len(self.slots)]
            if slot.free is not None:
                free, slot.free = slot.free, None
                return slot, free
        raise AssertionError("every slot is held")


def build(nc, io):
    ctx = ExitStack()
    with ctx:
        build_in(nc, io, ctx)


def build_in(nc, io, ctx):
    def sbuf(name, n, dt=F32):
        return ctx.enter_context(nc.sbuf_tensor(name, [P, n], dt))

    def sem(name):
        return ctx.enter_context(nc.semaphore(name))

    def chunks(ap, c):
        return ap.rearrange("p (c n) -> p c n", c=c)

    const_at, n_const = const_layout()
    small_at, n_small = small_layout()
    const = sbuf("const", n_const)
    small = sbuf("small", n_small)
    ring = sbuf("ring", RING * BLOCK)
    buf_a = chunks(sbuf("buf_a", KD * T)[:, :], KD)
    buf_b = chunks(sbuf("buf_b", KD * T)[:, :], KD)
    norm = sbuf("norm", 4 * T)
    stat = sbuf("stat", 512)
    area = sbuf("area", 24576)
    banks = Ring([ctx.enter_context(nc.psum_tensor(f"bank{i}", [P, T], F32))[:, :] for i in range(8)])
    tables_dram = nc.dram_tensor("turn_tables", [PPC, P, 2 * T], F32, kind="Internal").ap()
    combine_dram = nc.dram_tensor("combine", [NEXP, T], F32, kind="Internal").ap()
    slots_in = nc.dram_tensor("slots_in", [NEXP * SLOTS, D], F32, kind="Internal").ap()
    slots_out = nc.dram_tensor("slots_out", [NEXP * SLOTS, D], F32, kind="Internal").ap()

    def C(name, a=0, b=None):
        lo, hi = const_at[name]
        return const[:, lo + a:hi if b is None else lo + b]

    def S(name, a=0, b=None):
        lo, hi = small_at[name]
        return small[:, lo + a:hi if b is None else lo + b]

    def region(lo, n):
        return area[:, lo:lo + n]

    pe = Queue(sem("tensor_done"), False)
    dve = Queue(sem("vector_done"), True)
    act = Queue(sem("scalar_done"), True)
    pool = Queue(sem("pool_done"), True)
    sp = Queue(sem("sync_done"), False)
    block_loaded = [sem(f"block_loaded{i}") for i in range(RING)]

    def tt(q, out, a, b, op, after=(), free=False):
        return q.do(lambda e: e.tensor_tensor(out, a, b, op), after, free)

    def ts(q, out, a, s1, op0, s2=None, op1=None, after=(), free=False):
        if op1 is None:
            return q.do(lambda e: e.tensor_scalar(out, a, s1, None, op0), after, free)
        return q.do(lambda e: e.tensor_scalar(out, a, s1, s2, op0, op1), after, free)

    def stt(out, a, s, b, op0, op1, after=(), free=False):
        return dve.do(lambda e: e.scalar_tensor_tensor(out, a, s, b, op0, op1), after, free)

    def activate(out, a, func, scale=1.0, bias=0.0, accum=None, after=(), free=False):
        return act.do(lambda e: e.activation(out, a, func, bias=bias, scale=scale, accum_out=accum), after, free)

    def copy(q, out, a, after=(), free=False):
        if q is act:
            return activate(out, a, ACT.Copy, after=after, free=free)
        return q.do(lambda e: e.tensor_copy(out, a), after, free)

    def reciprocal(out, a, after=()):
        return dve.do(lambda e: e.reciprocal(out, a), after)

    def reduce(out, a, op, after=()):
        return dve.do(lambda e: e.tensor_reduce(out, a, AX.X, op), after)

    def scan(out, rate, a, after=(), free=False):
        return dve.do(lambda e: e.tensor_tensor_scan(out, rate, a, 0.0, ALU.mult, ALU.add), after, free)

    def memset(ap, value, after=()):
        return dve.do(lambda e: e.memset(ap, value), after)

    def top_eight(out, a):
        return dve.do(lambda e: e.max(out, a))

    def replace_eight(a, values, by):
        return dve.do(lambda e: e.match_replace(a, values, a, by))

    def where_eight(out, values, a):
        return dve.do(lambda e: e.max_index(out, values, a))

    def load(q, name, out, src, after=()):
        return q.dma(lambda e: e.dma_start(out, src), sem(name), 16, after)

    plan = weight_plan()
    places, n_blocks = place_pieces(plan)
    stream = {"next": 0, "block": -1}

    def load_block(b, after=()):
        slot = b % RING
        sp.dma(lambda e: e.dma_start(ring[:, slot * BLOCK:(slot + 1) * BLOCK], io["weights"][b]),
               block_loaded[slot], 0, after)

    def take(piece):
        block, col = places[stream["next"]]
        stream["next"] += 1
        if block != stream["block"]:
            if stream["block"] >= 0 and stream["block"] + RING < n_blocks:
                load_block(stream["block"] + RING, [pe.last()])
            stream["block"] = block
            pe.wait((block_loaded[block % RING], 16 * (block // RING + 1)))
        at = (block % RING) * BLOCK + col
        return ring[:, at:at + width_of(piece)]

    def matmul(out, lhsT, rhs, start, stop, after=()):
        pe.quiet(lambda e: e.matmul(out, lhsT, rhs, start=start, stop=stop), after)

    def accumulate(out, lhsT, rhs):
        pe.quiet(lambda e: e.matmul(out, lhsT, rhs, start=False, stop=True, skip_group_check=True))

    def transpose(out, in_, after=()):
        n = in_.shape[0]
        pe.quiet(lambda e: e.transpose(out, in_, C("ident")[0:n, 0:n]), after)

    def product(pieces, x, after=(), bank=None, start=True, stop=True, n=T):
        if bank is None:
            bank, free = banks.take()
            pe.wait(*free)
        pe.wait(*after)
        for k, piece in enumerate(pieces):
            w = take(piece)
            matmul(bank.ap[0:w.shape[1], 0:n], w, x[k], start and k == 0, stop and k == len(pieces) - 1)
        return bank, pe.last()

    def lead(name, x, ready):
        group = plan[name][:LEAD[name]]
        out = []
        for _ in group:
            bank, free = banks.take()
            pe.wait(*free)
            out.append(bank)
        for k in range(len(x)):
            for bank, pieces in zip(out, group):
                matmul(bank.ap[0:width_of(pieces[k]), :], take(pieces[k]), x[k], k == 0, k == len(x) - 1, [ready[k]])
        done = pe.last()
        return [(bank, done) for bank in out]

    def tokens_product(pieces, x, width, after=()):
        out = []
        for _ in range(TB):
            bank, free = banks.take()
            pe.wait(*free)
            out.append(bank)
        pe.wait(*after)
        for k, piece in enumerate(pieces):
            w = take(piece)
            for b in range(TB):
                matmul(out[b].ap[:, 0:width], x[k][:, b * P:(b + 1) * P], w, k == 0, k == len(pieces) - 1)
        return out, pe.last()

    for b in range(RING):
        load_block(b)
    x_loaded = load(act, "x_loaded", buf_a, io["x"].rearrange("(c p) t -> p c t", p=P))
    const_loaded = load(act, "const_loaded", const[:, :], io["const"])
    small_loaded = load(act, "small_loaded", small[:, :], io["small"])

    sums, square_sums = norm[:, 0:T], norm[:, T:2 * T]
    squares = Ring([norm[:, (2 + i) * T:(3 + i) * T] for i in range(2)])
    one_over_d = C("mean")
    summed = {}

    def add_to_sums(r, m, ready, plain=True):
        if m == 0:
            before = summed.get("read", [])
            activate(square_sums, r[:, 0, :], ACT.Square, after=[ready] + before)
            pool.wait(*before)
            summed["first"] = [ready]
            return
        slot, free = squares.take()
        a = activate(slot.ap, r[:, m, :], ACT.Square, after=[ready] + free)
        if plain:
            tt(pool, sums, r[:, 0, :] if m == 1 else sums, r[:, m, :], ALU.add, after=[ready] + summed["first"])
        g = tt(pool, square_sums, square_sums, slot.ap, ALU.add, after=[a], free=plain)
        slot.free = [g]
        summed["last"] = g

    def total(x):
        bank, free = banks.take()
        matmul(bank.ap, one_over_d, x, True, True, free + [summed["last"], const_loaded])
        return bank, pe.last()

    def layer_norm(src, ready, dst, g, b):
        mean, m_done = total(sums)
        square, s_done = total(square_sums)
        shift, scale = sums, square_sums
        v = copy(dve, shift, mean.ap, [m_done, s_done])
        mean.free = [v]
        tt(dve, scale, shift, shift, ALU.mult)
        v = stt(scale, scale, -1.0, square.ap, ALU.mult, ALU.add)
        square.free = [v]
        v = ts(dve, scale, scale, 0.0, ALU.max, LN_EPS, ALU.add)
        a = activate(scale, scale, ACT.Sqrt, after=[v])
        v = reciprocal(scale, scale, [a])
        c = tt(dve, shift, shift, scale, ALU.mult)
        out, reads = [], []
        for k in range(KD):
            q = pool if k in (2, 5) else dve
            tt(q, src[:, k, :], src[:, k, :], scale, ALU.mult, after=[v, c, ready[k]], free=q is dve and k > 0)
            n = tt(q, src[:, k, :], src[:, k, :], shift, ALU.subtract)
            reads.append(n)
            out.append(n)
        for k in (0, 1, 3, 4, 2, 6, 7, 5):
            out[k] = activate(dst[:, k, :], src[:, k, :], ACT.Identity, scale=S("ln_g", g + k, g + k + 1),
                              bias=S("ln_b", b + k, b + k + 1), after=[out[k], small_loaded], free=True)
        summed["read"] = reads
        return out

    def rms_norm(src, ready, dst, g):
        square, done = total(square_sums)
        scale = square_sums
        v = ts(dve, scale, square.ap, RMS_EPS, ALU.add, after=[done])
        square.free = [v]
        a = activate(scale, scale, ACT.Sqrt, after=[v])
        r = reciprocal(scale, scale, [a])
        out = [stt(dst[:, k, :], src[:, k, :], S(g, k, k + 1), scale, ALU.mult, ALU.mult,
                   after=[r, small_loaded, ready[k]], free=k > 0) for k in range(KD)]
        summed["read"] = out
        return out

    def ffn(name, h, ready, r, aside=()):
        aside = list(aside)
        hidden = chunks(region(0, KF * T), KF)
        x = [h[:, k, :] for k in range(KD)]
        written = []
        begun = lead(name + "_up", x, ready) if name + "_up" in LEAD else []
        for m in range(KF):
            gate, g_done = begun.pop(0) if begun else product(plan[name + "_up"][2 * m], x, ready)
            up, u_done = begun.pop(0) if begun else product(plan[name + "_up"][2 * m + 1], x)
            a = activate(hidden[:, m, :], gate.ap, ACT.Silu, after=[g_done])
            gate.free = [a]
            v = tt(dve, hidden[:, m, :], hidden[:, m, :], up.ap, ALU.mult, after=[a, u_done])
            up.free = [v]
            written.append(v)
            if aside:
                aside.pop(0)()
        out = []
        for m in range(KD):
            bank, done = product(plan[name + "_down"][m], [hidden[:, k, :] for k in range(KF)], written)
            a = activate(r[:, m, :], bank.ap, ACT.Copy, scale=0.5, after=[done])
            bank.free = [a]
            out.append(stt(r[:, m, :], h[:, m, :], ALPHA, r[:, m, :], ALU.mult, ALU.add, after=[a] + ready))
            add_to_sums(r, m, out[-1])
            if aside:
                aside.pop(0)()
        assert not aside
        return out

    def ple_proj(layer):
        begin = [pe.last()]
        pt, proj = chunks(region(0, 2 * T), 2), chunks(region(2 * T, KD * T), KD)
        p_loaded = load(act, f"p_loaded{layer}", pt, io["p"][layer].rearrange("(c p) t -> p c t", p=P), begin)
        out = []
        for m in range(KD):
            bank, done = product(plan[f"ple{layer}_proj"][m], [pt[:, k, :] for k in range(2)], [p_loaded])
            out.append(copy(act, proj[:, m, :], bank.ap, [done]))
            bank.free = [out[-1]]
        return proj, out

    def ple(layer, h, ready, r, proj, proj_ready, squares_too):
        gates = Ring([region((10 + i) * T, T) for i in range(2)])
        x = [h[:, k, :] for k in range(KD)]
        out, begun = [], lead(f"ple{layer}_gate", x, ready)
        for m in range(KD):
            gate, g_done = begun.pop(0) if begun else product(plan[f"ple{layer}_gate"][m], x)
            s, free = gates.take()
            a = activate(s.ap, gate.ap, ACT.Sigmoid, after=free + [g_done])
            gate.free = [a]
            tt(dve, s.ap, s.ap, proj[:, m, :], ALU.mult, after=[a, proj_ready[m]])
            v = tt(dve, r[:, m, :], s.ap, h[:, m, :], ALU.add, after=[ready[m]])
            s.free = [v]
            out.append(v)
            if squares_too:
                add_to_sums(r, m, v, plain=False)
        return out

    def reduce_angle(r, k, x):
        ts(dve, k, x, 1.0 / (2 * PI), ALU.mult, ROUND, ALU.add)
        ts(dve, k, k, -ROUND, ALU.add)
        stt(r, k, -TWO_PI_1, x, ALU.mult, ALU.add)
        stt(r, k, -TWO_PI_2, r, ALU.mult, ALU.add)
        return stt(r, k, -TWO_PI_3, r, ALU.mult, ALU.add)

    def sin_cos(sin, cos, r, half, double, after=()):
        a = activate(sin, r, ACT.Sin, scale=half, after=after)
        v = stt(cos, r, -1.0, r, ALU.mult, ALU.max, after=after)
        v = ts(dve, cos, cos, -half, ALU.mult, PI / 2, ALU.add)
        c = activate(r, cos, ACT.Sin, after=[v, a])
        v = tt(dve, cos, sin, sin, ALU.mult, after=[c])
        v = ts(dve, cos, cos, -2.0, ALU.mult, 1.0, ALU.add)
        return stt(sin, sin, double, r, ALU.mult, ALU.mult, after=[c])

    BASE = KF * T
    b_turned = region(BASE, STEPS * 2 * T).rearrange("p (k r c s) -> p k r c s", k=STEPS, r=2, c=KC)
    c_power = region(BASE + 8 * T, STEPS * 2 * T).rearrange("p (k r q c) -> p k r q c", k=STEPS, r=2, q=PAIRS)
    short = region(BASE + 16 * T, STEPS * T).rearrange("p (n c o) -> p n c o", n=STEPS, c=KC)
    top = BASE + 20 * T
    b_re, b_im, c_re, nc_im, fb_re, fb_im = (region(top + i * T, T).rearrange("p (q c) -> p q c", q=PAIRS) for i in range(6))
    st = [stat[:, i * PAIRS:(i + 1) * PAIRS] for i in range(32)]
    mag, f_re, f_im, turn_hi, turn_lo, t_small = st[0:6]
    power = [(st[14 + 2 * k], st[15 + 2 * k]) for k in range(STEPS + 1)]
    factor = [(st[24 + 2 * k], st[25 + 2 * k]) for k in range(STEPS)]
    s5 = {}

    def multiply(out, x, y, tmp):
        tt(dve, out[0], x[0], y[0], ALU.mult)
        tt(dve, tmp, x[1], y[1], ALU.mult)
        tt(dve, out[0], out[0], tmp, ALU.subtract)
        tt(dve, out[1], x[0], y[1], ALU.mult)
        tt(dve, tmp, x[1], y[0], ALU.mult)
        return tt(dve, out[1], out[1], tmp, ALU.add)

    def s5_factors():
        dt, lr, x, r, k, sn, cs, den = st[6:14]
        t = t_small
        w = [const_loaded, small_loaded]
        a = activate(dt, S("log_dt"), ACT.Exp, after=w)
        ts(dve, lr, S("lam_re"), -1e-4, ALU.min, after=w)
        tt(dve, x, S("lam_im"), dt, ALU.mult, after=[a])
        tt(dve, mag, lr, dt, ALU.mult)
        v = reduce_angle(r, k, x)
        a = activate(mag, mag, ACT.Exp, after=[v])
        ts(dve, turn_hi, r, 1.0 / (2 * PI), ALU.mult)
        ts(dve, turn_lo, turn_hi, ROUND13, ALU.add)
        ts(dve, k, turn_lo, -ROUND13, ALU.add)
        tt(dve, turn_lo, turn_hi, k, ALU.subtract)
        v = copy(dve, turn_hi, k)
        sin_cos(sn, cs, r, 0.5, 2.0, [v])
        tt(dve, power[1][0], cs, mag, ALU.mult, after=[a])
        tt(dve, power[1][1], sn, mag, ALU.mult)
        tt(dve, t, mag, mag, ALU.mult)
        tt(dve, mag, t, t, ALU.mult)
        for n in range(2, STEPS + 1):
            multiply(power[n], power[n - 1], power[1], t)
        ts(dve, cs, power[1][0], -1.0, ALU.add)
        tt(dve, den, lr, lr, ALU.mult)
        tt(dve, t, S("lam_im"), S("lam_im"), ALU.mult)
        tt(dve, den, den, t, ALU.add)
        reciprocal(den, den)
        tt(dve, f_re, cs, lr, ALU.mult)
        tt(dve, t, power[1][1], S("lam_im"), ALU.mult)
        tt(dve, f_re, f_re, t, ALU.add)
        tt(dve, f_re, f_re, den, ALU.mult)
        tt(dve, f_im, power[1][1], lr, ALU.mult)
        tt(dve, t, cs, S("lam_im"), ALU.mult)
        tt(dve, f_im, f_im, t, ALU.subtract)
        tt(dve, f_im, f_im, den, ALU.mult)
        copy(dve, factor[3][0], f_re)
        copy(dve, factor[3][1], f_im)
        for k in range(STEPS - 1):
            s5["factors"] = multiply(factor[k], power[3 - k], (f_re, f_im), t)
        s5["loaded"] = [load(act, f"s5_{n}_loaded", dst, io["s5_" + n])
                        for n, dst in (("b_re", b_re), ("b_im", b_im), ("c_re", c_re), ("c_im", nc_im))]
        s5["c"] = ts(dve, nc_im, nc_im, -1.0, ALU.mult, after=s5["loaded"])
        memset(short, 0.0)

    def over(column):
        return column.unsqueeze(2).to_broadcast([P, PAIRS, PCH])

    s5["operands"] = []

    def s5_b(k):
        gr, gi = factor[k]
        tmp = c_power[:, 3, 1]
        after = s5.get("fb_free", [])
        tt(dve, fb_re, b_re, over(gr), ALU.mult, after=s5["loaded"] + after)
        tt(dve, tmp, b_im, over(gi), ALU.mult)
        tt(dve, fb_re, fb_re, tmp, ALU.subtract)
        tt(dve, fb_im, b_im, over(gr), ALU.mult)
        tt(dve, tmp, b_re, over(gi), ALU.mult)
        s5["fb"] = tt(dve, fb_im, fb_im, tmp, ALU.add)

    def s5_turn_b(k):
        for r, src in ((0, fb_re), (1, fb_im)):
            bank, free = banks.take()
            pe.wait(*free)
            for ct in range(KC):
                transpose(bank.ap[:, ct * P:(ct + 1) * P], src[:, ct * PPC:(ct + 1) * PPC, :].rearrange("p q c -> p (q c)"),
                          [s5["fb"]])
            a = copy(act, b_turned[:, k, r].rearrange("p c s -> p (c s)"), bank.ap, [pe.last()])
            bank.free = [a]
            s5["operands"].append(a)
        bank, free = banks.take()
        pe.wait(*free)
        for ct in range(KC):
            for r, (f, c) in enumerate(((fb_re, c_re), (fb_im, nc_im))):
                pairs = slice(ct * PPC, (ct + 1) * PPC)
                matmul(bank.ap[:, ct * P:(ct + 1) * P], f[:, pairs, :].rearrange("p q c -> p (q c)"),
                       c[:, pairs, :].rearrange("p q c -> p (q c)"), r == 0, r == 1, [s5["c"]])
        done = pe.last()
        s5["fb_free"] = [done]
        for i in range(PPC):
            rows = slice(i * PCH, (i + 1) * PCH)
            a = activate(short[rows, STEPS - 1 - k, :, rows], chunks(bank.ap, KC)[rows, :, rows], ACT.Copy, after=[done, s5["fb"]])
        bank.free = [a]
        s5["operands"].append(a)

    def s5_c(k):
        ar, ai = power[k + 1]
        re, im = c_power[:, k, 0], c_power[:, k, 1]
        tmp = fb_re
        tt(dve, re, c_re, over(ar), ALU.mult, after=s5["fb_free"])
        tt(dve, im, nc_im, over(ai), ALU.mult)
        tt(dve, re, re, im, ALU.add)
        tt(dve, im, nc_im, over(ar), ALU.mult)
        tt(dve, tmp, c_re, over(ai), ALU.mult)
        s5["operands"].append(tt(dve, im, im, tmp, ALU.subtract))

    table_stored = [sem(f"table_stored{i}") for i in range(PPC)]
    s5["tables"] = []

    def s5_turn(i):
        both = region(top, 2 * T)
        cos, sin, r = region(top, T), region(top + T, T), region(top + 2 * T, T)
        steps = C("steps")[:, 0:T:STEPS]
        for ct in range(KC):
            q = ct * PPC + i
            ts(dve, chunks(r, KC)[:, ct, :], steps, turn_hi[:, q:q + 1], ALU.mult, after=s5["operands"] + s5["tables"])
        ts(dve, cos, r, ROUND, ALU.add, -ROUND, ALU.add)
        tt(dve, r, r, cos, ALU.subtract)
        for ct in range(KC):
            q = ct * PPC + i
            part = chunks(r, KC)[:, ct, :]
            v = stt(part, steps, turn_lo[:, q:q + 1], part, ALU.mult, ALU.add)
        v = sin_cos(sin, cos, r, PI, 2.0, [v])
        s5["tables"].append(act.dma(lambda e: e.dma_start(tables_dram[i], both), table_stored[i], 16, [v]))

    def mixer_ab(h, ready, r):
        hc = chunks(region(0, KC * T), KC)
        u = chunks(region(KC * T, KC * T), KC)
        y = chunks(region(2 * KC * T, KC * T), KC)
        gb = chunks(region(3 * KC * T, KC * T), KC)
        pad = region(4 * KC * T, T + 2)
        x = [h[:, k, :] for k in range(KD)]
        hc_done, gb_done = [], []
        zeroed = memset(pad[:, 0:2], 0.0, [pe.last()])
        begun = lead("ab_in", x, ready)
        for m in range(KC):
            bank, done = begun[m]
            hc_done.append(copy(act, hc[:, m, :], bank.ap, [done]))
            bank.free = [hc_done[-1]]
        for m in range(KC):
            bank, done = product(plan["ab_in"][KC + m], x)
            gb_done.append(copy(act, gb[:, m, :], bank.ap, [done]))
            bank.free = [gb_done[-1]]
        conv = []
        for m in range(KC):
            bank, done = product(plan["ab_in"][2 * KC + m], x)
            v = tt(dve, pad[:, 2:T + 2], hc[:, m, :], bank.ap, ALU.mult, after=[done, hc_done[m], zeroed])
            bank.free = [v]
            w = [S("conv_w", j * KC + m, j * KC + m + 1) for j in range(3)]
            ts(dve, hc[:, m, :], pad[:, 0:T], w[0], ALU.mult)
            stt(hc[:, m, :], pad[:, 1:T + 1], w[1], hc[:, m, :], ALU.mult, ALU.add)
            stt(hc[:, m, :], pad[:, 2:T + 2], w[2], hc[:, m, :], ALU.mult, ALU.add)
            conv.append(tt(dve, hc[:, m, :], hc[:, m, :], gb[:, m, :], ALU.mult, after=[gb_done[m]]))
        u_done = []
        for m in range(KC):
            bank, done = product(plan["ab_in"][3 * KC + m], x)
            u_done.append(copy(act, u[:, m, :], bank.ap, [done]))
            bank.free = [u_done[-1]]
        spare = 3 * KC * T
        turn = Ring([region(spare, 2 * T), region(spare + 2 * T, 2 * T)])
        turn_sems = [sem("turn_loaded0"), sem("turn_loaded1")]
        sets = Ring([region(4 * KC * T, 4 * T), region(2 * KC * T, 4 * T)])
        ends = Ring([region(top + n * 2 * KC * (NB + 1), 2 * KC * (NB + 1)).rearrange("p (r c j) -> p r c j", r=2, c=KC)
                     for n in range(2)])
        begun_at = conv + s5["tables"]
        for slot in ends.slots:
            zero = memset(slot.ap[:, :, :, 0:1], 0.0, begun_at)
        turns = []
        for i in range(2):
            tslot, free = turn.take()
            turns.append((tslot, act.dma(lambda e, i=i, tslot=tslot: e.dma_start(tslot.ap, tables_dram[i]),
                                         turn_sems[i], 16, free + begun_at)))
        inputs = []

        def to_ends(i):
            rows = slice(i * PCH, (i + 1) * PCH)
            got = []
            for part in range(2):
                bank, free = banks.take()
                pe.wait(*free)
                for ct in range(KC):
                    for k in range(STEPS):
                        matmul(bank.ap[:, ct * NB:(ct + 1) * NB], b_turned[rows, k, part, ct, :], u[rows, ct, k:T:STEPS],
                               k == 0, k == STEPS - 1, u_done + s5["operands"])
                got.append((bank, pe.last()))
            inputs.append(got)

        to_ends(0)
        to_ends(1)
        y_banks = []
        for ct in range(KC):
            bank, free = banks.take()
            pe.wait(*free)
            out, x_in = (a.rearrange("p (j k) -> p j k", k=STEPS) for a in (bank.ap, u[:, ct, :]))
            for n in range(STEPS):
                if n == 0:
                    matmul(bank.ap, short[:, n, ct, :], u[:, ct, :], True, True)
                else:
                    accumulate(out[:, :, n:STEPS], short[:, n, ct, :], x_in[:, :, 0:STEPS - n])
            y_banks.append(bank)
        for i in range(PPC):
            tslot, loaded = turns[i]
            cos, sin = tslot.ap[:, 0:T], tslot.ap[:, T:2 * T]
            (v_re, re_done), (v_im, im_done) = inputs[i]
            wslot, free = sets.take()
            w_re, w_im, z_re, z_im = (wslot.ap[:, n * T:(n + 1) * T] for n in range(4))
            tt(dve, w_re, cos, v_re.ap, ALU.mult, after=[loaded, re_done, im_done] + free)
            tt(dve, z_re, sin, v_im.ap, ALU.mult, free=True)
            tt(dve, w_im, cos, v_im.ap, ALU.mult, free=True)
            v = tt(dve, z_im, sin, v_re.ap, ALU.mult, free=True)
            v_re.free = v_im.free = [v]
            tt(dve, w_re, w_re, z_re, ALU.add)
            tt(dve, w_im, w_im, z_im, ALU.subtract, free=True)
            first = True
            for z, w in ((z_re, w_re), (z_im, w_im)):
                for ct in range(KC):
                    q = ct * PPC + i
                    rate = mag[:, q:q + 1].to_broadcast([P, NB])
                    v = scan(z[:, ct * NB:(ct + 1) * NB], rate, w[:, ct * NB:(ct + 1) * NB], (), not first)
                    first = False
            eslot, free = ends.take()
            e_re, e_im = eslot.ap[:, 0, :, 1:NB + 1], eslot.ap[:, 1, :, 1:NB + 1]
            g0 = tt(pool, w_re, z_re, sin, ALU.mult, after=[v])
            tt(pool, e_im, chunks(z_im, KC), chunks(cos, KC), ALU.mult, after=free + [zero], free=True)
            g = tt(pool, e_im, e_im, chunks(w_re, KC), ALU.add)
            tt(dve, w_im, z_im, sin, ALU.mult)
            tt(dve, e_re, chunks(z_re, KC), chunks(cos, KC), ALU.mult, after=free, free=True)
            v = tt(dve, e_re, e_re, chunks(w_im, KC), ALU.subtract)
            wslot.free = tslot.free = [v, g]
            if i + 2 < PPC:
                tslot, free = turn.take()
                turns.append((tslot, act.dma(lambda e, i=i, tslot=tslot: e.dma_start(tslot.ap, tables_dram[i + 2]),
                                             turn_sems[i % 2], 32, free)))
                to_ends(i + 2)
            rows = slice(i * PCH, (i + 1) * PCH)
            for ct in range(KC):
                out = y_banks[ct].ap.rearrange("p (j k) -> p j k", k=STEPS)[rows]
                for k in range(STEPS):
                    for part in range(2):
                        pe.wait(v, g)
                        accumulate(out[:, :, k], c_power[:, k, part, ct * PPC + i, :], eslot.ap[:, part, ct, 0:NB])
            eslot.free = [pe.last()]
        y_done = []
        for ct in range(KC):
            v = stt(y[:, ct, :], u[:, ct, :], S("s5_d", ct, ct + 1), y_banks[ct].ap, ALU.mult, ALU.add, after=[pe.last()])
            y_banks[ct].free = [v]
            y_done.append(v)
        z_done = []
        c2 = 2.0 * float(np.sqrt(2.0 / np.pi))
        for m in range(KC):
            t1, t2 = gb[:, 0, :], gb[:, 1, :]
            tt(dve, t1, y[:, m, :], y[:, m, :], ALU.mult)
            ts(dve, t1, t1, 0.044715, ALU.mult, 1.0, ALU.add)
            v = tt(dve, t1, t1, y[:, m, :], ALU.mult)
            a = activate(t2, t1, ACT.Sigmoid, scale=c2, after=[v])
            z_done.append(tt(dve, y[:, m, :], y[:, m, :], t2, ALU.mult, after=[a]))
        o_done = []
        for m in range(KC):
            bank, done = product(plan["glu"][m], [y[:, k, :] for k in range(KC)], z_done)
            a = activate(gb[:, 2 + m % 2, :], bank.ap, ACT.Sigmoid, bias=S("b_glu", m, m + 1), after=[done] + z_done + o_done)
            bank.free = [a]
            o_done.append(tt(dve, u[:, m, :], y[:, m, :], gb[:, 2 + m % 2, :], ALU.mult, after=[a]))
        cat = [hc[:, k, :] for k in range(KC)] + [u[:, k, :] for k in range(KC)]
        return residual("ab_out", cat, conv + o_done, h, r)

    def residual(name, x, x_ready, h, r):
        out = []
        for m in range(KD):
            bank, done = product(plan[name][m], x, x_ready)
            v = stt(r[:, m, :], h[:, m, :], ALPHA, bank.ap, ALU.mult, ALU.add, after=[done] + x_ready)
            bank.free = [v]
            out.append(v)
            add_to_sums(r, m, v)
        return out

    def turn_probabilities(p_ap, n, dst, p_ready, evac):
        bank, free = banks.take()
        pe.wait(*free)
        nch = -(-n // P)
        for c in range(nch):
            w = min(P, n - c * P)
            transpose(bank.ap[0:w, c * P:(c + 1) * P], p_ap[:, c * P:c * P + w], [p_ready])
        rows = min(P, n)
        a = copy(evac, dst[0:rows, 0:nch * P], bank.ap[0:rows, 0:nch * P], [pe.last()])
        bank.free = [a]
        return a

    def mixer_c(h, ready, r):
        at = [0]

        def get(n):
            at[0] += n
            assert at[0] <= 24576
            return region(at[0] - n, n)

        x = [h[:, k, :] for k in range(KD)]
        qT, kT = chunks(get(HEADS * T), HEADS), chunks(get(KVH * T), KVH)
        qi, ki = chunks(get(4 * T), 4), get(T)
        v_tok = chunks(get(TB * 256), TB)
        wi = chunks(get(TB * IH), TB)
        bias = [get((b + 1) * P) for b in range(TB)]
        rope = {n: (get(T), get(T)) for n in "ai"}
        raws = Ring([get(T) for _ in range(2)])
        score = get(T)
        relus = Ring([get(T) for _ in range(2)])
        begin = [pe.last()]
        pos_i, ang, kk = raws.slots[0].ap, score, relus.slots[0].ap
        pos_loaded = load(act, "pos_loaded", pos_i.bitcast(I32), io["positions"], begin)
        pos = relus.slots[1].ap
        copy(dve, pos, pos_i.bitcast(I32), [pos_loaded] + begin)
        rope_ready = []
        for n in "ai":
            cos, sin = rope[n]
            ts(dve, ang, pos, C(f"inv_{n}"), ALU.mult)
            v = reduce_angle(ang, kk, ang)
            rope_ready.append(sin_cos(sin, cos, ang, 0.5, C(f"sgn_{n}"), [v]))

        def rotated(pieces, dst, n, begun=None):
            cos, sin = rope[n]
            bank, done = begun or product(pieces, x, ready)
            slot, free = raws.take()
            a = copy(act, slot.ap, bank.ap, [done, rope_ready[0]] + free)
            bank.free = [a]
            other, free = banks.take()
            matmul(other.ap, C(f"swap_{n}"), slot.ap, True, True, free + [a])
            done = pe.last()
            tt(pool, dst, slot.ap, cos, ALU.mult, after=[a] + rope_ready)
            g = pool.last()
            v = tt(dve, slot.ap, other.ap, sin, ALU.mult, after=[done, g])
            other.free = [v]
            v = tt(dve, dst, dst, slot.ap, ALU.add)
            slot.free = [v]
            return v

        begun = lead("c_index", x, ready)
        qi_ready = [rotated(None, qi[:, m, :], "i", begun[m]) for m in range(4)]
        ki_ready = rotated(None, ki, "i", begun[4])
        outs, done = tokens_product(plan["c_weight"][0], x, IH)
        for b in range(TB):
            wi_ready = ts(dve, wi[:, b, :], outs[b].ap[:, 0:IH], float(IH ** -0.5 * ID ** -0.5), ALU.mult, after=[done])
            outs[b].free = [wi_ready]
        outs, done = tokens_product(plan["c_value"][0], x, 256)
        v_ready = []
        for b in range(TB):
            v_ready.append(copy(act, v_tok[:, b, :], outs[b].ap[:, 0:256], [done]))
            outs[b].free = [v_ready[-1]]
        bias_ready = []
        top8 = stat[:, 0:8]
        for b in range(TB):
            n = (b + 1) * P
            far = C("far_causal", T - P - b * P, T)
            if b == 0:
                bias_ready.append(ts(dve, bias[b], far, -1e29, ALU.is_le, NEG, ALU.mult))
                continue
            for i in range(IH):
                half = slice((i % 2) * ID, (i % 2 + 1) * ID)
                bank, free = banks.take()
                matmul(bank.ap[:, 0:n], qi[half, i // 2, b * P:(b + 1) * P], ki[half, 0:n], True, True,
                       free + qi_ready + [ki_ready])
                done = pe.last()
                slot, free = relus.take()
                a = activate(slot.ap[:, 0:n], bank.ap[:, 0:n], ACT.Relu, after=[done] + free + rope_ready)
                bank.free = [a]
                w = wi[:, b, i:i + 1]
                if i == 0:
                    v = ts(dve, score[:, 0:n], slot.ap[:, 0:n], w, ALU.mult, after=[a])
                else:
                    v = stt(score[:, 0:n], slot.ap[:, 0:n], w, score[:, 0:n], ALU.mult, ALU.add, after=[a])
                slot.free = [v]
            slot, free = relus.take()
            ts(dve, slot.ap[:, 0:n], far, -1e29, ALU.is_le, CAUSAL_FILL, ALU.mult, after=free)
            v = tt(dve, score[:, 0:n], score[:, 0:n], slot.ap[:, 0:n], ALU.add)
            slot.free = [v]
            for _ in range(TOPK // 8):
                top_eight(top8, score[:, 0:n])
                replace_eight(score[:, 0:n], top8, TAKEN)
            bias_ready.append(ts(dve, bias[b], score[:, 0:n], -2e38, ALU.is_ge, NEG, ALU.mult))
        qk_ready = []
        for m in range(HEADS + KVH):
            qk_ready.append(rotated(plan["c_qk"][m], qT[:, m, :] if m < HEADS else kT[:, m - HEADS, :], "a"))
        logits = Ring([raws.slots[0].ap, raws.slots[1].ap])
        turned = Ring([relus.slots[0].ap, relus.slots[1].ap, rope["i"][0], rope["i"][1]])
        stats = Ring([stat[:, 16 + 4 * i:20 + 4 * i] for i in range(4)])
        scale = float(HD ** -0.5)
        items = [(hd, b) for hd in range(HEADS) for b in range(TB)]
        state, o_ready, o_bank = {}, [], {}

        def scores(i):
            hd, b = items[i]
            n = (b + 1) * P
            bank, free = banks.take()
            matmul(bank.ap[:, 0:n], qT[:, hd, b * P:(b + 1) * P], kT[:, hd // 4, 0:n], True, True, free + qk_ready)
            state[i] = (bank, pe.last())

        def weigh(i):
            hd, b = items[i]
            n = (b + 1) * P
            bank, done = state[i]
            slot, free = logits.take()
            l = slot.ap[:, 0:n]
            st, sfree = stats.take()
            m, z = st.ap[:, 0:1], st.ap[:, 1:2]
            v = tt(dve, l, bias[b], bank.ap[:, 0:n], ALU.add, after=[done] + free + sfree + qk_ready)
            bank.free = [v]
            reduce(m, l, ALU.max)
            v = ts(dve, m, m, -scale, ALU.mult)
            a = activate(l, l, ACT.Exp, scale=scale, bias=m, accum=z, after=[v])
            reciprocal(z, z, [a])
            v = ts(dve, l, l, z, ALU.mult)
            st.free = [v]
            state[i] = (slot, v)

        def attend(i):
            hd, b = items[i]
            n = (b + 1) * P
            slot, p_ready = state[i]
            pt, free = turned.take()
            pe.wait(*free)
            act.wait(*free)
            a = turn_probabilities(slot.ap, n, pt.ap, p_ready, act)
            slot.free = [pe.last()]
            if b == 0:
                o_bank[hd], free = banks.take()
                pe.wait(*free)
            for c in range(b + 1):
                matmul(o_bank[hd].ap[:, b * P:(b + 1) * P], v_tok[:, c, (hd // 4) * HD:(hd // 4 + 1) * HD],
                       pt.ap[:, c * P:(c + 1) * P], c == 0, c == b, [a] + v_ready)
            pt.free = [pe.last()]
            if b == TB - 1:
                o_ready.append(copy(act, qT[:, hd, :], o_bank[hd].ap, [pe.last()]))
                o_bank[hd].free = [o_ready[-1]]

        scores(0)
        for i in range(len(items) + 1):
            if i + 1 < len(items):
                scores(i + 1)
            if i < len(items):
                weigh(i)
            if i >= 1:
                attend(i - 1)
        return residual("c_out", [qT[:, k, :] for k in range(HEADS)], o_ready, h, r)

    def nsa(h, ready, r, r_ready):
        at = [0]

        def get(n):
            at[0] += n
            assert at[0] <= 24576, at[0]
            return region(at[0] - n, n)

        x = [h[:, k, :] for k in range(KD)]
        begin = [pe.last()] + r_ready
        q = chunks(get(8 * T), 8)
        keys = chunks(get(3 * T), 3)
        vals = chunks(get(TB * 384), TB)
        gate = chunks(get(TB * 24), TB)
        kc = get(NCMP + 1)
        vc = get(P)
        merge_at = at[0]
        cmp_in = [get(T) for _ in range(2)]
        blocks = chunks(get(CL * 2 * NCMP), CL)
        hid = [[get(2 * NCMP) for _ in range(2)] for _ in range(2)]
        sig = get(2 * NCMP)
        hid_ready = [[], []]
        cin = []
        begun = lead("b_compress_in", x, ready)
        for c in range(2):
            bank, done = begun[c]
            cin.append(copy(act, cmp_in[c], bank.ap, [done] + begin))
            bank.free = [cin[-1]]
        for c in range(2):
            z = memset(blocks, 0.0, [pe.last()] + begin)
            for kv in range(2):
                half = slice(kv * BD, (kv + 1) * BD)
                for l in range(2):
                    src = cmp_in[c][half, l * CS:l * CS + NCMP * CS].rearrange("p (b l) -> p l b", l=CS)
                    dst = blocks[half, l * CS:(l + 1) * CS, kv * NCMP:(kv + 1) * NCMP]
                    pos = S("pos_k" if c == 0 else "pos_v", l * CS, (l + 1) * CS)[half, :]
                    v = tt(dve, dst, src, pos.unsqueeze(2).to_broadcast([BD, CS, NCMP]), ALU.add, after=[cin[c]])
            for m in range(2):
                bank, free = banks.take()
                pe.wait(*free)
                pieces = plan["b_compress"][2 * c + m]
                for l in range(CL):
                    w = take(pieces[l])
                    matmul(bank.ap[:, 0:2 * NCMP], w, blocks[:, l, :], l == 0, l == CL - 1, [v])
                a = activate(hid[c][m], bank.ap[:, 0:2 * NCMP], ACT.Silu, after=[pe.last()])
                bank.free = [a]
                hid_ready[c].append(a)
        bank, free = banks.take()
        for k in range(2):
            w = take(plan["b_compress_k"][0][k])
            matmul(bank.ap[:, 0:2 * NCMP], w, hid[0][k], k == 0, k == 1, free + hid_ready[0])
        done = pe.last()
        for kv in range(2):
            half = slice(kv * BD, (kv + 1) * BD)
            cmp_ready = copy(dve, kc[half, 0:NCMP], bank.ap[half, kv * NCMP:(kv + 1) * NCMP], [done])
        bank.free = [cmp_ready]
        bank, free = banks.take()
        pe.wait(*free)
        ws = [take(plan["b_compress_v"][0][k]) for k in range(2)]
        for kv in range(2):
            for k in range(2):
                matmul(bank.ap[0:NCMP, kv * BD:(kv + 1) * BD], hid[1][k][:, kv * NCMP:(kv + 1) * NCMP], ws[k],
                       k == 0, k == 1, hid_ready[1])
        vc_ready = copy(dve, vc[0:NCMP, :], bank.ap[0:NCMP, 0:P], [pe.last()])
        bank.free = [vc_ready]
        outs, done = tokens_product(plan["b_value"][0], x, 384)
        for b in range(TB):
            v_ready = copy(act, vals[:, b, :], outs[b].ap[:, 0:384], [done])
            outs[b].free = [v_ready]
        outs, done = tokens_product(plan["b_gate"][0], x, 24)
        for b in range(TB):
            gate_ready = activate(gate[:, b, :], outs[b].ap[:, 0:24], ACT.Sigmoid, after=[done])
            outs[b].free = [gate_ready]
        k_ready = []
        for i in range(3):
            bank, done = product(plan["b_key"][i], x)
            k_ready.append(copy(act, keys[:, i, :], bank.ap, [done]))
            bank.free = [k_ready[-1]]
        q_ready = []
        for j in range(8):
            bank, done = product(plan["b_query"][j], x)
            q_ready.append(activate(q[:, j, :], bank.ap, ACT.Copy, scale=float(BD ** -0.5), after=[done]))
            bank.free = [q_ready[-1]]
        at[0] = merge_at
        freed = [pe.last(), (dve.done, dve.count), (act.done, act.count)]
        logits = Ring([get(T) for _ in range(8)])
        turned = Ring([get(T) for _ in range(6)])
        m_at = at[0]
        stats = Ring([stat[:, 16 + 8 * i:24 + 8 * i] for i in range(12)])
        inputs = q_ready + k_ready + [v_ready, gate_ready, cmp_ready, vc_ready]

        def branches(kind, head, b):
            if kind == "b":
                return [("swa", max(0, b - 1) * P)]
            return [("cmp", 0), ("slc", 0), ("win", max(0, b - 2) * P)]

        items = [(kind, j, kv, b) for kind in "ab" for j in range(4) for kv in range(2) for b in range(TB)]
        state, o_ready, o_bank = {}, [], {}
        far_of = {"slc": "far_causal", "win": "far_256", "swa": "far_128"}
        key_of = {"slc": 0, "win": 1, "swa": 2}

        def span(name, s0, b):
            return NCMP if name == "cmp" else (b + 1) * P - s0

        def scores(i):
            kind, j, kv, b = items[i]
            half = slice(kv * BD, (kv + 1) * BD)
            qq = q[half, j + (4 if kind == "b" else 0), b * P:(b + 1) * P]
            got = []
            for name, s0 in branches(kind, j + 4 * kv, b):
                n = span(name, s0, b)
                bank, free = banks.take()
                kk = kc[half, 0:NCMP] if name == "cmp" else keys[half, key_of[name], s0:s0 + n]
                matmul(bank.ap[:, 0:n], qq, kk, True, True, free + inputs)
                got.append((name, s0, bank, pe.last()))
            state[i] = got

        def weigh(i):
            kind, j, kv, b = items[i]
            head = j + 4 * kv
            got = []
            for name, s0, bank, done in state[i]:
                n = span(name, s0, b)
                slope = float(SLOPES[head + (0 if name == "swa" else 8)])
                slot, free = logits.take()
                l = slot.ap[:, 0:n]
                st, sfree = stats.take()
                m, z, w = (st.ap[:, c:c + 1] for c in range(3))
                far = (C("far_cmp", b * (NCMP + 1), b * (NCMP + 1) + NCMP) if name == "cmp" else
                       C(far_of[name], T - P - b * P + s0, T))
                v = stt(l, far, slope, bank.ap[:, 0:n], ALU.mult, ALU.add, after=[done] + free + sfree + freed + inputs)
                bank.free = [v]
                reduce(m, l, ALU.max)
                if name == "swa":
                    ts(dve, m, m, S("sinks", head, head + 1), ALU.max)
                v = ts(dve, m, m, -1.0, ALU.mult)
                if name == "swa":
                    activate(w, S("sinks", head, head + 1), ACT.Exp, bias=m, after=[v])
                a = activate(l, l, ACT.Exp, bias=m, accum=z, after=[v])
                if name == "cmp":
                    tt(dve, l, l, C("see_cmp", b * (NCMP + 1), b * (NCMP + 1) + NCMP), ALU.mult, after=[a])
                    reduce(z, l, ALU.add)
                    ts(dve, z, z, 1e-30, ALU.max)
                if name == "swa":
                    tt(dve, z, z, w, ALU.add, after=[a])
                reciprocal(z, z, [a])
                if name != "swa":
                    g = 3 * head + {"cmp": 0, "slc": 1, "win": 2}[name]
                    tt(dve, z, z, gate[:, b, g:g + 1], ALU.mult)
                v = ts(dve, l, l, z, ALU.mult)
                st.free = [v]
                got.append((name, s0, slot, v))
            state[i] = got

        def attend(i):
            kind, j, kv, b = items[i]
            rows = slice(kv * BD, (kv + 1) * BD)
            pts = []
            for name, s0, slot, p_ready in state[i]:
                pt, free = turned.take()
                act.wait(*free)
                a = turn_probabilities(slot.ap, span(name, s0, b), pt.ap, p_ready, act)
                slot.free = [pe.last()]
                pts.append((name, s0, pt, a))
            if b == 0:
                o_bank[kv], free = banks.take()
                pe.wait(*free)
            steps = []
            for name, s0, pt, a in pts:
                if name == "cmp":
                    steps.append((vc[0:NCMP, kv * BD:(kv + 1) * BD], pt.ap[0:NCMP, 0:P], a))
                    continue
                for c in range(span(name, s0, b) // P):
                    col = key_of[name] * P + kv * BD
                    steps.append((vals[:, s0 // P + c, col:col + BD], pt.ap[:, c * P:(c + 1) * P], a))
            for n, (w, p, a) in enumerate(steps):
                matmul(o_bank[kv].ap[rows, b * P:(b + 1) * P], w, p, n == 0, n == len(steps) - 1, [a])
            for _, _, pt, _ in pts:
                pt.free = [pe.last()]
            if b == TB - 1:
                o_ready.append(copy(act, q[rows, j + (4 if kind == "b" else 0), :], o_bank[kv].ap[rows, :], [pe.last()]))
                o_bank[kv].free = [o_ready[-1]]

        scores(0)
        for i in range(len(items) + 1):
            if i < len(items):
                weigh(i)
            if i + 1 < len(items):
                scores(i + 1)
            if i >= 1:
                attend(i - 1)
        at[0] = 8 * T
        mix = chunks(get(KD * T), KD)
        tmp = Ring([get(2 * T) for _ in range(2)])
        done_all = [pe.last(), (act.done, act.count), (dve.done, dve.count)]
        mix_ready = []
        for m in range(KD):
            pc = plan["b_merge"][4 * m:4 * m + 4]
            ga, ga_done = product(pc[0], x)
            gb, gb_done = product(pc[1], x)
            pa, pa_done = product(pc[2], [q[:, k, :] for k in range(4)], o_ready)
            pb, pb_done = product(pc[3], [q[:, 4 + k, :] for k in range(4)])
            slot, free = tmp.take()
            t1, t2 = slot.ap[:, 0:T], slot.ap[:, T:2 * T]
            a1 = activate(t1, ga.ap, ACT.Sigmoid, after=[ga_done] + free + done_all)
            a2 = activate(t2, gb.ap, ACT.Sigmoid, after=[gb_done])
            ga.free, gb.free = [a1], [a2]
            v1 = tt(dve, t1, t1, pa.ap, ALU.mult, after=[a1, pa_done])
            v2 = tt(dve, t2, t2, pb.ap, ALU.mult, after=[a2, pb_done])
            pa.free, pb.free = [v1], [v2]
            v = tt(dve, mix[:, m, :], t1, t2, ALU.add, after=done_all)
            slot.free = [v]
            mix_ready.append(v)
        out = []
        for m in range(KD):
            bank, done = product(plan["b_out"][m], [mix[:, k, :] for k in range(KD)], mix_ready)
            v = tt(dve, r[:, m, :], r[:, m, :], bank.ap, ALU.add, after=[done])
            bank.free = [v]
            out.append(v)
            add_to_sums(r, m, v, plain=False)
        return out

    def turn_tokens(src, b, dst, ready, after):
        for half in range(2):
            bank, free = banks.take()
            pe.wait(*free)
            for k in range(4):
                transpose(bank.ap[:, k * P:(k + 1) * P], src[:, 4 * half + k, b * P:(b + 1) * P], ready)
            q = act if half else dve
            done = copy(q, dst[:, half * T:(half + 1) * T], bank.ap, [pe.last()] + after)
            bank.free = [done]
            yield done

    def route(h, ready, begin):
        x = [h[:, k, :] for k in range(KD)]
        logit = chunks(region(0, TB * 40), TB)
        one = chunks(region(160, 2 * TB * NEXP), 2 * TB)
        both = chunks(region(416, TB * NEXP), TB)
        comb = chunks(region(544, TB * NEXP), TB)
        tmp = region(672, NEXP)
        weight = stat[:, 64:64 + 2 * TB]
        slot = stat[:, 72:72 + 2 * TB]
        slot_i = stat[:, 80:80 + 2 * TB].bitcast(I32)
        flag = stat[:, 88:89].bitcast(I32)
        memset(region(0, TB * 40), -3e38, begin)
        outs, done = tokens_product(plan["router"][0], x, NGRP, ready)
        for b in range(TB):
            v = tt(dve, logit[:, b, 0:NGRP], outs[b].ap[:, 0:NGRP], S("b_group"), ALU.add, after=[done])
            outs[b].free = [v]
        outs, done = tokens_product(plan["router"][1], x, NEXP)
        for b in range(TB):
            v = tt(dve, logit[:, b, 8:40], outs[b].ap[:, 0:NEXP], S("b_expert"), ALU.add, after=[done])
            outs[b].free = [v]
        combs = []
        for b in range(TB):
            gtop, gidx = stat[:, 0:8], stat[:, 8:16].bitcast(U32)
            etop, eidx = stat[:, 16:24], stat[:, 24:32].bitcast(U32)
            gi, ei, chosen, ge, gz, e_in, m, w = (stat[:, 32:33], stat[:, 33:35], stat[:, 40:44], stat[:, 44:48],
                                                 stat[:, 48:49], stat[:, 56:64], stat[:, 49:50],
                                                 weight[:, 2 * b:2 * b + 2])
            gl, el = logit[:, b, 0:8], logit[:, b, 8:40]
            top_eight(gtop, gl)
            where_eight(gidx, gtop, gl)
            copy(dve, gi, gidx[:, 0:1])
            v = ts(dve, m, gtop[:, 0:1], -1.0, ALU.mult)
            a = activate(ge, gl[:, 0:NGRP], ACT.Exp, bias=m, accum=gz, after=[v])
            ts(dve, chosen, C("group", 0, NGRP), gi, ALU.is_equal)
            ts(dve, e_in, el[:, 0:EPG], chosen[:, 0:1], ALU.mult)
            for g in range(1, NGRP):
                stt(e_in, el[:, g * EPG:(g + 1) * EPG], chosen[:, g:g + 1], e_in, ALU.mult, ALU.add)
            top_eight(etop, e_in)
            where_eight(eidx, etop, e_in)
            copy(dve, ei, eidx[:, 0:2])
            for i in range(2):
                stt(ei[:, i:i + 1], gi, float(EPG), ei[:, i:i + 1], ALU.mult, ALU.add)
            v = tt(dve, m, etop[:, 1:2], etop[:, 0:1], ALU.subtract, after=[a])
            a = activate(w[:, 1:2], m, ACT.Exp, after=[v])
            ts(dve, m, w[:, 1:2], 1.0, ALU.add, after=[a])
            tt(dve, m, m, gz, ALU.mult)
            reciprocal(m, m)
            copy(dve, w[:, 0:1], m)
            tt(dve, w[:, 1:2], w[:, 1:2], m, ALU.mult)
            for i in range(2):
                ts(dve, one[:, 2 * b + i, :], C("expert"), ei[:, i:i + 1], ALU.is_equal)
            tt(dve, both[:, b, :], one[:, 2 * b, :], one[:, 2 * b + 1, :], ALU.add)
            ts(dve, tmp, one[:, 2 * b, :], w[:, 0:1], ALU.mult)
            v = stt(comb[:, b, :], one[:, 2 * b + 1, :], w[:, 1:2], tmp, ALU.mult, ALU.add)
            combs.append(v)
        bank, free = banks.take()
        pe.wait(*free)
        for b in range(TB):
            for c in range(b + 1):
                matmul(bank.ap[:, b * NEXP:(b + 1) * NEXP], C("before") if c == b else C("ones"), both[:, c, :],
                       c == 0, c == b, [combs[-1]])
        for c in range(TB):
            matmul(bank.ap[:, TB * NEXP:(TB + 1) * NEXP], C("ones"), both[:, c, :], c == 0, c == TB - 1)
        ranked = pe.last()
        count = stat[:, 90:91]
        reduce(count, bank.ap[:, TB * NEXP:(TB + 1) * NEXP], ALU.max, [ranked])
        flagged = ts(dve, flag, count, float(SLOTS), ALU.is_gt)
        for b in range(TB):
            stt(tmp, C("expert"), float(SLOTS), bank.ap[:, b * NEXP:(b + 1) * NEXP], ALU.mult, ALU.add)
            for i in range(2):
                tt(dve, one[:, 2 * b + i, :], one[:, 2 * b + i, :], tmp, ALU.mult)
                reduce(slot[:, 2 * b + i:2 * b + i + 1], one[:, 2 * b + i, :], ALU.add)
        slotted = copy(dve, slot_i, slot)
        bank.free = [slotted]
        return comb, combs[-1], weight, slot_i, slotted, flag, flagged

    def final_norm(b, xt, ready, gain, gain_loaded):
        square, s = region(12288, D), stat[:, 92:93]
        v = activate(square, xt, ACT.Square, accum=s, after=ready)
        v = ts(dve, s, s, 1.0 / D, ALU.mult, RMS_EPS, ALU.add, after=[v])
        a = activate(s, s, ACT.Sqrt, after=[v])
        reciprocal(s, s, [a])
        v = stt(xt, xt, s, gain, ALU.mult, ALU.mult, after=[gain_loaded])
        return [v]

    def store_out(b, xt, ready):
        return act.dma(lambda e: e.dma_start(io["out"][b * P:(b + 1) * P, :], xt), out_stored, 16 * (b + 1), ready)

    def moe_all(h, r, comb, comb_ready):
        x = [h[:, k, :] for k in range(KD)]
        combT = region(1024, T)
        bank, free = banks.take()
        pe.wait(*free)
        for b in range(TB):
            transpose(bank.ap[0:NEXP, b * P:(b + 1) * P], comb[:, b, :], [comb_ready])
        a = copy(act, combT[0:NEXP, :], bank.ap[0:NEXP, :], [pe.last()])
        bank.free = [a]
        stored = act.dma(lambda e: e.dma_start(combine_dram, combT[0:NEXP, :]), sem("combine_stored"), 16, [a])
        act.wait(stored)
        hidden = Ring([region(4 * T + i * 2 * T, 2 * T) for i in range(2)])
        wts = Ring([region(8 * T + i * T, T) for i in range(4)])
        wsems = [sem(f"combine_loaded{i}") for i in range(4)]
        out = None
        for e_ in range(NEXP):
            hslot, hfree = hidden.take()
            hid = chunks(hslot.ap, 2)
            wt, free = wts.take()
            loaded = sp.dma(lambda e, e_=e_, wt=wt: e.dma_start(wt.ap, combine_dram[e_:e_ + 1, :].to_broadcast([P, T])),
                            wsems[e_ % 4], 16 * (e_ // 4 + 1), free + [stored])
            written = []
            for m in range(2):
                gate, g_done = product(plan[f"moe{e_}_up"][2 * m], x)
                up, u_done = product(plan[f"moe{e_}_up"][2 * m + 1], x)
                a = activate(hid[:, m, :], gate.ap, ACT.Silu, after=[g_done] + hfree)
                gate.free = [a]
                v = tt(dve, hid[:, m, :], hid[:, m, :], up.ap, ALU.mult, after=[a, u_done])
                up.free = [v]
                v = tt(pool, hid[:, m, :], hid[:, m, :], wt.ap, ALU.mult, after=[v, loaded])
                written.append(v)
            wt.free = [v]
            down = [take(piece) for piece in plan[f"moe{e_}_down"][0]]
            pe.wait(*written)
            out = []
            for m in range(KD):
                bank, free = banks.take()
                pe.wait(*free)
                for k in range(2):
                    w = down[2 * k + m // 4][:, (m % 4) * P:(m % 4 + 1) * P]
                    matmul(bank.ap, w, hid[:, k, :], k == 0, k == 1)
                v = tt(dve, r[:, m, :], r[:, m, :], bank.ap, ALU.add, after=[pe.last()])
                bank.free = [v]
                out.append(v)
            hslot.free = [pe.last()]
        for b in range(TB):
            xt = region(8192 + b * D, D)
            done = list(turn_tokens(r, b, xt, out, []))
            store_out(b, xt, final_norm(b, xt, done, gain, gain_loaded))

    def moe_slots(h, r, weight, slot_i, slotted, ready, r_ready):
        xrows = [region(2048 + b * D, D) for b in range(TB)]
        scattered = sem("rows_scattered")
        for b in range(TB):
            done = list(turn_tokens(h, b, xrows[b], ready, []))
            for i in range(2):
                def scatter(e, b=b, i=i):
                    return e.indirect_dma_start(out=slots_in, out_offset=bass.IndirectOffsetOnAxis(
                        ap=slot_i[:, 2 * b + i:2 * b + i + 1], axis=0), in_=xrows[b], in_offset=None)
                rows = pool.dma(scatter, scattered, 16 * (2 * b + i + 1), done + [slotted, zero_filled])
        xt = [region(8192 + b * D, D) for b in range(TB)]
        xt_ready = [list(turn_tokens(r, b, xt[b], r_ready, [])) for b in range(TB)]
        rows_in = Ring([region(13312 + i * D, D) for i in range(3)])
        in_sems = [sem(f"rows_in{i}") for i in range(3)]
        turned = Ring([region(16384 + i * T, T) for i in range(2)])
        hidden = Ring([region(17408 + i * 256, 2 * SLOTS) for i in range(2)])
        rows_out = Ring([region(18432 + i * D, D) for i in range(2)])
        out_sems = [sem(f"rows_out{i}") for i in range(2)]
        state = {}

        def bring(e_):
            slot, free = rows_in.take()
            loaded = sp.dma(lambda e: e.dma_start(slot.ap[0:SLOTS, :], slots_in[e_ * SLOTS:(e_ + 1) * SLOTS, :]),
                            in_sems[e_ % 3], 16 * (e_ // 3 + 1), free + [rows])
            state[e_] = (slot, loaded)

        def turn(e_):
            slot, loaded = state[e_]
            xs, free = turned.take()
            bank, bfree = banks.take()
            pe.wait(*bfree)
            for k in range(KD):
                transpose(bank.ap[:, k * SLOTS:(k + 1) * SLOTS], slot.ap[0:SLOTS, k * P:(k + 1) * P], [loaded])
            slot.free = [pe.last()]
            a = copy(act, xs.ap[:, 0:KD * SLOTS], bank.ap[:, 0:KD * SLOTS], [pe.last()] + free)
            bank.free = [a]
            state[e_] = (xs, a)

        for e_ in range(2):
            bring(e_)
        turn(0)
        stores = []
        for e_ in range(NEXP):
            if e_ + 2 < NEXP:
                bring(e_ + 2)
            xs, ready_x = state[e_]
            x = [xs.ap[:, k * SLOTS:(k + 1) * SLOTS] for k in range(KD)]
            hslot, hfree = hidden.take()
            written = []
            for m in range(2):
                gate, g_done = product(plan[f"moe{e_}_up"][2 * m], x, [ready_x], n=SLOTS)
                up, u_done = product(plan[f"moe{e_}_up"][2 * m + 1], x, n=SLOTS)
                hid = hslot.ap[:, m * SLOTS:(m + 1) * SLOTS]
                a = activate(hid, gate.ap[:, 0:SLOTS], ACT.Silu, after=[g_done] + hfree)
                gate.free = [a]
                v = tt(dve, hid, hid, up.ap[:, 0:SLOTS], ALU.mult, after=[a, u_done])
                up.free = [v]
                written.append(v)
            xs.free = [pe.last()]
            if e_ + 1 < NEXP:
                turn(e_ + 1)
            down = [take(piece) for piece in plan[f"moe{e_}_down"][0]]
            oslot, ofree = rows_out.take()
            copied = []
            for n in range(2):
                bank, free = banks.take()
                pe.wait(*free)
                for k in range(2):
                    matmul(bank.ap[0:SLOTS, :], hslot.ap[:, k * SLOTS:(k + 1) * SLOTS], down[2 * k + n],
                           k == 0, k == 1, written)
                v = copy(dve, oslot.ap[0:SLOTS, n * T:(n + 1) * T], bank.ap[0:SLOTS, :], [pe.last()] + ofree)
                bank.free = [v]
                copied.append(v)
            hslot.free = [pe.last()]
            stored = act.dma(lambda e, e_=e_, oslot=oslot: e.dma_start(slots_out[e_ * SLOTS:(e_ + 1) * SLOTS, :],
                                                                       oslot.ap[0:SLOTS, :]),
                             out_sems[e_ % 2], 16 * (e_ // 2 + 1), copied)
            oslot.free = [stored]
            stores.append(stored)
        gathered = [[sem(f"gathered{b}{i}") for i in range(2)] for b in range(TB)]
        ys = Ring([region(2048 + i * D, D) for i in range(4)])
        for b in range(TB):
            got = []
            for i in range(2):
                y, free = ys.take()

                def gather(e, b=b, i=i, y=y):
                    return e.indirect_dma_start(out=y.ap, out_offset=None, in_=slots_out,
                                                in_offset=bass.IndirectOffsetOnAxis(
                                                    ap=slot_i[:, 2 * b + i:2 * b + i + 1], axis=0))
                loaded = pool.dma(gather, gathered[b][i], 16, free + stores[-2:] + [rows])
                got.append((y, loaded))
            for i, (y, loaded) in enumerate(got):
                w = weight[:, 2 * b + i:2 * b + i + 1]
                v = stt(xt[b], y.ap, w, xt[b], ALU.mult, ALU.add, after=[loaded] + xt_ready[b])
                y.free = [v]
            store_out(b, xt[b], final_norm(b, xt[b], [v], gain, gain_loaded))

    aside = [s5_factors, lambda: s5_b(0)]
    for k in range(STEPS):
        aside.append(lambda k=k: s5_turn_b(k))
        aside.append(lambda k=k: s5_b(k + 1) if k + 1 < STEPS else None)
    for k in range(STEPS):
        aside.append(lambda k=k: s5_c(k))
    for i in range(PPC):
        aside.append(lambda i=i: s5_turn(i))
    r_ready = ffn("ffn0", buf_a, [x_loaded], buf_b, aside)
    h_ready = layer_norm(buf_b, r_ready, buf_a, 0, 0)
    r_ready = mixer_ab(buf_a, h_ready, buf_b)
    h_ready = layer_norm(buf_b, r_ready, buf_a, KD, KD)
    r_ready = ffn("ffn1", buf_a, h_ready, buf_b)
    h_ready = layer_norm(buf_b, r_ready, buf_a, 2 * KD, 2 * KD)
    r_ready = ple(0, buf_a, h_ready, buf_b, *ple_proj(0), False)
    zeros = region(20480, D)
    zeroed = memset(zeros, 0.0)
    slots_rows = slots_in.rearrange("(n p) d -> p n d", p=P)
    zero_filled = load(act, "zero_filled", slots_rows, zeros.unsqueeze(1).to_broadcast([P, NEXP * SLOTS // P, D]), [zeroed])
    r_ready = ffn("ffn2", buf_b, r_ready, buf_a)
    h_ready = layer_norm(buf_a, r_ready, buf_b, 3 * KD, 3 * KD)
    r_ready = mixer_c(buf_b, h_ready, buf_a)
    h_ready = layer_norm(buf_a, r_ready, buf_b, 4 * KD, 4 * KD)
    r_ready = ffn("ffn3", buf_b, h_ready, buf_a)
    h_ready = layer_norm(buf_a, r_ready, buf_b, 5 * KD, 5 * KD)
    r_ready = ple(1, buf_b, h_ready, buf_a, *ple_proj(1), True)
    h_ready = rms_norm(buf_a, r_ready, buf_b, "mix_g")
    r_ready = nsa(buf_b, h_ready, buf_a, r_ready)
    h_ready = rms_norm(buf_a, r_ready, buf_b, "ffn_g")
    out_stored = sem("out_stored")
    gain = region(21504, D)
    gain_loaded = load(act, "gain_loaded", gain, io["gain"], [pe.last()] + r_ready)
    comb, comb_ready, weight, slot_i, slotted, flag, flagged = route(buf_b, h_ready, [pe.last()] + r_ready)
    queues = (pe, dve, act, pool, sp)
    for q in queues:
        q.wait(flagged)
    states = [q.branch(flag[0:1, :]) for q in queues]
    kept = ([list(b.free) for b in banks.slots], banks.n, dict(stream))
    moe_all(buf_b, buf_a, comb, comb_ready)
    act.wait((out_stored, 16 * TB))
    assert stream["next"] == len(places)
    for q, state in zip(queues, states):
        q.branch(None, state)
    for b, free in zip(banks.slots, kept[0]):
        b.free = free
    banks.n = kept[1]
    stream.update(kept[2])
    moe_slots(buf_b, buf_a, weight, slot_i, slotted, h_ready, r_ready)
    act.wait((out_stored, 16 * TB))
    assert stream["next"] == len(places)

    block = ctx.enter_context(nc.Block())

    @block.tensor
    def _(e):
        pe.issue(e)

    @block.vector
    def _(e):
        dve.issue(e)

    @block.scalar
    def _(e):
        act.issue(e)

    @block.gpsimd
    def _(e):
        pool.issue(e)

    @block.sync
    def _(e):
        sp.issue(e)


def pack_weights(inputs):
    plan = weight_plan()
    places, n_blocks = place_pieces(plan)
    out = np.zeros((n_blocks, P, BLOCK), np.float32)
    for (b, c), (_, (name, index, rows, cols)) in zip(places, in_order(plan)):
        w = inputs[name][index]
        r = 0
        for r0, nr in rows:
            at = c
            for c0, nc_ in cols:
                out[b, r:r + nr, at:at + nc_] = w[r0:r0 + nr, c0:c0 + nc_]
                at += nc_
            r += nr
    return out


def by_chunk(a):
    a = np.asarray(a)
    return a.reshape(-1, P).T


def pack_small(inp):
    at, n = small_layout()
    out = np.zeros((P, n), np.float32)

    def put(name, value):
        out[:, at[name][0]:at[name][1]] = value

    put("ln_g", by_chunk(inp["ln_g"]))
    put("ln_b", by_chunk(inp["ln_b"]))
    put("conv_w", by_chunk(inp["conv_w"][0]))
    put("s5_d", by_chunk(inp["s5_d"][0]))
    put("b_glu", by_chunk(inp["s5_b_glu"][0]))
    put("log_dt", np.repeat(inp["s5_log_dt"][0].reshape(PAIRS, 2, 1), STATES, axis=2).reshape(PAIRS, P).T)
    put("lam_re", inp["s5_lam_re"][0].reshape(PAIRS, P).T)
    put("lam_im", inp["s5_lam_im"][0].reshape(PAIRS, P).T)
    put("mix_g", by_chunk(inp["norm_mix_g_2"][0]))
    put("ffn_g", by_chunk(inp["norm_ffn_g_2"][0]))
    put("pos_k", np.tile(inp["cmp_pos_k_2"][0].T, (2, 1)))
    put("pos_v", np.tile(inp["cmp_pos_v_2"][0].T, (2, 1)))
    put("sinks", np.broadcast_to(inp["sinks_2"][0], (P, BH)))
    put("b_group", np.broadcast_to(inp["b_group_2"][0], (P, NGRP)))
    put("b_expert", np.broadcast_to(inp["b_expert_2"][0], (P, NEXP)))
    return out


def spread_pairs(a):
    out = np.zeros((P, PAIRS, PCH), np.float32)
    for g in range(GROUPS):
        q, half = g // 2, g % 2
        out[half * STATES:(half + 1) * STATES, q, half * GCH:(half + 1) * GCH] = a[g]
    return out


def kernel(**inputs):
    import concourse.bacc as bacc
    from concourse.bass_utils import run_bass_kernel_spmd

    inp = {k: np.asarray(v) for k, v in inputs.items()}
    arrays = {
        "x": np.ascontiguousarray(inp["x"][0].T),
        "p": np.ascontiguousarray(inp["p"][:, 0].transpose(0, 2, 1)),
        "positions": np.ascontiguousarray(np.broadcast_to(inp["positions"][0].astype(np.int32), (P, T))),
        "weights": pack_weights(inp),
        "small": pack_small(inp),
        "const": constants(),
        "gain": np.ascontiguousarray(np.broadcast_to(inp["norm_final_g_2"], (P, D))),
        "s5_b_re": spread_pairs(inp["s5_b_re"][0]),
        "s5_b_im": spread_pairs(inp["s5_b_im"][0]),
        "s5_c_re": spread_pairs(inp["s5_c_re"][0].transpose(0, 2, 1)),
        "s5_c_im": spread_pairs(inp["s5_c_im"][0].transpose(0, 2, 1)),
    }
    nc = bacc.Bacc("TRN2", target_bir_lowering=False, num_devices=1)
    io = {n: nc.dram_tensor("in_" + n, a.shape, mybir.dt.from_np(a.dtype), kind="ExternalInput").ap()
          for n, a in arrays.items()}
    io["out"] = nc.dram_tensor("out", [T, D], F32, kind="ExternalOutput").ap()
    build(nc, io)
    got = run_bass_kernel_spmd(nc, [{"in_" + n: a for n, a in arrays.items()}], core_ids=[0])
    return got.results[0]["out"][None]
```

```python
from contextlib import ExitStack

import numpy as np

import concourse.bass as bass
from concourse import mybir

F32 = mybir.dt.float32
I32 = mybir.dt.int32
U32 = mybir.dt.uint32
ALU = mybir.AluOpType
ACT = mybir.ActivationFunctionType
AX = mybir.AxisListType

P = 128
T = 512
TB = T // P
D = 1024
KD = D // P
DEPTH = 2
FF = 2816
KF = FF // P
PLE = 256
CC = 512
KC = CC // P
GROUPS, GCH, STATES = 32, 16, 64
PAIRS = GROUPS // 2
PCH = 2 * GCH
PPC = P // PCH
STEPS = 4
NB = T // STEPS
HEADS, HD, KVH = 8, 128, 2
IH, ID = 8, 64
TOPK = 128
AQ, AK, AV, AI, AKI, AW = np.cumsum([0, 1024, 256, 256, 512, 64]).tolist()
THETA = 500000.0
LN_EPS, RMS_EPS = 1e-5, 1e-6
ALPHA = float((2 * DEPTH) ** 0.25)
BH, BD = 8, 64
CL, CS, CHID = 32, 16, 256
NCMP = T // CS - CL // CS + 1
(BQA, BKC, BVC, BKS, BVS, BKW, BVW, BG, BQB, BKB, BVB, BM) = np.cumsum(
    [0, 512, 128, 128, 128, 128, 128, 128, 24, 512, 128, 128]).tolist()
NGRP, EPG, NEXP, EFF = 4, 8, 32, 256
SLOTS = 64
NEG = -1e30
HELD = -1e20
CAUSAL_FILL = -1e30
TAKEN = -3e38
SLOPES = 2.0 ** (-8.0 * np.arange(1, 17) / 16)
SLOPES = np.asarray(SLOPES, np.float32)
PI = float(np.pi)
ROUND = 12582912.0
ROUND13 = 1536.0
TWO_PI_1 = 6.28125
TWO_PI_2 = 0.0019350051879882812
TWO_PI_3 = float(2 * np.pi - TWO_PI_1 - TWO_PI_2)

BLOCK = 16 * P
RING = 6


def dense(name, index, n_rows, col0, n_cols, width=P):
    return [[(name, index, ((k * P, P),), ((col0 + m * width, min(width, n_cols - m * width)),))
             for k in range(n_rows // P)] for m in range(-(-n_cols // width))]


def columns(name, index, n_rows, *segments):
    return [(name, index, ((k * P, P),), tuple(segments)) for k in range(n_rows // P)]


def ffn_pieces(layer, i):
    up = []
    for g, u in zip(dense("ffn_w1", (layer, i), D, 0, FF), dense("ffn_w3", (layer, i), D, 0, FF)):
        up += [g, u]
    return up, dense("ffn_w2", (layer, i), FF, 0, D)


def pair_rows(name, index, first):
    return [[(name, index, ((j * BD, BD), ((4 + j) * BD, BD)), ((m * P, P),)) for j in range(4)]
            for m in range(D // P)]


def head_columns(base, j):
    return ((base + j * BD, BD), (base + (4 + j) * BD, BD))


def weight_plan():
    plan = {}
    plan["ffn0_up"], plan["ffn0_down"] = ffn_pieces(0, 0)
    plan["ab_in"] = dense("ab_w_in", (0,), D, 0, 4 * CC)
    plan["glu"] = dense("s5_w_glu", (0,), CC, 0, CC)
    plan["ab_out"] = dense("ab_w_out", (0,), 2 * CC, 0, D)
    plan["ffn1_up"], plan["ffn1_down"] = ffn_pieces(0, 1)
    plan["ple0_proj"] = dense("ple_w_proj", (0,), PLE, 0, D)
    plan["ple0_gate"] = dense("ple_w_gate", (0,), D, 0, D)
    plan["ffn2_up"], plan["ffn2_down"] = ffn_pieces(1, 0)
    plan["c_index"] = (dense("c_w_in", (0,), D, AI, IH * ID) +
                       [columns("c_w_in", (0,), D, (AKI, ID), (AKI, ID))])
    plan["c_weight"] = [columns("c_w_in", (0,), D, (AW, IH))]
    plan["c_qk"] = dense("c_w_in", (0,), D, AQ, HEADS * HD) + dense("c_w_in", (0,), D, AK, KVH * HD)
    plan["c_value"] = [columns("c_w_in", (0,), D, (AV, 256))]
    plan["c_out"] = dense("c_w_out", (0,), D, 0, D)
    plan["ffn3_up"], plan["ffn3_down"] = ffn_pieces(1, 1)
    plan["ple1_proj"] = dense("ple_w_proj", (1,), PLE, 0, D)
    plan["ple1_gate"] = dense("ple_w_gate", (1,), D, 0, D)
    w = ("w_in_2", (0,), D)
    plan["b_compress_in"] = [columns(*w, (BKC, P)), columns(*w, (BVC, P))]
    plan["b_value"] = [columns(*w, (BVS, P), (BVW, P), (BVB, P))]
    plan["b_gate"] = [columns(*w, *[(BG + 3 * head + g, 1) for head in range(BH) for g in (0, 2, 1)])]
    compress = [
        [[(f"cmp_w1_{c}_2", (0,), ((l * BD, BD), (l * BD, BD)), ((m * P, P),)) for l in range(CL)]
         for m in range(CHID // P)] for c in "kv"]
    plan["b_compress_0"] = compress[0]
    plan["b_key"] = [columns(*w, (b, P)) for b in (BKS, BKW, BKB)]
    plan["b_compress_1"] = compress[1]
    plan["b_query"] = [columns(*w, *head_columns(b, j)) for b in (BQA, BQB) for j in range(4)]
    plan["b_compress_k"] = [[("cmp_w2_k_2", (0,), ((k * P, P),), ((0, BD), (0, BD))) for k in range(CHID // P)]]
    plan["b_compress_v"] = [[("cmp_w2_v_2", (0,), ((k * P, P),), ((0, BD),)) for k in range(CHID // P)]]
    plan["b_merge"] = []
    for m in range(KD):
        plan["b_merge"] += [columns(*w, (BM + m * P, P)), columns(*w, (BM + D + m * P, P)),
                            pair_rows("w_a_2", (0,), 0)[m], pair_rows("w_b_2", (0,), 0)[m]]
    plan["b_out"] = dense("w_o_2", (0,), D, 0, D)
    plan["router"] = [columns("w_group_2", (0,), D, (0, NGRP)), columns("w_expert_2", (0,), D, (0, NEXP))]
    for e in range(NEXP):
        up = []
        for g, u in zip(dense("w_gate_e_2", (0, e), D, 0, EFF), dense("w_up_e_2", (0, e), D, 0, EFF)):
            up += [g, u]
        plan[f"moe{e}_up"] = up
        plan[f"moe{e}_down"] = [[("w_down_e_2", (0, e), ((k * P, P),), ((n * T, T),))
                                 for k in range(EFF // P) for n in range(D // T)]]
    return plan


def width_of(piece):
    return sum(n for _, n in piece[3])


LEAD = {"ffn1_up": 4, "ffn2_up": 4, "ffn3_up": 4, "ab_in": 4, "c_index": 5, "ple0_gate": 4, "ple1_gate": 4,
        "b_compress_in": 2}


def in_order(plan):
    for name, products in plan.items():
        n = LEAD.get(name, 0)
        for pieces in zip(*products[:n]):
            for piece in pieces:
                yield name, piece
        for product in products[n:]:
            for piece in product:
                yield name, piece


def place_pieces(plan):
    places, block, col, last = [], 0, 0, None
    for name, piece in in_order(plan):
        if name != last and name.startswith("moe") and col:
            block, col = block + 1, 0
        last = name
        n = width_of(piece)
        if col + n > BLOCK:
            block, col = block + 1, 0
        places.append((block, col))
        col += n
    return places, block + 1


def small_layout():
    at, n = {}, 0
    for name, width in (("ln_g", DEPTH * 3 * KD), ("ln_b", DEPTH * 3 * KD), ("conv_w", 3 * KC), ("s5_d", KC),
                        ("b_glu", KC), ("log_dt", PAIRS), ("lam_re", PAIRS), ("lam_im", PAIRS),
                        ("mix_g", KD), ("ffn_g", KD), ("pos_k", CL), ("pos_v", CL),
                        ("sinks", BH), ("b_group", NGRP), ("b_expert", NEXP)):
        at[name] = (n, n + width)
        n += width
    return at, n


def const_layout():
    at, n = {}, 0
    for name, width in (("ident", P), ("mean", P), ("far_causal", T), ("far_256", T), ("far_128", T),
                        ("steps", T), ("swap_a", P), ("swap_i", P), ("inv_a", 1), ("inv_i", 1),
                        ("sgn_a", 1), ("sgn_i", 1), ("far_cmp", TB * (NCMP + 1)),
                        ("expert", NEXP), ("group", EPG), ("before", P), ("ones", P)):
        at[name] = (n, n + width)
        n += width
    return at, n


def constants():
    at, n = const_layout()
    c = np.zeros((P, n), np.float32)

    def put(name, value):
        c[:, at[name][0]:at[name][1]] = value

    p = np.arange(P)[:, None]
    put("ident", np.eye(P))
    put("mean", np.full((P, P), 1.0 / D))
    back = (np.arange(T)[None, :] - (T - P)) - p
    for name, window in (("far_causal", T), ("far_256", 256), ("far_128", 128)):
        put(name, np.where((back <= 0) & (back > -window), back, NEG))
    put("steps", np.arange(T)[None, :])
    for name, rot, period, inv in (("a", HD // 4, HD, "inv_a"), ("i", ID // 4, ID, "inv_i")):
        half = rot // 2
        swap, freq, sign = np.zeros((P, P)), np.zeros((P, 1), np.float32), np.ones((P, 1))
        table = np.float32(THETA) ** (-np.arange(0, rot, 2, dtype=np.float32) / np.float32(rot))
        for base in range(0, P, period):
            for j in range(half):
                swap[base + j + half, base + j] = swap[base + j, base + j + half] = 1
                freq[base + j] = freq[base + j + half] = table[j]
                sign[base + j] = -1
        put(f"swap_{name}", swap)
        put(inv, freq)
        put(f"sgn_{name}", 2 * sign)
    end = np.arange(NCMP) * CS + CL - 1
    far = np.full((P, TB, NCMP + 1), NEG, np.float32)
    for b in range(TB):
        back = end[None, :] - (b * P + p)
        far[:, b, :NCMP] = np.where(back <= 0, back, NEG)
    put("far_cmp", far.reshape(P, -1))
    put("expert", np.arange(NEXP)[None, :])
    put("group", np.arange(EPG)[None, :])
    put("before", p < np.arange(P)[None, :])
    put("ones", 1.0)
    return c


class Queue:

    def __init__(self, done, chained):
        self.done, self.chained, self.count, self.items, self.seen = done, chained, 0, [], {}
        self.flag, self.branches = None, []

    def branch(self, flag, state=None):
        if state is None:
            self.common, self.flag = self.items, flag
            state = (self.count, dict(self.seen))
        self.count, self.seen = state[0], dict(state[1])
        self.items = []
        self.branches.append(self.items)
        return state

    def wait(self, *after):
        for sem, value in after:
            if self.seen.get(id(sem), 0) < value:
                self.seen[id(sem)] = value
                self.items.append(["wait", sem, value])

    def last(self):
        if self.items and self.items[-1][0] == "quiet":
            self.items[-1][0] = "signal"
            self.count += 1
        return (self.done, self.count)

    def do(self, instruction, after=(), free=False):
        if self.chained and not free and self.count:
            self.wait((self.done, self.count))
        self.wait(*after)
        self.count += 1
        self.items.append(["signal", instruction, None])
        return (self.done, self.count)

    def quiet(self, instruction, after=()):
        self.wait(*after)
        self.items.append(["quiet", instruction, None])

    def dma(self, instruction, sem, value, after=()):
        self.wait(*after)
        self.items.append(["dma", instruction, sem])
        return (sem, value)

    def issue(self, engine):
        self.issue_items(engine, self.common)
        flag = engine.value_load(self.flag, min_val=0, max_val=1)
        with engine.If(flag != 0):
            self.issue_items(engine, self.branches[0])
        with engine.Else():
            self.issue_items(engine, self.branches[1])

    def issue_items(self, engine, items):
        for kind, what, arg in items:
            if kind == "wait":
                engine.wait_ge(what, arg)
            elif kind == "signal":
                what(engine).then_inc(self.done, 1)
            elif kind == "quiet":
                what(engine)
            else:
                what(engine).then_inc(arg, 16)


class Slot:

    def __init__(self, ap):
        self.ap, self.free = ap, []


class Ring:
    def __init__(self, aps):
        self.slots, self.n = [Slot(a) for a in aps], 0

    def take(self):
        for _ in self.slots:
            self.n += 1
            slot = self.slots[(self.n - 1) % len(self.slots)]
            if slot.free is not None:
                free, slot.free = slot.free, None
                return slot, free
        raise AssertionError("every slot is held")


def build(nc, io):
    ctx = ExitStack()
    with ctx:
        build_in(nc, io, ctx)


def build_in(nc, io, ctx):
    def sbuf(name, n, dt=F32):
        return ctx.enter_context(nc.sbuf_tensor(name, [P, n], dt))

    def sem(name):
        return ctx.enter_context(nc.semaphore(name))

    def chunks(ap, c):
        return ap.rearrange("p (c n) -> p c n", c=c)

    const_at, n_const = const_layout()
    small_at, n_small = small_layout()
    const = sbuf("const", n_const)
    small = sbuf("small", n_small)
    ring = sbuf("ring", RING * BLOCK)
    buf_a = chunks(sbuf("buf_a", KD * T)[:, :], KD)
    buf_b = chunks(sbuf("buf_b", KD * T)[:, :], KD)
    norm = sbuf("norm", 4 * T)
    stat = sbuf("stat", 512)
    area = sbuf("area", 24576)
    banks = Ring([ctx.enter_context(nc.psum_tensor(f"bank{i}", [P, T], F32))[:, :] for i in range(8)])
    tables_dram = nc.dram_tensor("turn_tables", [PPC, P, 2 * T], F32, kind="Internal").ap()
    combine_dram = nc.dram_tensor("combine", [NEXP, T], F32, kind="Internal").ap()
    slots_in = nc.dram_tensor("slots_in", [NEXP * SLOTS, D], F32, kind="Internal").ap()
    slots_out = nc.dram_tensor("slots_out", [NEXP * SLOTS, D], F32, kind="Internal").ap()

    def C(name, a=0, b=None):
        lo, hi = const_at[name]
        return const[:, lo + a:hi if b is None else lo + b]

    def S(name, a=0, b=None):
        lo, hi = small_at[name]
        return small[:, lo + a:hi if b is None else lo + b]

    def region(lo, n):
        return area[:, lo:lo + n]

    pe = Queue(sem("tensor_done"), False)
    dve = Queue(sem("vector_done"), True)
    act = Queue(sem("scalar_done"), True)
    pool = Queue(sem("pool_done"), True)
    sp = Queue(sem("sync_done"), False)
    block_loaded = [sem(f"block_loaded{i}") for i in range(RING)]

    def tt(q, out, a, b, op, after=(), free=False):
        return q.do(lambda e: e.tensor_tensor(out, a, b, op), after, free)

    def ts(q, out, a, s1, op0, s2=None, op1=None, after=(), free=False):
        if op1 is None:
            return q.do(lambda e: e.tensor_scalar(out, a, s1, None, op0), after, free)
        return q.do(lambda e: e.tensor_scalar(out, a, s1, s2, op0, op1), after, free)

    def stt(out, a, s, b, op0, op1, after=(), free=False):
        return dve.do(lambda e: e.scalar_tensor_tensor(out, a, s, b, op0, op1), after, free)

    def activate(out, a, func, scale=1.0, bias=0.0, accum=None, after=(), free=False):
        return act.do(lambda e: e.activation(out, a, func, bias=bias, scale=scale, accum_out=accum), after, free)

    def copy(q, out, a, after=(), free=False):
        if q is act:
            return activate(out, a, ACT.Copy, after=after, free=free)
        return q.do(lambda e: e.tensor_copy(out, a), after, free)

    def reciprocal(out, a, after=()):
        return dve.do(lambda e: e.reciprocal(out, a), after)

    def reduce(out, a, op, after=()):
        return dve.do(lambda e: e.tensor_reduce(out, a, AX.X, op), after)

    def scan(out, rate, a, after=(), free=False):
        return dve.do(lambda e: e.tensor_tensor_scan(out, rate, a, 0.0, ALU.mult, ALU.add), after, free)

    def memset(ap, value, after=()):
        return dve.do(lambda e: e.memset(ap, value), after)

    def top_eight(out, a):
        return dve.do(lambda e: e.max(out, a))

    def replace_eight(a, values, by):
        return dve.do(lambda e: e.match_replace(a, values, a, by))

    def where_eight(out, values, a):
        return dve.do(lambda e: e.max_index(out, values, a))

    def load(q, name, out, src, after=()):
        return q.dma(lambda e: e.dma_start(out, src), sem(name), 16, after)

    plan = weight_plan()
    places, n_blocks = place_pieces(plan)
    stream = {"next": 0, "block": -1}

    def load_block(b, after=()):
        slot = b % RING
        sp.dma(lambda e: e.dma_start(ring[:, slot * BLOCK:(slot + 1) * BLOCK], io["weights"][b]),
               block_loaded[slot], 0, after)

    def take(piece):
        block, col = places[stream["next"]]
        stream["next"] += 1
        if block != stream["block"]:
            if stream["block"] >= 0 and stream["block"] + RING < n_blocks:
                load_block(stream["block"] + RING, [pe.last()])
            stream["block"] = block
            pe.wait((block_loaded[block % RING], 16 * (block // RING + 1)))
        at = (block % RING) * BLOCK + col
        return ring[:, at:at + width_of(piece)]

    def matmul(out, lhsT, rhs, start, stop, after=()):
        pe.quiet(lambda e: e.matmul(out, lhsT, rhs, start=start, stop=stop), after)

    def accumulate(out, lhsT, rhs):
        pe.quiet(lambda e: e.matmul(out, lhsT, rhs, start=False, stop=True, skip_group_check=True))

    def transpose(out, in_, after=()):
        n = in_.shape[0]
        pe.quiet(lambda e: e.transpose(out, in_, C("ident")[0:n, 0:n]), after)

    def product(pieces, x, after=(), bank=None, start=True, stop=True, n=T):
        if bank is None:
            bank, free = banks.take()
            pe.wait(*free)
        pe.wait(*after)
        for k, piece in enumerate(pieces):
            w = take(piece)
            matmul(bank.ap[0:w.shape[1], 0:n], w, x[k], start and k == 0, stop and k == len(pieces) - 1)
        return bank, pe.last()

    def lead(name, x, ready):
        group = plan[name][:LEAD[name]]
        out = []
        for _ in group:
            bank, free = banks.take()
            pe.wait(*free)
            out.append(bank)
        for k in range(len(x)):
            for bank, pieces in zip(out, group):
                matmul(bank.ap[0:width_of(pieces[k]), :], take(pieces[k]), x[k], k == 0, k == len(x) - 1, [ready[k]])
        done = pe.last()
        return [(bank, done) for bank in out]

    def tokens_product(pieces, x, width, after=()):
        out = []
        for _ in range(TB):
            bank, free = banks.take()
            pe.wait(*free)
            out.append(bank)
        pe.wait(*after)
        for k, piece in enumerate(pieces):
            w = take(piece)
            for b in range(TB):
                matmul(out[b].ap[:, 0:width], x[k][:, b * P:(b + 1) * P], w, k == 0, k == len(pieces) - 1)
        return out, pe.last()

    for b in range(RING):
        load_block(b)
    x_loaded = load(act, "x_loaded", buf_a, io["x"].rearrange("(c p) t -> p c t", p=P))
    const_loaded = load(act, "const_loaded", const[:, :], io["const"])
    small_loaded = load(act, "small_loaded", small[:, :], io["small"])

    sums, square_sums = norm[:, 0:T], norm[:, T:2 * T]
    squares = Ring([norm[:, (2 + i) * T:(3 + i) * T] for i in range(2)])
    one_over_d = C("mean")
    summed = {}

    def add_to_sums(r, m, ready, plain=True):
        if m == 0:
            before = summed.get("read", [])
            activate(square_sums, r[:, 0, :], ACT.Square, after=[ready] + before)
            pool.wait(*before)
            summed["first"] = [ready]
            return
        slot, free = squares.take()
        a = activate(slot.ap, r[:, m, :], ACT.Square, after=[ready] + free)
        if m == KD - 1:
            summed["chunk"], summed["square"] = (r[:, m, :], ready), (slot, a)
            return
        if plain:
            tt(pool, sums, r[:, 0, :] if m == 1 else sums, r[:, m, :], ALU.add, after=[ready] + summed["first"])
        g = tt(pool, square_sums, square_sums, slot.ap, ALU.add, after=[a], free=plain)
        slot.free = [g]
        summed["last"] = g

    def total(x, last, ready):
        bank, free = banks.take()
        matmul(bank.ap, one_over_d, x, True, False, free + [summed["last"], const_loaded])
        matmul(bank.ap, one_over_d, last, False, True, [ready])
        return bank, pe.last()

    def total_squares():
        slot, ready = summed["square"]
        bank, done = total(square_sums, slot.ap, ready)
        slot.free = [done]
        return bank, done

    def layer_norm(src, ready, dst, g, b, meanwhile=()):
        mean, m_done = total(sums, *summed["chunk"])
        square, s_done = total_squares()
        shift, scale = sums, square_sums
        v = copy(dve, shift, mean.ap, [m_done, s_done])
        mean.free = [v]
        tt(dve, scale, shift, shift, ALU.mult)
        v = stt(scale, scale, -1.0, square.ap, ALU.mult, ALU.add)
        square.free = [v]
        v = ts(dve, scale, scale, 0.0, ALU.max, LN_EPS, ALU.add)
        a = activate(scale, scale, ACT.Sqrt, after=[v])
        for step in meanwhile[:1]:
            step()
        v = reciprocal(scale, scale, [a])
        c = tt(dve, shift, shift, scale, ALU.mult)
        out, reads = [], []
        for k in range(KD):
            q = pool if k in (2, 5) else dve
            tt(q, src[:, k, :], src[:, k, :], scale, ALU.mult, after=[v, c, ready[k]], free=q is dve and k > 0)
            n = tt(q, src[:, k, :], src[:, k, :], shift, ALU.subtract)
            reads.append(n)
            out.append(n)
        for k in (0, 1, 3, 4, 2, 6, 7, 5):
            out[k] = activate(dst[:, k, :], src[:, k, :], ACT.Identity, scale=S("ln_g", g + k, g + k + 1),
                              bias=S("ln_b", b + k, b + k + 1), after=[out[k], small_loaded], free=True)
        for step in meanwhile[1:]:
            step()
        summed["read"] = reads
        return out

    def rms_norm(src, ready, dst, g):
        square, done = total_squares()
        scale = square_sums
        v = ts(dve, scale, square.ap, RMS_EPS, ALU.add, after=[done])
        square.free = [v]
        a = activate(scale, scale, ACT.Sqrt, after=[v])
        r = reciprocal(scale, scale, [a])
        out = [stt(dst[:, k, :], src[:, k, :], S(g, k, k + 1), scale, ALU.mult, ALU.mult,
                   after=[r, small_loaded, ready[k]], free=k > 0) for k in range(KD)]
        summed["read"] = out
        return out

    def ffn(name, h, ready, r, aside=()):
        aside = list(aside)
        hidden = chunks(region(0, KF * T), KF)
        x = [h[:, k, :] for k in range(KD)]
        written, scaled = [], []
        begun = lead(name + "_up", x, ready) if name + "_up" in LEAD else []
        for m in range(KF):
            gate, g_done = begun.pop(0) if begun else product(plan[name + "_up"][2 * m], x, ready)
            up, u_done = begun.pop(0) if begun else product(plan[name + "_up"][2 * m + 1], x)
            a = activate(hidden[:, m, :], gate.ap, ACT.Silu, after=[g_done])
            gate.free = [a]
            v = tt(dve, hidden[:, m, :], hidden[:, m, :], up.ap, ALU.mult, after=[a, u_done])
            up.free = [v]
            written.append(v)
            if m >= KF - KD:
                k = m - (KF - KD)
                scaled.append(activate(r[:, k, :], h[:, k, :], ACT.Copy, scale=ALPHA, after=ready, free=True))
            if aside:
                aside.pop(0)()
        out = []
        for m in range(KD):
            bank, done = product(plan[name + "_down"][m], [hidden[:, k, :] for k in range(KF)], written)
            out.append(stt(r[:, m, :], bank.ap, 0.5, r[:, m, :], ALU.mult, ALU.add, after=[done, scaled[m]]))
            bank.free = [out[-1]]
            add_to_sums(r, m, out[-1])
            if aside:
                aside.pop(0)()
        assert not aside
        return out

    def ple_proj(layer):
        pt, proj = chunks(region(BASE, 2 * T), 2), chunks(region(BASE + 2 * T, KD * T), KD)
        loaded, out = [], []

        def load_p():
            begin = [pe.last()] + [(q.done, q.count) for q in (dve, act, pool)]
            loaded.append(load(act, f"p_loaded{layer}", pt, io["p"][layer].rearrange("(c p) t -> p c t", p=P), begin))

        def half(lo):
            for m in range(lo, lo + KD // 2):
                bank, done = product(plan[f"ple{layer}_proj"][m], [pt[:, k, :] for k in range(2)], loaded)
                out.append(copy(act, proj[:, m, :], bank.ap, [done]))
                bank.free = [out[-1]]

        return load_p, [lambda: half(0), lambda: half(KD // 2)], proj, out

    def ple(layer, h, ready, r, proj, proj_ready, squares_too):
        gates = Ring([region((10 + i) * T, T) for i in range(2)])
        x = [h[:, k, :] for k in range(KD)]
        out, begun = [], lead(f"ple{layer}_gate", x, ready)
        for m in range(KD):
            gate, g_done = begun.pop(0) if begun else product(plan[f"ple{layer}_gate"][m], x)
            s, free = gates.take()
            a = activate(s.ap, gate.ap, ACT.Sigmoid, after=free + [g_done])
            gate.free = [a]
            tt(dve, s.ap, s.ap, proj[:, m, :], ALU.mult, after=[a, proj_ready[m]])
            v = tt(dve, r[:, m, :], s.ap, h[:, m, :], ALU.add, after=[ready[m]])
            s.free = [v]
            out.append(v)
            if squares_too:
                add_to_sums(r, m, v, plain=False)
        return out

    def reduce_angle(r, k, x):
        ts(dve, k, x, 1.0 / (2 * PI), ALU.mult, ROUND, ALU.add)
        ts(dve, k, k, -ROUND, ALU.add)
        stt(r, k, -TWO_PI_1, x, ALU.mult, ALU.add)
        stt(r, k, -TWO_PI_2, r, ALU.mult, ALU.add)
        return stt(r, k, -TWO_PI_3, r, ALU.mult, ALU.add)

    def sin_cos(sin, cos, r, half, double, after=()):
        a = activate(sin, r, ACT.Sin, scale=half, after=after)
        v = stt(cos, r, -1.0, r, ALU.mult, ALU.max, after=after)
        v = ts(dve, cos, cos, -half, ALU.mult, PI / 2, ALU.add)
        c = activate(r, cos, ACT.Sin, after=[v, a])
        v = tt(dve, cos, sin, sin, ALU.mult, after=[c])
        v = ts(dve, cos, cos, -2.0, ALU.mult, 1.0, ALU.add)
        return stt(sin, sin, double, r, ALU.mult, ALU.mult, after=[c])

    BASE = KF * T
    b_turned = region(BASE, STEPS * 2 * T).rearrange("p (k r c s) -> p k r c s", k=STEPS, r=2, c=KC)
    c_power = region(BASE + 8 * T, STEPS * 2 * T).rearrange("p (k r q c) -> p k r q c", k=STEPS, r=2, q=PAIRS)
    short = region(BASE + 16 * T, STEPS * T).rearrange("p (n c o) -> p n c o", n=STEPS, c=KC)
    top = BASE + 20 * T
    b_re, b_im, c_re, nc_im, fb_re, fb_im = (region(top + i * T, T).rearrange("p (q c) -> p q c", q=PAIRS) for i in range(6))
    st = [stat[:, i * PAIRS:(i + 1) * PAIRS] for i in range(32)]
    mag, f_re, f_im, turn_hi, turn_lo, t_small = st[0:6]
    power = [(st[14 + 2 * k], st[15 + 2 * k]) for k in range(STEPS + 1)]
    factor = [(st[24 + 2 * k], st[25 + 2 * k]) for k in range(STEPS)]
    s5 = {}

    def multiply(out, x, y, tmp):
        tt(dve, out[0], x[0], y[0], ALU.mult)
        tt(dve, tmp, x[1], y[1], ALU.mult)
        tt(dve, out[0], out[0], tmp, ALU.subtract)
        tt(dve, out[1], x[0], y[1], ALU.mult)
        tt(dve, tmp, x[1], y[0], ALU.mult)
        return tt(dve, out[1], out[1], tmp, ALU.add)

    def s5_factors():
        dt, lr, x, r, k, sn, cs, den = st[6:14]
        t = t_small
        w = [const_loaded, small_loaded]
        a = activate(dt, S("log_dt"), ACT.Exp, after=w)
        ts(dve, lr, S("lam_re"), -1e-4, ALU.min, after=w)
        tt(dve, x, S("lam_im"), dt, ALU.mult, after=[a])
        tt(dve, mag, lr, dt, ALU.mult)
        v = reduce_angle(r, k, x)
        a = activate(mag, mag, ACT.Exp, after=[v])
        ts(dve, turn_hi, r, 1.0 / (2 * PI), ALU.mult)
        ts(dve, turn_lo, turn_hi, ROUND13, ALU.add)
        ts(dve, k, turn_lo, -ROUND13, ALU.add)
        tt(dve, turn_lo, turn_hi, k, ALU.subtract)
        v = copy(dve, turn_hi, k)
        sin_cos(sn, cs, r, 0.5, 2.0, [v])
        tt(dve, power[1][0], cs, mag, ALU.mult, after=[a])
        tt(dve, power[1][1], sn, mag, ALU.mult)
        tt(dve, t, mag, mag, ALU.mult)
        tt(dve, mag, t, t, ALU.mult)
        for n in range(2, STEPS + 1):
            multiply(power[n], power[n - 1], power[1], t)
        ts(dve, cs, power[1][0], -1.0, ALU.add)
        tt(dve, den, lr, lr, ALU.mult)
        tt(dve, t, S("lam_im"), S("lam_im"), ALU.mult)
        tt(dve, den, den, t, ALU.add)
        reciprocal(den, den)
        tt(dve, f_re, cs, lr, ALU.mult)
        tt(dve, t, power[1][1], S("lam_im"), ALU.mult)
        tt(dve, f_re, f_re, t, ALU.add)
        tt(dve, f_re, f_re, den, ALU.mult)
        tt(dve, f_im, power[1][1], lr, ALU.mult)
        tt(dve, t, cs, S("lam_im"), ALU.mult)
        tt(dve, f_im, f_im, t, ALU.subtract)
        tt(dve, f_im, f_im, den, ALU.mult)
        copy(dve, factor[3][0], f_re)
        copy(dve, factor[3][1], f_im)
        for k in range(STEPS - 1):
            s5["factors"] = multiply(factor[k], power[3 - k], (f_re, f_im), t)
        s5["loaded"] = [load(act, f"s5_{n}_loaded", dst, io["s5_" + n])
                        for n, dst in (("b_re", b_re), ("b_im", b_im), ("c_re", c_re), ("c_im", nc_im))]
        s5["c"] = ts(dve, nc_im, nc_im, -1.0, ALU.mult, after=s5["loaded"])
        memset(short, 0.0)

    def over(column):
        return column.unsqueeze(2).to_broadcast([P, PAIRS, PCH])

    s5["operands"] = []

    def s5_b(k):
        gr, gi = factor[k]
        tmp = c_power[:, 3, 1]
        after = s5.get("fb_free", [])
        tt(dve, fb_re, b_re, over(gr), ALU.mult, after=s5["loaded"] + after)
        tt(dve, tmp, b_im, over(gi), ALU.mult)
        tt(dve, fb_re, fb_re, tmp, ALU.subtract)
        tt(dve, fb_im, b_im, over(gr), ALU.mult)
        tt(dve, tmp, b_re, over(gi), ALU.mult)
        s5["fb"] = tt(dve, fb_im, fb_im, tmp, ALU.add)

    def s5_turn_b(k):
        for r, src in ((0, fb_re), (1, fb_im)):
            bank, free = banks.take()
            pe.wait(*free)
            for ct in range(KC):
                transpose(bank.ap[:, ct * P:(ct + 1) * P], src[:, ct * PPC:(ct + 1) * PPC, :].rearrange("p q c -> p (q c)"),
                          [s5["fb"]])
            a = copy(act, b_turned[:, k, r].rearrange("p c s -> p (c s)"), bank.ap, [pe.last()])
            bank.free = [a]
            s5["operands"].append(a)
        bank, free = banks.take()
        pe.wait(*free)
        for ct in range(KC):
            for r, (f, c) in enumerate(((fb_re, c_re), (fb_im, nc_im))):
                pairs = slice(ct * PPC, (ct + 1) * PPC)
                matmul(bank.ap[:, ct * P:(ct + 1) * P], f[:, pairs, :].rearrange("p q c -> p (q c)"),
                       c[:, pairs, :].rearrange("p q c -> p (q c)"), r == 0, r == 1, [s5["c"]])
        done = pe.last()
        s5["fb_free"] = [done]
        for i in range(PPC):
            rows = slice(i * PCH, (i + 1) * PCH)
            a = activate(short[rows, STEPS - 1 - k, :, rows], chunks(bank.ap, KC)[rows, :, rows], ACT.Copy, after=[done, s5["fb"]])
        bank.free = [a]
        s5["operands"].append(a)

    def s5_c(k):
        ar, ai = power[k + 1]
        re, im = c_power[:, k, 0], c_power[:, k, 1]
        tmp = fb_re
        tt(dve, re, c_re, over(ar), ALU.mult, after=s5["fb_free"])
        tt(dve, im, nc_im, over(ai), ALU.mult)
        tt(dve, re, re, im, ALU.add)
        tt(dve, im, nc_im, over(ar), ALU.mult)
        tt(dve, tmp, c_re, over(ai), ALU.mult)
        s5["operands"].append(tt(dve, im, im, tmp, ALU.subtract))

    table_stored = [sem(f"table_stored{i}") for i in range(PPC)]
    s5["tables"] = []

    def s5_turn(i):
        both = region(top, 2 * T)
        cos, sin, r = region(top, T), region(top + T, T), region(top + 2 * T, T)
        steps = C("steps")[:, 0:T:STEPS]
        for ct in range(KC):
            q = ct * PPC + i
            ts(dve, chunks(r, KC)[:, ct, :], steps, turn_hi[:, q:q + 1], ALU.mult, after=s5["operands"] + s5["tables"])
        ts(dve, cos, r, ROUND, ALU.add, -ROUND, ALU.add)
        tt(dve, r, r, cos, ALU.subtract)
        for ct in range(KC):
            q = ct * PPC + i
            part = chunks(r, KC)[:, ct, :]
            v = stt(part, steps, turn_lo[:, q:q + 1], part, ALU.mult, ALU.add)
        v = sin_cos(sin, cos, r, PI, 2.0, [v])
        s5["tables"].append(act.dma(lambda e: e.dma_start(tables_dram[i], both), table_stored[i], 16, [v]))

    def mixer_ab(h, ready, r):
        hc = chunks(region(0, KC * T), KC)
        u = chunks(region(KC * T, KC * T), KC)
        y = chunks(region(2 * KC * T, KC * T), KC)
        gb = chunks(region(3 * KC * T, KC * T), KC)
        pad = region(4 * KC * T, T + 2)
        x = [h[:, k, :] for k in range(KD)]
        hc_done, gb_done = [], []
        zeroed = memset(pad[:, 0:2], 0.0, [pe.last()])
        begun = lead("ab_in", x, ready)
        for m in range(KC):
            bank, done = begun[m]
            hc_done.append(copy(act, hc[:, m, :], bank.ap, [done]))
            bank.free = [hc_done[-1]]
        for m in range(KC):
            bank, done = product(plan["ab_in"][KC + m], x)
            gb_done.append(copy(act, gb[:, m, :], bank.ap, [done]))
            bank.free = [gb_done[-1]]
        conv = []
        for m in range(KC):
            bank, done = product(plan["ab_in"][2 * KC + m], x)
            v = tt(dve, pad[:, 2:T + 2], hc[:, m, :], bank.ap, ALU.mult, after=[done, hc_done[m], zeroed])
            bank.free = [v]
            w = [S("conv_w", j * KC + m, j * KC + m + 1) for j in range(3)]
            ts(dve, hc[:, m, :], pad[:, 0:T], w[0], ALU.mult)
            stt(hc[:, m, :], pad[:, 1:T + 1], w[1], hc[:, m, :], ALU.mult, ALU.add)
            stt(hc[:, m, :], pad[:, 2:T + 2], w[2], hc[:, m, :], ALU.mult, ALU.add)
            conv.append(tt(dve, hc[:, m, :], hc[:, m, :], gb[:, m, :], ALU.mult, after=[gb_done[m]]))
        u_done = []
        for m in range(KC):
            bank, done = product(plan["ab_in"][3 * KC + m], x)
            u_done.append(copy(act, u[:, m, :], bank.ap, [done]))
            bank.free = [u_done[-1]]
        spare = 3 * KC * T
        turn = Ring([region(spare, 2 * T), region(spare + 2 * T, 2 * T)])
        turn_sems = [sem("turn_loaded0"), sem("turn_loaded1")]
        sets = Ring([region(4 * KC * T, 4 * T), region(2 * KC * T, 4 * T)])
        ends = Ring([region(top + n * 2 * KC * (NB + 1), 2 * KC * (NB + 1)).rearrange("p (r c j) -> p r c j", r=2, c=KC)
                     for n in range(2)])
        begun_at = conv + s5["tables"]
        for slot in ends.slots:
            zero = memset(slot.ap[:, :, :, 0:1], 0.0, begun_at)
        turns = []
        for i in range(2):
            tslot, free = turn.take()
            turns.append((tslot, act.dma(lambda e, i=i, tslot=tslot: e.dma_start(tslot.ap, tables_dram[i]),
                                         turn_sems[i], 16, free + begun_at)))
        inputs = []

        def to_ends(i):
            rows = slice(i * PCH, (i + 1) * PCH)
            got = []
            for part in range(2):
                bank, free = banks.take()
                pe.wait(*free)
                for ct in range(KC):
                    for k in range(STEPS):
                        matmul(bank.ap[:, ct * NB:(ct + 1) * NB], b_turned[rows, k, part, ct, :], u[rows, ct, k:T:STEPS],
                               k == 0, k == STEPS - 1, u_done + s5["operands"])
                got.append((bank, pe.last()))
            inputs.append(got)

        to_ends(0)
        to_ends(1)
        y_banks = []
        for ct in range(KC):
            bank, free = banks.take()
            pe.wait(*free)
            out, x_in = (a.rearrange("p (j k) -> p j k", k=STEPS) for a in (bank.ap, u[:, ct, :]))
            for n in range(STEPS):
                if n == 0:
                    matmul(bank.ap, short[:, n, ct, :], u[:, ct, :], True, True)
                else:
                    accumulate(out[:, :, n:STEPS], short[:, n, ct, :], x_in[:, :, 0:STEPS - n])
            y_banks.append(bank)
        for i in range(PPC):
            tslot, loaded = turns[i]
            cos, sin = tslot.ap[:, 0:T], tslot.ap[:, T:2 * T]
            (v_re, re_done), (v_im, im_done) = inputs[i]
            wslot, free = sets.take()
            w_re, w_im, z_re, z_im = (wslot.ap[:, n * T:(n + 1) * T] for n in range(4))
            tt(dve, w_re, cos, v_re.ap, ALU.mult, after=[loaded, re_done, im_done] + free)
            tt(dve, z_re, sin, v_im.ap, ALU.mult, free=True)
            tt(dve, w_im, cos, v_im.ap, ALU.mult, free=True)
            v = tt(dve, z_im, sin, v_re.ap, ALU.mult, free=True)
            v_re.free = v_im.free = [v]
            tt(dve, w_re, w_re, z_re, ALU.add)
            tt(dve, w_im, w_im, z_im, ALU.subtract, free=True)
            first = True
            for z, w in ((z_re, w_re), (z_im, w_im)):
                for ct in range(KC):
                    q = ct * PPC + i
                    rate = mag[:, q:q + 1].to_broadcast([P, NB])
                    v = scan(z[:, ct * NB:(ct + 1) * NB], rate, w[:, ct * NB:(ct + 1) * NB], (), not first)
                    first = False
            eslot, free = ends.take()
            e_re, e_im = eslot.ap[:, 0, :, 1:NB + 1], eslot.ap[:, 1, :, 1:NB + 1]
            g0 = tt(pool, w_re, z_re, sin, ALU.mult, after=[v])
            tt(pool, e_im, chunks(z_im, KC), chunks(cos, KC), ALU.mult, after=free + [zero], free=True)
            g = tt(pool, e_im, e_im, chunks(w_re, KC), ALU.add)
            tt(dve, w_im, z_im, sin, ALU.mult)
            tt(dve, e_re, chunks(z_re, KC), chunks(cos, KC), ALU.mult, after=free, free=True)
            v = tt(dve, e_re, e_re, chunks(w_im, KC), ALU.subtract)
            wslot.free = tslot.free = [v, g]
            if i + 2 < PPC:
                tslot, free = turn.take()
                turns.append((tslot, act.dma(lambda e, i=i, tslot=tslot: e.dma_start(tslot.ap, tables_dram[i + 2]),
                                             turn_sems[i % 2], 32, free)))
                to_ends(i + 2)
            rows = slice(i * PCH, (i + 1) * PCH)
            for ct in range(KC):
                out = y_banks[ct].ap.rearrange("p (j k) -> p j k", k=STEPS)[rows]
                for k in range(STEPS):
                    for part in range(2):
                        pe.wait(v, g)
                        accumulate(out[:, :, k], c_power[:, k, part, ct * PPC + i, :], eslot.ap[:, part, ct, 0:NB])
            eslot.free = [pe.last()]
        y_done = []
        for ct in range(KC):
            v = stt(y[:, ct, :], u[:, ct, :], S("s5_d", ct, ct + 1), y_banks[ct].ap, ALU.mult, ALU.add, after=[pe.last()])
            y_banks[ct].free = [v]
            y_done.append(v)
        z_done = []
        c2 = 2.0 * float(np.sqrt(2.0 / np.pi))
        for m in range(KC):
            t1, t2 = gb[:, 0, :], gb[:, 1, :]
            tt(dve, t1, y[:, m, :], y[:, m, :], ALU.mult)
            ts(dve, t1, t1, 0.044715, ALU.mult, 1.0, ALU.add)
            v = tt(dve, t1, t1, y[:, m, :], ALU.mult)
            a = activate(t2, t1, ACT.Sigmoid, scale=c2, after=[v])
            z_done.append(tt(dve, y[:, m, :], y[:, m, :], t2, ALU.mult, after=[a]))
        o_done = []
        for m in range(KC):
            bank, done = product(plan["glu"][m], [y[:, k, :] for k in range(KC)], z_done)
            a = activate(gb[:, 2 + m % 2, :], bank.ap, ACT.Sigmoid, bias=S("b_glu", m, m + 1), after=[done] + z_done + o_done)
            bank.free = [a]
            o_done.append(tt(dve, u[:, m, :], y[:, m, :], gb[:, 2 + m % 2, :], ALU.mult, after=[a]))
        cat = [hc[:, k, :] for k in range(KC)] + [u[:, k, :] for k in range(KC)]
        return residual("ab_out", cat, conv + o_done, h, r)

    def residual(name, x, x_ready, h, r):
        out = []
        for m in range(KD):
            bank, done = product(plan[name][m], x, x_ready)
            v = stt(r[:, m, :], h[:, m, :], ALPHA, bank.ap, ALU.mult, ALU.add, after=[done] + x_ready)
            bank.free = [v]
            out.append(v)
            add_to_sums(r, m, v)
        return out

    def attention(items, rings, turned, stats, begin, evacuate):
        state = {}

        def scores(i):
            item = items[i]
            got = []
            for group in item["groups"]:
                bank, free = banks.take()
                pe.wait(*free, *item["ready"])
                for br in group:
                    matmul(bank.ap[:, br["at"]:br["at"] + br["n"]], br["q"], br["k"], True, True)
                got.append((bank, pe.last()))
            state[i] = got

        def logits(i):
            item = items[i]
            st, sfree = stats.take()
            n_br = sum(len(g) for g in item["groups"])
            m, z, w = st.ap[:, 0:n_br], st.ap[:, 4:4 + n_br], st.ap[:, 8:9]
            slots, todo, j = [], [], 0
            dve.wait(*sfree, *begin)
            for g, (group, (bank, done)) in enumerate(zip(item["groups"], state[i])):
                slot, free = rings[item["rings"][g]].take()
                for br in group:
                    cols = slice(br["at"], br["at"] + br["n"])
                    l = slot.ap[:, cols]
                    if br["slope"] is None:
                        v = tt(dve, l, br["far"], bank.ap[:, cols], ALU.add, after=[done] + free, free=True)
                    else:
                        v = stt(l, br["far"], br["slope"], bank.ap[:, cols], ALU.mult, ALU.add, after=[done] + free, free=True)
                    todo.append((l, j))
                    j += 1
                bank.free = [v]
                slots.append(slot)
            for n, (l, j) in enumerate(todo):
                out = m[:, j:j + 1]
                dve.do(lambda e, out=out, l=l: e.tensor_reduce(out, l, AX.X, ALU.max), (), n > 0)
            if item["sink"] is not None:
                ts(dve, m, m, item["sink"], ALU.max)
            v = ts(dve, m, m, HELD, ALU.max, -item["scale"], ALU.mult)
            act.wait(v)
            if item["sink"] is not None:
                activate(w, item["sink"], ACT.Exp, bias=m, free=True)
            for l, j in todo:
                a = activate(l, l, ACT.Exp, scale=item["scale"], bias=m[:, j:j + 1], accum=z[:, j:j + 1], free=True)
            state[i] = (slots, todo, st, a)

        def weights(i):
            item = items[i]
            slots, todo, st, a = state[i]
            n_br = len(todo)
            z, w = st.ap[:, 4:4 + n_br], st.ap[:, 8:9]
            dve.wait(a)
            if item["sink"] is not None:
                tt(dve, z, z, w, ALU.add, free=True)
            else:
                ts(dve, z, z, 1e-30, ALU.max, free=True)
            v = reciprocal(z, z)
            if item["z"] is not None:
                v = tt(dve, z, z, item["z"], ALU.mult)
            pool.wait(v)
            for l, j in todo:
                g = ts(pool, l, l, z[:, j:j + 1], ALU.mult, free=True)
            st.free = [g]
            state[i] = (slots, g)

        o_bank = {}

        def turn(i):
            item = items[i]
            slots, ready = state[i]
            pts = []
            for g, (group, slot) in enumerate(zip(item["groups"], slots)):
                pt, free = turned.take()
                bank, bfree = banks.take()
                pe.wait(*bfree, ready)
                lo = min(br["at"] for br in group)
                hi = max(br["at"] + br["width"] for br in group)
                for c in range(lo, hi, P):
                    transpose(bank.ap[:, c:c + P], slot.ap[:, c:c + P])
                slot.free = [pe.last()]
                a = copy(dve if (g + i) % 2 else act, pt.ap[:, lo:hi], bank.ap[:, lo:hi], [pe.last()] + free + begin, free=True)
                bank.free = [a]
                pts.append((group, pt, a))
            state[i] = pts

        def attend(i):
            item = items[i]
            pts = state.pop(i)
            if item["b"] == 0:
                o_bank[0], free = banks.take()
                pe.wait(*free)
            rows, cols = item["rows"], slice(item["b"] * P, (item["b"] + 1) * P)
            steps = [(w, pt.ap[:, br["at"] + c * P:br["at"] + (c + 1) * P], a)
                     for group, pt, a in pts for br in group for c, w in enumerate(br["values"])]
            for n, (w, p, a) in enumerate(steps):
                matmul(o_bank[0].ap[rows, cols], w, p, n == 0, n == len(steps) - 1, [a])
            for _, pt, _ in pts:
                pt.free = [pe.last()]
            if item["b"] == TB - 1:
                o_bank[0].free = [evacuate(item, o_bank[0].ap[rows, :], pe.last())]

        for i in range(-1, len(items) + 3):
            if 0 <= i + 1 < len(items):
                scores(i + 1)
            if 0 <= i < len(items):
                logits(i)
            if 0 <= i - 1 < len(items):
                weights(i - 1)
            if 0 <= i - 2 < len(items):
                turn(i - 2)
            if 0 <= i - 3 < len(items):
                attend(i - 3)

    def mixer_c(h, ready, r):
        at = [0]

        def get(n):
            at[0] += n
            assert at[0] <= 24576
            return region(at[0] - n, n)

        x = [h[:, k, :] for k in range(KD)]
        qT, kT = chunks(get(HEADS * T), HEADS), chunks(get(KVH * T), KVH)
        qi, ki = chunks(get(4 * T), 4), get(T)
        v_tok = chunks(get(TB * 256), TB)
        wi = chunks(get(TB * IH), TB)
        bias = [get((b + 1) * P) for b in range(TB)]
        rope = {n: (get(T), get(T)) for n in "ai"}
        raws = Ring([get(T) for _ in range(3)])
        score = [None] + [get((b + 1) * P) for b in range(1, TB)]
        ang = get(T)
        relus = Ring([get(T) for _ in range(3)])
        begin = [pe.last()]
        pos_i, kk = raws.slots[0].ap, relus.slots[0].ap
        pos_loaded = load(act, "pos_loaded", pos_i.bitcast(I32), io["positions"], begin)
        pos = relus.slots[1].ap
        copy(dve, pos, pos_i.bitcast(I32), [pos_loaded] + begin)
        rope_ready = []
        for n in "ai":
            cos, sin = rope[n]
            ts(dve, ang, pos, C(f"inv_{n}"), ALU.mult)
            v = reduce_angle(ang, kk, ang)
            rope_ready.append(sin_cos(sin, cos, ang, 0.5, C(f"sgn_{n}"), [v]))

        def rotated(pieces, dst, n, begun=None):
            cos, sin = rope[n]
            bank, done = begun or product(pieces, x, ready)
            slot, free = raws.take()
            a = copy(act, slot.ap, bank.ap, [done, rope_ready[0]] + free)
            bank.free = [a]
            other, free = banks.take()
            matmul(other.ap, C(f"swap_{n}"), slot.ap, True, True, free + [a])
            done = pe.last()
            tt(pool, dst, slot.ap, cos, ALU.mult, after=[a] + rope_ready)
            g = pool.last()
            v = tt(dve, slot.ap, other.ap, sin, ALU.mult, after=[done, g])
            other.free = [v]
            v = tt(dve, dst, dst, slot.ap, ALU.add)
            slot.free = [v]
            return v

        begun = lead("c_index", x, ready)
        qi_ready = [rotated(None, qi[:, m, :], "i", begun[m]) for m in range(4)]
        ki_ready = rotated(None, ki, "i", begun[4])
        outs, done = tokens_product(plan["c_weight"][0], x, IH)
        for b in range(TB):
            wi_ready = ts(dve, wi[:, b, :], outs[b].ap[:, 0:IH], float(IH ** -0.5 * ID ** -0.5), ALU.mult, after=[done])
            outs[b].free = [wi_ready]
        scored, bias_ready = [], []
        for b in range(1, TB):
            n = (b + 1) * P
            for i in range(IH):
                half = slice((i % 2) * ID, (i % 2 + 1) * ID)
                bank, free = banks.take()
                matmul(bank.ap[:, 0:n], qi[half, i // 2, b * P:(b + 1) * P], ki[half, 0:n], True, True,
                       free + qi_ready + [ki_ready])
                done = pe.last()
                slot, free = relus.take()
                a = activate(slot.ap[:, 0:n], bank.ap[:, 0:n], ACT.Relu, after=[done] + free + rope_ready)
                bank.free = [a]
                w = wi[:, b, i:i + 1]
                if i == 0:
                    v = ts(dve, score[b][:, 0:n], slot.ap[:, 0:n], w, ALU.mult, after=[a])
                else:
                    v = stt(score[b][:, 0:n], slot.ap[:, 0:n], w, score[b][:, 0:n], ALU.mult, ALU.add, after=[a])
                slot.free = [v]
        top8 = stat[:, 0:8]
        steps = []

        def far_of(b):
            return C("far_causal", T - P - b * P, T)

        def first_block():
            bias_ready.append(ts(dve, bias[0], far_of(0), -1e29, ALU.is_le, NEG, ALU.mult))

        def fill(b):
            mask = bias[b]
            ts(dve, mask, far_of(b), -1e29, ALU.is_le, CAUSAL_FILL, ALU.mult)
            tt(dve, score[b], score[b], mask, ALU.add)

        def rank(b):
            top_eight(top8, score[b])
            replace_eight(score[b], top8, TAKEN)

        def chosen(b):
            bias_ready.append(ts(dve, bias[b], score[b], -2e38, ALU.is_ge, NEG, ALU.mult))

        steps.append(first_block)
        for b in range(1, TB):
            steps += [lambda b=b: fill(b)] + [lambda b=b: rank(b)] * (TOPK // 8) + [lambda b=b: chosen(b)]
        qk_ready = []
        per = -(-len(steps) // (HEADS + KVH))
        for m in range(HEADS + KVH):
            qk_ready.append(rotated(plan["c_qk"][m], qT[:, m, :] if m < HEADS else kT[:, m - HEADS, :], "a"))
            for _ in range(per):
                if steps:
                    steps.pop(0)()
        assert not steps
        outs, done = tokens_product(plan["c_value"][0], x, 256)
        v_ready = []
        for b in range(TB):
            v_ready.append(copy(act, v_tok[:, b, :], outs[b].ap[:, 0:256], [done]))
            outs[b].free = [v_ready[-1]]
        o_ready = []

        def evacuate(item, o, done):
            o_ready.append(copy(act, qT[:, item["head"], :], o, [done], free=True))
            return o_ready[-1]

        items = []
        for hd in range(HEADS):
            kv = hd // (HEADS // KVH)
            for b in range(TB):
                n = (b + 1) * P
                branch = {"q": qT[:, hd, b * P:(b + 1) * P], "k": kT[:, kv, 0:n], "at": 0, "n": n, "width": n,
                          "far": bias[b], "slope": None,
                          "values": [v_tok[:, c, kv * HD:(kv + 1) * HD] for c in range(b + 1)]}
                items.append({"groups": [[branch]], "rings": [0], "z": None, "sink": None, "scale": float(HD ** -0.5),
                              "b": b, "rows": slice(0, P), "head": hd, "ready": qk_ready + v_ready})
        attention(items, [Ring([get(T) for _ in range(4)])], Ring([get(T) for _ in range(3)]),
                  Ring([stat[:, 16 + 16 * i:32 + 16 * i] for i in range(8)]), bias_ready + qk_ready, evacuate)
        return residual("c_out", [qT[:, k, :] for k in range(HEADS)], o_ready, h, r)

    def nsa(h, ready, r, r_ready):
        at = [0]

        def get(n):
            at[0] += n
            assert at[0] <= 24576, at[0]
            return region(at[0] - n, n)

        x = [h[:, k, :] for k in range(KD)]
        begin = [pe.last()] + r_ready
        q = chunks(get(8 * T), 8)
        keys = chunks(get(3 * T), 3)
        vals = chunks(get(TB * 384), TB)
        gate = chunks(get(TB * 24), TB)
        kc = get(NCMP + 1)
        vc = get(P)
        merge_at = at[0]
        cmp_in = [get(T) for _ in range(2)]
        blocks = chunks(get(CL * 2 * NCMP), CL)
        hid = [[get(2 * NCMP) for _ in range(2)] for _ in range(2)]
        sig = get(2 * NCMP)
        hid_ready = [[], []]
        cin = []
        begun = lead("b_compress_in", x, ready)
        for c in range(2):
            bank, done = begun[c]
            cin.append(copy(act, cmp_in[c], bank.ap, [done] + begin))
            bank.free = [cin[-1]]
        outs, done = tokens_product(plan["b_value"][0], x, 384)
        for b in range(TB):
            v_ready = copy(act, vals[:, b, :], outs[b].ap[:, 0:384], [done])
            outs[b].free = [v_ready]
        outs, done = tokens_product(plan["b_gate"][0], x, 24)
        for b in range(TB):
            gate_ready = activate(gate[:, b, :], outs[b].ap[:, 0:24], ACT.Sigmoid, after=[done])
            outs[b].free = [gate_ready]

        def compress(c):
            z = memset(blocks, 0.0, [pe.last()] + begin)
            for kv in range(2):
                half = slice(kv * BD, (kv + 1) * BD)
                for l in range(2):
                    src = cmp_in[c][half, l * CS:l * CS + NCMP * CS].rearrange("p (b l) -> p l b", l=CS)
                    dst = blocks[half, l * CS:(l + 1) * CS, kv * NCMP:(kv + 1) * NCMP]
                    pos = S("pos_k" if c == 0 else "pos_v", l * CS, (l + 1) * CS)[half, :]
                    v = tt(dve, dst, src, pos.unsqueeze(2).to_broadcast([BD, CS, NCMP]), ALU.add, after=[cin[c]])
            for m in range(2):
                bank, free = banks.take()
                pe.wait(*free)
                pieces = plan[f"b_compress_{c}"][m]
                for l in range(CL):
                    w = take(pieces[l])
                    matmul(bank.ap[:, 0:2 * NCMP], w, blocks[:, l, :], l == 0, l == CL - 1, [v])
                a = activate(hid[c][m], bank.ap[:, 0:2 * NCMP], ACT.Silu, after=[pe.last()])
                bank.free = [a]
                hid_ready[c].append(a)

        compress(0)
        k_ready = []
        for i in range(3):
            bank, done = product(plan["b_key"][i], x)
            k_ready.append(copy(act, keys[:, i, :], bank.ap, [done]))
            bank.free = [k_ready[-1]]
        compress(1)
        q_ready = []
        for j in range(8):
            bank, done = product(plan["b_query"][j], x)
            q_ready.append(activate(q[:, j, :], bank.ap, ACT.Copy, scale=float(BD ** -0.5), after=[done]))
            bank.free = [q_ready[-1]]
        bank, free = banks.take()
        for k in range(2):
            w = take(plan["b_compress_k"][0][k])
            matmul(bank.ap[:, 0:2 * NCMP], w, hid[0][k], k == 0, k == 1, free + hid_ready[0])
        done = pe.last()
        for kv in range(2):
            half = slice(kv * BD, (kv + 1) * BD)
            cmp_ready = copy(dve, kc[half, 0:NCMP], bank.ap[half, kv * NCMP:(kv + 1) * NCMP], [done])
        bank.free = [cmp_ready]
        bank, free = banks.take()
        pe.wait(*free)
        ws = [take(plan["b_compress_v"][0][k]) for k in range(2)]
        for kv in range(2):
            for k in range(2):
                matmul(bank.ap[0:NCMP, kv * BD:(kv + 1) * BD], hid[1][k][:, kv * NCMP:(kv + 1) * NCMP], ws[k],
                       k == 0, k == 1, hid_ready[1])
        memset(vc, 0.0, begin)
        vc_ready = copy(dve, vc[0:NCMP, :], bank.ap[0:NCMP, 0:P], [pe.last()])
        bank.free = [vc_ready]
        at[0] = merge_at
        freed = [pe.last(), (dve.done, dve.count), (act.done, act.count)]
        wide, packed = Ring([get(T) for _ in range(4)]), Ring([get(T) for _ in range(4)])
        turned = Ring([get(T) for _ in range(5)])
        stats = Ring([stat[:, 16 + 16 * i:32 + 16 * i] for i in range(8)])
        zeros_in = [memset(slot.ap[:, 0:P], 0.0, freed) for slot in packed.slots]
        inputs = q_ready + k_ready + [v_ready, gate_ready, cmp_ready, vc_ready]
        o_ready = []

        def evacuate(item, o, done):
            o_ready.append(copy(act, q[item["rows"], item["tile"], :], o, [done], free=True))
            return o_ready[-1]

        def keyed(name, tile, kv, b, at):
            which, back, far = {"selected": (0, TB, "far_causal"), "window": (1, 2, "far_256"),
                                "sliding": (2, 1, "far_128")}[name]
            half, head = slice(kv * BD, (kv + 1) * BD), tile % 4 + 4 * kv
            s0 = max(0, b - back)
            n = (b + 1 - s0) * P
            return {"q": q[half, tile, b * P:(b + 1) * P], "k": keys[half, which, s0 * P:s0 * P + n], "at": at, "n": n,
                    "width": n, "far": C(far, T - P - b * P + s0 * P, T),
                    "slope": float(SLOPES[head + (0 if name == "sliding" else 8)]),
                    "values": [vals[:, s0 + c, which * P + kv * BD:which * P + (kv + 1) * BD] for c in range(n // P)]}

        items = []
        for tile in range(8):
            for kv in range(2):
                half, head = slice(kv * BD, (kv + 1) * BD), tile % 4 + 4 * kv
                for b in range(TB):
                    item = {"b": b, "rows": half, "tile": tile, "scale": 1.0, "ready": inputs}
                    if tile < 4:
                        compressed = {"q": q[half, tile, b * P:(b + 1) * P], "k": kc[half, 0:NCMP], "at": 0, "n": NCMP,
                                      "width": P, "far": C("far_cmp", b * (NCMP + 1), b * (NCMP + 1) + NCMP),
                                      "slope": float(SLOPES[head + 8]), "values": [vc[:, kv * BD:(kv + 1) * BD]]}
                        item["groups"] = [[compressed, keyed("window", tile, kv, b, P)], [keyed("selected", tile, kv, b, 0)]]
                        item["rings"] = [1, 0]
                        item["z"], item["sink"] = gate[:, b, 3 * head:3 * head + 3], None
                    else:
                        item["groups"], item["rings"] = [[keyed("sliding", tile, kv, b, 0)]], [0]
                        item["z"], item["sink"] = None, S("sinks", head, head + 1)
                    items.append(item)
        attention(items, [wide, packed], turned, stats, freed + zeros_in[-1:] + inputs, evacuate)
        at[0] = 8 * T
        mix = chunks(get(KD * T), KD)
        tmp = Ring([get(2 * T) for _ in range(2)])
        done_all = [pe.last(), (act.done, act.count), (dve.done, dve.count)]
        mix_ready = []
        for m in range(KD):
            pc = plan["b_merge"][4 * m:4 * m + 4]
            ga, ga_done = product(pc[0], x)
            gb, gb_done = product(pc[1], x)
            pa, pa_done = product(pc[2], [q[:, k, :] for k in range(4)], o_ready)
            pb, pb_done = product(pc[3], [q[:, 4 + k, :] for k in range(4)])
            slot, free = tmp.take()
            t1, t2 = slot.ap[:, 0:T], slot.ap[:, T:2 * T]
            a1 = activate(t1, ga.ap, ACT.Sigmoid, after=[ga_done] + free + done_all)
            a2 = activate(t2, gb.ap, ACT.Sigmoid, after=[gb_done])
            ga.free, gb.free = [a1], [a2]
            v1 = tt(dve, t1, t1, pa.ap, ALU.mult, after=[a1, pa_done])
            v2 = tt(dve, t2, t2, pb.ap, ALU.mult, after=[a2, pb_done])
            pa.free, pb.free = [v1], [v2]
            v = tt(dve, mix[:, m, :], t1, t2, ALU.add, after=done_all)
            slot.free = [v]
            mix_ready.append(v)
        out = []
        for m in range(KD):
            bank, done = product(plan["b_out"][m], [mix[:, k, :] for k in range(KD)], mix_ready)
            v = tt(dve, r[:, m, :], r[:, m, :], bank.ap, ALU.add, after=[done])
            bank.free = [v]
            out.append(v)
            add_to_sums(r, m, v, plain=False)
        return out

    def turn_tokens(src, b, dst, ready, after, q=None):
        for half in range(2):
            bank, free = banks.take()
            pe.wait(*free)
            for k in range(4):
                transpose(bank.ap[:, k * P:(k + 1) * P], src[:, 4 * half + k, b * P:(b + 1) * P], ready)
            done = copy(q or (act if half else dve), dst[:, half * T:(half + 1) * T], bank.ap, [pe.last()] + after)
            bank.free = [done]
            yield done

    def route(h, ready, r, r_ready, xrows, xt, begin):
        x = [h[:, k, :] for k in range(KD)]
        logit = chunks(region(0, TB * 40), TB)
        one = chunks(region(160, 2 * TB * NEXP), 2 * TB)
        both = chunks(region(416, TB * NEXP), TB)
        comb = chunks(region(544, TB * NEXP), TB)
        tmp = chunks(region(672, TB * NEXP), TB)
        weight = stat[:, 64:64 + 2 * TB]
        slot = stat[:, 72:72 + 2 * TB]
        slot_i = stat[:, 80:80 + 2 * TB].bitcast(I32)
        flag = stat[:, 88:89].bitcast(I32)
        memset(region(0, TB * 40), -3e38, begin)
        outs, done = tokens_product(plan["router"][0], x, NGRP, ready)
        for b in range(TB):
            v = tt(dve, logit[:, b, 0:NGRP], outs[b].ap[:, 0:NGRP], S("b_group"), ALU.add, after=[done], free=b > 0)
            outs[b].free = [v]
        outs, done = tokens_product(plan["router"][1], x, NEXP)
        for b in range(TB):
            v = tt(dve, logit[:, b, 8:40], outs[b].ap[:, 0:NEXP], S("b_expert"), ALU.add, after=[done], free=b > 0)
            outs[b].free = [v]
        xrows_ready = [list(turn_tokens(h, b, xrows[b], ready, begin, act)) for b in range(TB)]

        def place(lo, n, dt=F32):
            return chunks(stat[:, lo:lo + TB * n].bitcast(dt), TB)

        gtop, gidx, etop, eidx = place(96, 8), place(128, 8, U32), place(160, 8), place(192, 8, U32)
        gi, ei, chosen, ge, gz = place(224, 1), place(228, 2), place(240, NGRP), place(256, NGRP), place(272, 1)
        m, e_in, w = place(276, 1), place(288, EPG), chunks(weight, TB)
        by_group = chunks(region(800, TB * NEXP), TB)

        def top_and_where(top, idx, a):
            for b in range(TB):
                dve.do(lambda e, b=b: e.max(top[:, b, :], a[:, b, :]), (), b > 0)
            for b in range(TB):
                dve.do(lambda e, b=b: e.max_index(idx[:, b, :], top[:, b, :], a[:, b, :]), (), b > 0)

        top_and_where(gtop, gidx, logit[:, :, 0:8])
        copy(dve, gi, gidx[:, :, 0:1])
        v = tt(dve, ge, logit[:, :, 0:NGRP], gtop[:, :, 0:1].to_broadcast([P, TB, NGRP]), ALU.subtract)
        a = activate(ge, ge, ACT.Exp, after=[v])
        tt(dve, chosen, C("group", 0, NGRP).unsqueeze(1).to_broadcast([P, TB, NGRP]), gi.to_broadcast([P, TB, NGRP]),
           ALU.is_equal)
        for g in range(NGRP):
            tt(dve, by_group[:, :, g * EPG:(g + 1) * EPG], logit[:, :, 8 + g * EPG:8 + (g + 1) * EPG],
               chosen[:, :, g:g + 1].to_broadcast([P, TB, EPG]), ALU.mult, free=g > 0)
        reduce(e_in, by_group.rearrange("p b (g e) -> p b e g", g=NGRP), ALU.add)
        top_and_where(etop, eidx, e_in)
        copy(dve, ei, eidx[:, :, 0:2])
        stt(ei, gi.to_broadcast([P, TB, 2]), float(EPG), ei, ALU.mult, ALU.add)
        v = tt(dve, m, etop[:, :, 1:2], etop[:, :, 0:1], ALU.subtract)
        a2 = activate(w[:, :, 1:2], m, ACT.Exp, after=[v])
        reduce(gz, ge, ALU.add, [a])
        tt(dve, one, C("expert").unsqueeze(1).to_broadcast([P, 2 * TB, NEXP]),
           stat[:, 228:228 + 2 * TB].unsqueeze(2).to_broadcast([P, 2 * TB, NEXP]), ALU.is_equal)
        pairs = one.rearrange("p (b i) e -> p b i e", i=2)
        first, second = pairs[:, :, 0, :], pairs[:, :, 1, :]
        both_ready = tt(dve, both, first, second, ALU.add)
        ts(dve, m, w[:, :, 1:2], 1.0, ALU.add, after=[a2])
        tt(dve, m, m, gz, ALU.mult)
        reciprocal(m, m)
        copy(dve, w[:, :, 0:1], m)
        tt(dve, w[:, :, 1:2], w[:, :, 1:2], m, ALU.mult)
        tt(dve, tmp, first, w[:, :, 0:1].to_broadcast([P, TB, NEXP]), ALU.mult)
        tt(dve, comb, second, w[:, :, 1:2].to_broadcast([P, TB, NEXP]), ALU.mult)
        comb_ready = tt(dve, comb, comb, tmp, ALU.add)
        bank, free = banks.take()
        pe.wait(*free)
        for b in range(TB):
            for c in range(b + 1):
                matmul(bank.ap[:, b * NEXP:(b + 1) * NEXP], C("before") if c == b else C("ones"), both[:, c, :],
                       c == 0, c == b, [both_ready])
        for c in range(TB):
            matmul(bank.ap[:, TB * NEXP:(TB + 1) * NEXP], C("ones"), both[:, c, :], c == 0, c == TB - 1)
        ranked = pe.last()
        xt_ready = [list(turn_tokens(r, b, xt[b], r_ready, begin, act)) for b in range(TB)]
        count = stat[:, 90:91]
        reduce(count, bank.ap[:, TB * NEXP:(TB + 1) * NEXP], ALU.max, [ranked])
        flagged = ts(dve, flag, count, float(SLOTS), ALU.is_gt)
        stt(tmp, C("expert").unsqueeze(1).to_broadcast([P, TB, NEXP]), float(SLOTS),
            chunks(bank.ap[:, 0:TB * NEXP], TB), ALU.mult, ALU.add)
        for each in (first, second):
            tt(dve, each, each, tmp, ALU.mult, free=each is second)
        reduce(slot, one, ALU.add)
        slotted = copy(dve, slot_i, slot)
        bank.free = [slotted]
        return comb, comb_ready, weight, slot_i, slotted, flag, flagged, xrows_ready, xt_ready

    def final_norm(b, xt, ready, gain, gain_loaded):
        square, s = region(12288, D), stat[:, 92:93]
        v = activate(square, xt, ACT.Square, accum=s, after=ready)
        v = ts(dve, s, s, 1.0 / D, ALU.mult, RMS_EPS, ALU.add, after=[v])
        a = activate(s, s, ACT.Sqrt, after=[v])
        reciprocal(s, s, [a])
        v = stt(xt, xt, s, gain, ALU.mult, ALU.mult, after=[gain_loaded])
        return [v]

    def store_out(b, xt, ready):
        return act.dma(lambda e: e.dma_start(io["out"][b * P:(b + 1) * P, :], xt), out_stored, 16 * (b + 1), ready)

    def moe_all(h, r, comb, comb_ready):
        x = [h[:, k, :] for k in range(KD)]
        combT = region(1024, T)
        bank, free = banks.take()
        pe.wait(*free)
        for b in range(TB):
            transpose(bank.ap[0:NEXP, b * P:(b + 1) * P], comb[:, b, :], [comb_ready])
        a = copy(act, combT[0:NEXP, :], bank.ap[0:NEXP, :], [pe.last()])
        bank.free = [a]
        stored = act.dma(lambda e: e.dma_start(combine_dram, combT[0:NEXP, :]), sem("combine_stored"), 16, [a])
        act.wait(stored)
        hidden = Ring([region(4 * T + i * 2 * T, 2 * T) for i in range(2)])
        wts = Ring([region(8 * T + i * T, T) for i in range(4)])
        wsems = [sem(f"combine_loaded{i}") for i in range(4)]
        out = None
        for e_ in range(NEXP):
            hslot, hfree = hidden.take()
            hid = chunks(hslot.ap, 2)
            wt, free = wts.take()
            loaded = sp.dma(lambda e, e_=e_, wt=wt: e.dma_start(wt.ap, combine_dram[e_:e_ + 1, :].to_broadcast([P, T])),
                            wsems[e_ % 4], 16 * (e_ // 4 + 1), free + [stored])
            written = []
            for m in range(2):
                gate, g_done = product(plan[f"moe{e_}_up"][2 * m], x)
                up, u_done = product(plan[f"moe{e_}_up"][2 * m + 1], x)
                a = activate(hid[:, m, :], gate.ap, ACT.Silu, after=[g_done] + hfree)
                gate.free = [a]
                v = tt(dve, hid[:, m, :], hid[:, m, :], up.ap, ALU.mult, after=[a, u_done])
                up.free = [v]
                v = tt(pool, hid[:, m, :], hid[:, m, :], wt.ap, ALU.mult, after=[v, loaded])
                written.append(v)
            wt.free = [v]
            down = [take(piece) for piece in plan[f"moe{e_}_down"][0]]
            pe.wait(*written)
            out = []
            for m in range(KD):
                bank, free = banks.take()
                pe.wait(*free)
                for k in range(2):
                    w = down[2 * k + m // 4][:, (m % 4) * P:(m % 4 + 1) * P]
                    matmul(bank.ap, w, hid[:, k, :], k == 0, k == 1)
                v = tt(dve, r[:, m, :], r[:, m, :], bank.ap, ALU.add, after=[pe.last()])
                bank.free = [v]
                out.append(v)
            hslot.free = [pe.last()]
        for b in range(TB):
            xt = region(8192 + b * D, D)
            done = list(turn_tokens(r, b, xt, out, []))
            store_out(b, xt, final_norm(b, xt, done, gain, gain_loaded))

    def moe_slots(weight, slot_i, slotted, xrows, xrows_ready, xt, xt_ready):
        scattered = sem("rows_scattered")
        for b in range(TB):
            for i in range(2):
                def scatter(e, b=b, i=i):
                    return e.indirect_dma_start(out=slots_in, out_offset=bass.IndirectOffsetOnAxis(
                        ap=slot_i[:, 2 * b + i:2 * b + i + 1], axis=0), in_=xrows[b], in_offset=None)
                rows = pool.dma(scatter, scattered, 16 * (2 * b + i + 1), xrows_ready[b] + [slotted, zero_filled])
        rows_in = Ring([region(13312 + i * D, D) for i in range(3)])
        in_sems = [sem(f"rows_in{i}") for i in range(3)]
        turned = Ring([region(16384 + i * T, T) for i in range(2)])
        hidden = Ring([region(17408 + i * 256, 2 * SLOTS) for i in range(2)])
        rows_out = Ring([region(18432 + i * D, D) for i in range(2)])
        out_sems = [sem(f"rows_out{i}") for i in range(2)]
        state = {}

        def bring(e_):
            slot, free = rows_in.take()
            loaded = sp.dma(lambda e: e.dma_start(slot.ap[0:SLOTS, :], slots_in[e_ * SLOTS:(e_ + 1) * SLOTS, :]),
                            in_sems[e_ % 3], 16 * (e_ // 3 + 1), free + [rows])
            state[e_] = (slot, loaded)

        def turn(e_):
            slot, loaded = state[e_]
            xs, free = turned.take()
            bank, bfree = banks.take()
            pe.wait(*bfree)
            for k in range(KD):
                transpose(bank.ap[:, k * SLOTS:(k + 1) * SLOTS], slot.ap[0:SLOTS, k * P:(k + 1) * P], [loaded])
            slot.free = [pe.last()]
            a = copy(act, xs.ap[:, 0:KD * SLOTS], bank.ap[:, 0:KD * SLOTS], [pe.last()] + free)
            bank.free = [a]
            state[e_] = (xs, a)

        for e_ in range(2):
            bring(e_)
        turn(0)
        stores = []
        for e_ in range(NEXP):
            if e_ + 2 < NEXP:
                bring(e_ + 2)
            xs, ready_x = state[e_]
            x = [xs.ap[:, k * SLOTS:(k + 1) * SLOTS] for k in range(KD)]
            hslot, hfree = hidden.take()
            written = []
            for m in range(2):
                gate, g_done = product(plan[f"moe{e_}_up"][2 * m], x, [ready_x], n=SLOTS)
                up, u_done = product(plan[f"moe{e_}_up"][2 * m + 1], x, n=SLOTS)
                hid = hslot.ap[:, m * SLOTS:(m + 1) * SLOTS]
                a = activate(hid, gate.ap[:, 0:SLOTS], ACT.Silu, after=[g_done] + hfree)
                gate.free = [a]
                v = tt(dve, hid, hid, up.ap[:, 0:SLOTS], ALU.mult, after=[a, u_done])
                up.free = [v]
                written.append(v)
            xs.free = [pe.last()]
            if e_ + 1 < NEXP:
                turn(e_ + 1)
            down = [take(piece) for piece in plan[f"moe{e_}_down"][0]]
            oslot, ofree = rows_out.take()
            copied = []
            for n in range(2):
                bank, free = banks.take()
                pe.wait(*free)
                for k in range(2):
                    matmul(bank.ap[0:SLOTS, :], hslot.ap[:, k * SLOTS:(k + 1) * SLOTS], down[2 * k + n],
                           k == 0, k == 1, written)
                v = copy(dve, oslot.ap[0:SLOTS, n * T:(n + 1) * T], bank.ap[0:SLOTS, :], [pe.last()] + ofree)
                bank.free = [v]
                copied.append(v)
            hslot.free = [pe.last()]
            stored = act.dma(lambda e, e_=e_, oslot=oslot: e.dma_start(slots_out[e_ * SLOTS:(e_ + 1) * SLOTS, :],
                                                                       oslot.ap[0:SLOTS, :]),
                             out_sems[e_ % 2], 16 * (e_ // 2 + 1), copied)
            oslot.free = [stored]
            stores.append(stored)
        gathered = [[sem(f"gathered{b}{i}") for i in range(2)] for b in range(TB)]
        ys = Ring([region(2048 + i * D, D) for i in range(4)])
        for b in range(TB):
            got = []
            for i in range(2):
                y, free = ys.take()

                def gather(e, b=b, i=i, y=y):
                    return e.indirect_dma_start(out=y.ap, out_offset=None, in_=slots_out,
                                                in_offset=bass.IndirectOffsetOnAxis(
                                                    ap=slot_i[:, 2 * b + i:2 * b + i + 1], axis=0))
                loaded = pool.dma(gather, gathered[b][i], 16, free + stores[-2:] + [rows])
                got.append((y, loaded))
            for i, (y, loaded) in enumerate(got):
                w = weight[:, 2 * b + i:2 * b + i + 1]
                v = stt(xt[b], y.ap, w, xt[b], ALU.mult, ALU.add, after=[loaded] + xt_ready[b])
                y.free = [v]
            store_out(b, xt[b], final_norm(b, xt[b], [v], gain, gain_loaded))

    aside = [s5_factors, lambda: s5_b(0)]
    for k in range(STEPS):
        aside.append(lambda k=k: s5_turn_b(k))
        aside.append(lambda k=k: s5_b(k + 1) if k + 1 < STEPS else None)
    for k in range(STEPS):
        aside.append(lambda k=k: s5_c(k))
    for i in range(PPC):
        aside.append(lambda i=i: s5_turn(i))
    r_ready = ffn("ffn0", buf_a, [x_loaded], buf_b, aside)
    h_ready = layer_norm(buf_b, r_ready, buf_a, 0, 0)
    r_ready = mixer_ab(buf_a, h_ready, buf_b)
    h_ready = layer_norm(buf_b, r_ready, buf_a, KD, KD)
    load_p, halves, proj, proj_ready = ple_proj(0)
    r_ready = ffn("ffn1", buf_a, h_ready, buf_b, [load_p])
    h_ready = layer_norm(buf_b, r_ready, buf_a, 2 * KD, 2 * KD, halves)
    r_ready = ple(0, buf_a, h_ready, buf_b, proj, proj_ready, False)
    zeros = region(20480, D)
    zeroed = memset(zeros, 0.0)
    slots_rows = slots_in.rearrange("(n p) d -> p n d", p=P)
    zero_filled = load(act, "zero_filled", slots_rows, zeros.unsqueeze(1).to_broadcast([P, NEXP * SLOTS // P, D]), [zeroed])
    r_ready = ffn("ffn2", buf_b, r_ready, buf_a)
    h_ready = layer_norm(buf_a, r_ready, buf_b, 3 * KD, 3 * KD)
    r_ready = mixer_c(buf_b, h_ready, buf_a)
    h_ready = layer_norm(buf_a, r_ready, buf_b, 4 * KD, 4 * KD)
    load_p, halves, proj, proj_ready = ple_proj(1)
    r_ready = ffn("ffn3", buf_b, h_ready, buf_a, [load_p])
    h_ready = layer_norm(buf_a, r_ready, buf_b, 5 * KD, 5 * KD, halves)
    r_ready = ple(1, buf_b, h_ready, buf_a, proj, proj_ready, True)
    h_ready = rms_norm(buf_a, r_ready, buf_b, "mix_g")
    r_ready = nsa(buf_b, h_ready, buf_a, r_ready)
    h_ready = rms_norm(buf_a, r_ready, buf_b, "ffn_g")
    out_stored = sem("out_stored")
    gain = region(21504, D)
    gain_loaded = load(act, "gain_loaded", gain, io["gain"], [pe.last()] + r_ready)
    xrows, xt = ([region(at + b * D, D) for b in range(TB)] for at in (2048, 8192))
    comb, comb_ready, weight, slot_i, slotted, flag, flagged, xrows_ready, xt_ready = route(
        buf_b, h_ready, buf_a, r_ready, xrows, xt, [pe.last()] + r_ready)
    queues = (pe, dve, act, pool, sp)
    for q in queues:
        q.wait(flagged, xt_ready[-1][-1])
    states = [q.branch(flag[0:1, :]) for q in queues]
    kept = ([list(b.free) for b in banks.slots], banks.n, dict(stream))
    moe_all(buf_b, buf_a, comb, comb_ready)
    act.wait((out_stored, 16 * TB))
    assert stream["next"] == len(places)
    for q, state in zip(queues, states):
        q.branch(None, state)
    for b, free in zip(banks.slots, kept[0]):
        b.free = free
    banks.n = kept[1]
    stream.update(kept[2])
    moe_slots(weight, slot_i, slotted, xrows, xrows_ready, xt, xt_ready)
    act.wait((out_stored, 16 * TB))
    assert stream["next"] == len(places)

    block = ctx.enter_context(nc.Block())

    @block.tensor
    def _(e):
        pe.issue(e)

    @block.vector
    def _(e):
        dve.issue(e)

    @block.scalar
    def _(e):
        act.issue(e)

    @block.gpsimd
    def _(e):
        pool.issue(e)

    @block.sync
    def _(e):
        sp.issue(e)


def pack_weights(inputs):
    plan = weight_plan()
    places, n_blocks = place_pieces(plan)
    out = np.zeros((n_blocks, P, BLOCK), np.float32)
    for (b, c), (_, (name, index, rows, cols)) in zip(places, in_order(plan)):
        w = inputs[name][index]
        r = 0
        for r0, nr in rows:
            at = c
            for c0, nc_ in cols:
                out[b, r:r + nr, at:at + nc_] = w[r0:r0 + nr, c0:c0 + nc_]
                at += nc_
            r += nr
    return out


def by_chunk(a):
    a = np.asarray(a)
    return a.reshape(-1, P).T


def pack_small(inp):
    at, n = small_layout()
    out = np.zeros((P, n), np.float32)

    def put(name, value):
        out[:, at[name][0]:at[name][1]] = value

    put("ln_g", by_chunk(inp["ln_g"]))
    put("ln_b", by_chunk(inp["ln_b"]))
    put("conv_w", by_chunk(inp["conv_w"][0]))
    put("s5_d", by_chunk(inp["s5_d"][0]))
    put("b_glu", by_chunk(inp["s5_b_glu"][0]))
    put("log_dt", np.repeat(inp["s5_log_dt"][0].reshape(PAIRS, 2, 1), STATES, axis=2).reshape(PAIRS, P).T)
    put("lam_re", inp["s5_lam_re"][0].reshape(PAIRS, P).T)
    put("lam_im", inp["s5_lam_im"][0].reshape(PAIRS, P).T)
    put("mix_g", by_chunk(inp["norm_mix_g_2"][0]))
    put("ffn_g", by_chunk(inp["norm_ffn_g_2"][0]))
    put("pos_k", np.tile(inp["cmp_pos_k_2"][0].T, (2, 1)))
    put("pos_v", np.tile(inp["cmp_pos_v_2"][0].T, (2, 1)))
    put("sinks", np.broadcast_to(inp["sinks_2"][0], (P, BH)))
    put("b_group", np.broadcast_to(inp["b_group_2"][0], (P, NGRP)))
    put("b_expert", np.broadcast_to(inp["b_expert_2"][0], (P, NEXP)))
    return out


def spread_pairs(a):
    out = np.zeros((P, PAIRS, PCH), np.float32)
    for g in range(GROUPS):
        q, half = g // 2, g % 2
        out[half * STATES:(half + 1) * STATES, q, half * GCH:(half + 1) * GCH] = a[g]
    return out


def kernel(**inputs):
    import concourse.bacc as bacc
    from concourse.bass_utils import run_bass_kernel_spmd

    inp = {k: np.asarray(v) for k, v in inputs.items()}
    arrays = {
        "x": np.ascontiguousarray(inp["x"][0].T),
        "p": np.ascontiguousarray(inp["p"][:, 0].transpose(0, 2, 1)),
        "positions": np.ascontiguousarray(np.broadcast_to(inp["positions"][0].astype(np.int32), (P, T))),
        "weights": pack_weights(inp),
        "small": pack_small(inp),
        "const": constants(),
        "gain": np.ascontiguousarray(np.broadcast_to(inp["norm_final_g_2"], (P, D))),
        "s5_b_re": spread_pairs(inp["s5_b_re"][0]),
        "s5_b_im": spread_pairs(inp["s5_b_im"][0]),
        "s5_c_re": spread_pairs(inp["s5_c_re"][0].transpose(0, 2, 1)),
        "s5_c_im": spread_pairs(inp["s5_c_im"][0].transpose(0, 2, 1)),
    }
    nc = bacc.Bacc("TRN2", target_bir_lowering=False, num_devices=1)
    io = {n: nc.dram_tensor("in_" + n, a.shape, mybir.dt.from_np(a.dtype), kind="ExternalInput").ap()
          for n, a in arrays.items()}
    io["out"] = nc.dram_tensor("out", [T, D], F32, kind="ExternalOutput").ap()
    build(nc, io)
    got = run_bass_kernel_spmd(nc, [{"in_" + n: a for n, a in arrays.items()}], core_ids=[0])
    return got.results[0]["out"][None]
```
